# Optimizing a Trainium2 kernel written in Bass

```python
import math
import jax
import jax.numpy as jnp
from jax import lax
import numpy as np

D_MODEL = 2048
BATCH = 1
SEQ = 256
DEPTH = 2

N_META = 16
HEAD_DIM = 64
SSM_WIDTH = D_MODEL // 2
SSM_GROUP = 16
SSM_GROUPS = SSM_WIDTH // SSM_GROUP
SSM_STATE = 64
FOX_WIDTH = D_MODEL // 4
FOX_HEADS = FOX_WIDTH // HEAD_DIM
DSA_WIDTH = D_MODEL - SSM_WIDTH - FOX_WIDTH
DSA_HEADS = DSA_WIDTH // HEAD_DIM
KV_RANK = D_MODEL // 16
IDX_HEADS = 16
IDX_DIM = 64
TOPK_MAX = 256
ROPE_THETA = 500000.0
ROT_DIM = HEAD_DIM // 4
D_FF = 11 * D_MODEL // 4
CONV_WIDTH = 3
Q_BLOCK = 128
LN_EPS = 1e-5
RMS_EPS = 1e-6
NEG_INF = -1e30
DT_MIN = 0.001
DT_MAX = 0.1
ALPHA = (2.0 * DEPTH) ** 0.25
BETA = (8.0 * DEPTH) ** -0.25

IN_SPLITS = (SSM_WIDTH, FOX_WIDTH, FOX_WIDTH, FOX_WIDTH, FOX_HEADS, DSA_WIDTH, KV_RANK,
             IDX_HEADS * IDX_DIM, IDX_DIM, IDX_HEADS)
IN_WIDTH = sum(IN_SPLITS)
SPLIT_POINTS = tuple(int(s) for s in np.cumsum(IN_SPLITS)[:-1])
GROUP_SPLIT_POINTS = (SSM_WIDTH, SSM_WIDTH + FOX_WIDTH)

kernel_name = 'hybrid_s5_fox_dsa_trunk'

def _layer_norm(x, g, b):
    xf = x.astype(jnp.float32)
    mu = jnp.mean(xf, axis=-1, keepdims=True)
    var = jnp.mean(jnp.square(xf - mu), axis=-1, keepdims=True)
    y = (xf - mu) * lax.rsqrt(var + LN_EPS) * g.astype(jnp.float32) + b.astype(jnp.float32)
    return y.astype(x.dtype)

def _rms_norm(x, g):
    xf = x.astype(jnp.float32)
    y = xf * lax.rsqrt(jnp.mean(jnp.square(xf), axis=-1, keepdims=True) + RMS_EPS) * g.astype(jnp.float32)
    return y.astype(x.dtype)

def _rope_tables(n):
    pos = jnp.arange(n, dtype=jnp.float32)
    inv_freq = ROPE_THETA ** (-jnp.arange(0, ROT_DIM, 2, dtype=jnp.float32) / ROT_DIM)
    ang = pos[:, None] * inv_freq[None, :]
    return jnp.cos(ang), jnp.sin(ang)

def _partial_rope(x, cos, sin):
    half = ROT_DIM // 2
    xr = x[..., :ROT_DIM].astype(jnp.float32)
    x1, x2 = xr[..., :half], xr[..., half:]
    c = cos[None, :, None, :]
    s = sin[None, :, None, :]
    rot = jnp.concatenate([x1 * c - x2 * s, x2 * c + x1 * s], axis=-1).astype(x.dtype)
    return jnp.concatenate([rot, x[..., ROT_DIM:]], axis=-1)

def _to_query_blocks(a, pad):
    a = jnp.pad(a, [(0, 0), (pad, 0)] + [(0, 0)] * (a.ndim - 2))
    a = a.reshape(a.shape[0], a.shape[1] // Q_BLOCK, Q_BLOCK, *a.shape[2:])
    return jnp.moveaxis(a, 1, 0)

def _from_query_blocks(o, pad):
    o = jnp.moveaxis(o, 0, 1)
    o = o.reshape(o.shape[0], o.shape[1] * o.shape[2], *o.shape[3:])
    return o[:, pad:]

def _query_positions(n, pad):
    kpos = jnp.arange(n, dtype=jnp.int32)
    qpos = jnp.concatenate([jnp.zeros((pad,), jnp.int32), kpos]).reshape(-1, Q_BLOCK)
    return kpos, qpos

def _complex_affine_combine(e1, e2):
    a1r, a1i, b1r, b1i = e1
    a2r, a2i, b2r, b2i = e2
    return (a1r * a2r - a1i * a2i,
            a1r * a2i + a1i * a2r,
            a2r * b1r - a2i * b1i + b2r,
            a2r * b1i + a2i * b1r + b2i)

def _s5_mixer(u, lam_re, lam_im, log_dt, b_re, b_im, c_re, c_im, d_skip, glu_w, glu_b):
    f32 = jnp.float32
    bsz, n, _ = u.shape
    uf = u.astype(f32)
    ug = uf.reshape(bsz, n, SSM_GROUPS, SSM_GROUP)
    lr, li = lam_re.astype(f32), lam_im.astype(f32)
    dt = jnp.exp(log_dt.astype(f32))[:, None]
    mag = jnp.exp(lr * dt)
    ab_re, ab_im = mag * jnp.cos(li * dt), mag * jnp.sin(li * dt)
    den = lr * lr + li * li
    nr, ni = ab_re - 1.0, ab_im
    zr = (nr * lr + ni * li) / den
    zi = (ni * lr - nr * li) / den
    br, bi = b_re.astype(f32), b_im.astype(f32)
    bb_re = zr[..., None] * br - zi[..., None] * bi
    bb_im = zr[..., None] * bi + zi[..., None] * br
    bu_re = jnp.einsum('gpc,btgc->btgp', bb_re, ug)
    bu_im = jnp.einsum('gpc,btgc->btgp', bb_im, ug)
    a_re = jnp.broadcast_to(ab_re, (1, n) + ab_re.shape)
    a_im = jnp.broadcast_to(ab_im, (1, n) + ab_im.shape)
    _, _, s_re, s_im = lax.associative_scan(_complex_affine_combine, (a_re, a_im, bu_re, bu_im), axis=1)
    y = (jnp.einsum('gcp,btgp->btgc', c_re.astype(f32), s_re)
         - jnp.einsum('gcp,btgp->btgc', c_im.astype(f32), s_im))
    y = y.reshape(bsz, n, SSM_WIDTH) + d_skip.astype(f32) * uf
    g = jax.nn.gelu(y)
    out = g * jax.nn.sigmoid(g @ glu_w.astype(f32) + glu_b.astype(f32))
    return out.astype(u.dtype)

def _fox_attention(q, k, v, f_logit, f_bias):
    f32 = jnp.float32
    bsz, n, h, dh = q.shape
    log_f = jax.nn.log_sigmoid(f_logit.astype(f32) + f_bias.astype(f32))
    cum = jnp.cumsum(log_f, axis=1)
    cum_k = jnp.transpose(cum, (0, 2, 1))
    pad = (-n) % Q_BLOCK
    kpos, qpos = _query_positions(n, pad)
    scale = dh ** -0.5

    def block(args):
        qb, cq, pq = args
        s = jnp.einsum('bqhd,bkhd->bhqk', qb, k, preferred_element_type=f32) * scale
        s = s + jnp.transpose(cq, (0, 2, 1))[..., None] - cum_k[:, :, None, :]
        s = jnp.where((kpos[None, :] <= pq[:, None])[None, None], s, NEG_INF)
        p = jax.nn.softmax(s, axis=-1)
        return jnp.einsum('bhqk,bkhd->bqhd', p.astype(v.dtype), v)

    out = lax.map(block, (_to_query_blocks(q, pad), _to_query_blocks(cum, pad), qpos))
    return _from_query_blocks(out, pad)

def _dsa_attention(q, k, v, iq, ik, iw, topk):
    f32 = jnp.float32
    bsz, n, h, dh = q.shape
    k_flat = k.reshape(bsz, n, h * dh)
    v_flat = v.reshape(bsz, n, h * dh)
    ikf = ik.astype(f32)
    pad = (-n) % Q_BLOCK
    kpos, qpos = _query_positions(n, pad)
    scale = dh ** -0.5
    bidx = jnp.arange(bsz)[:, None]

    def block(args):
        qb, iqb, iwb, pq = args
        logits = jnp.einsum('bqjd,bkd->bqjk', iqb.astype(f32), ikf) * (IDX_DIM ** -0.5)
        score = jnp.einsum('bqjk,bqj->bqk', jax.nn.relu(logits), iwb.astype(f32) * (IDX_HEADS ** -0.5))
        score = jnp.where((kpos[None, :] <= pq[:, None])[None], score, NEG_INF)
        _, idx = lax.top_k(score, topk)
        flat = idx.reshape(bsz, Q_BLOCK * topk)
        kg = k_flat[bidx, flat].reshape(bsz, Q_BLOCK, topk, h, dh)
        vg = v_flat[bidx, flat].reshape(bsz, Q_BLOCK, topk, h, dh)
        s = jnp.einsum('bqhd,bqkhd->bhqk', qb, kg, preferred_element_type=f32) * scale
        valid = (idx <= pq[None, :, None])[:, None]
        s = jnp.where(valid, s, NEG_INF)
        p = jax.nn.softmax(s, axis=-1)
        return jnp.einsum('bhqk,bqkhd->bqhd', p.astype(vg.dtype), vg)

    out = lax.map(block, (_to_query_blocks(q, pad), _to_query_blocks(iq, pad),
                          _to_query_blocks(iw, pad), qpos))
    return _from_query_blocks(out, pad)

def _mixer(h, cos, sin, topk, w_in, lam_re, lam_im, log_dt, b_re, b_im, c_re, c_im, d_skip,
           glu_w, glu_b, f_bias, kv_norm_g, w_kv_up, mix_norm_g, w_out):
    bsz, n, _ = h.shape
    proj = h @ w_in
    u, fq, fk, fv, ff, dq, ckv, iq, ik, iw = jnp.split(proj, SPLIT_POINTS, axis=-1)
    y_ssm = _s5_mixer(u, lam_re, lam_im, log_dt, b_re, b_im, c_re, c_im, d_skip, glu_w, glu_b)
    y_fox = _fox_attention(fq.reshape(bsz, n, FOX_HEADS, HEAD_DIM), fk.reshape(bsz, n, FOX_HEADS, HEAD_DIM),
                           fv.reshape(bsz, n, FOX_HEADS, HEAD_DIM), ff, f_bias)
    kv = _rms_norm(ckv, kv_norm_g) @ w_kv_up
    dk, dv = jnp.split(kv, 2, axis=-1)
    dq = _partial_rope(dq.reshape(bsz, n, DSA_HEADS, HEAD_DIM), cos, sin)
    dk = _partial_rope(dk.reshape(bsz, n, DSA_HEADS, HEAD_DIM), cos, sin)
    dv = dv.reshape(bsz, n, DSA_HEADS, HEAD_DIM)
    iq = _partial_rope(iq.reshape(bsz, n, IDX_HEADS, IDX_DIM), cos, sin)
    ik = _partial_rope(ik[:, :, None, :], cos, sin)[:, :, 0, :]
    y_dsa = _dsa_attention(dq, dk, dv, iq, ik, iw, topk)
    g_ssm, g_fox, g_dsa = jnp.split(mix_norm_g, GROUP_SPLIT_POINTS)
    y = jnp.concatenate([_rms_norm(y_ssm, g_ssm),
                         _rms_norm(y_fox.reshape(bsz, n, FOX_WIDTH), g_fox),
                         _rms_norm(y_dsa.reshape(bsz, n, DSA_WIDTH), g_dsa)], axis=-1)
    return y @ w_out

def _conv_ffn(h, w_up, conv_w, conv_b, w_down):
    a = h @ w_up
    c = a.shape[-1]
    a = lax.conv_general_dilated(a, conv_w[:, None, :].astype(a.dtype), window_strides=(1,),
                                 padding=[(CONV_WIDTH - 1, 0)],
                                 dimension_numbers=('NWC', 'WIO', 'NWC'),
                                 feature_group_count=c) + conv_b
    val, gate = jnp.split(a, 2, axis=-1)
    return (jax.nn.silu(gate) * val) @ w_down

def setup_inputs(seed: int = 0) -> dict:
    key = jax.random.key(seed)
    ks = jax.random.split(key, 32)
    f32 = jnp.float32
    L = DEPTH

    def nrm(k, shape, scale):
        return jax.random.normal(k, shape, f32) * scale

    x = nrm(ks[0], (BATCH, SEQ, D_MODEL), 1.0)
    meta_tokens = nrm(ks[1], (N_META, D_MODEL), 1.0)
    ln_in_g = 1.0 + nrm(ks[2], (D_MODEL,), 0.02)
    ln_in_b = nrm(ks[3], (D_MODEL,), 0.02)
    w_in = nrm(ks[4], (L, D_MODEL, IN_WIDTH), D_MODEL ** -0.5)
    n_idx = jnp.arange(SSM_STATE, dtype=f32)
    ssm_lam_re = -0.5 + nrm(ks[5], (L, SSM_GROUPS, SSM_STATE), 0.01)
    ssm_lam_im = jnp.pi * n_idx + nrm(ks[6], (L, SSM_GROUPS, SSM_STATE), 0.01)
    ssm_log_dt = jax.random.uniform(ks[7], (L, SSM_GROUPS), f32, math.log(DT_MIN), math.log(DT_MAX))
    b_scale = (2.0 * SSM_GROUP) ** -0.5
    ssm_b_re = nrm(ks[8], (L, SSM_GROUPS, SSM_STATE, SSM_GROUP), b_scale)
    ssm_b_im = nrm(ks[9], (L, SSM_GROUPS, SSM_STATE, SSM_GROUP), b_scale)
    c_scale = SSM_STATE ** -0.5
    ssm_c_re = nrm(ks[10], (L, SSM_GROUPS, SSM_GROUP, SSM_STATE), c_scale)
    ssm_c_im = nrm(ks[11], (L, SSM_GROUPS, SSM_GROUP, SSM_STATE), c_scale)
    ssm_d = nrm(ks[12], (L, SSM_WIDTH), 1.0)
    ssm_glu_w = nrm(ks[13], (L, SSM_WIDTH, SSM_WIDTH), SSM_WIDTH ** -0.5)
    ssm_glu_b = nrm(ks[14], (L, SSM_WIDTH), 0.02)
    fox_f_bias = jax.random.uniform(ks[15], (L, FOX_HEADS), f32, 2.0, 5.0)
    kv_norm_g = 1.0 + nrm(ks[16], (L, KV_RANK), 0.02)
    w_kv_up = nrm(ks[17], (L, KV_RANK, 2 * DSA_WIDTH), KV_RANK ** -0.5)
    mix_norm_g = 1.0 + nrm(ks[18], (L, D_MODEL), 0.02)
    w_out = nrm(ks[19], (L, D_MODEL, D_MODEL), BETA * D_MODEL ** -0.5)
    ln1_g = 1.0 + nrm(ks[20], (L, D_MODEL), 0.02)
    ln1_b = nrm(ks[21], (L, D_MODEL), 0.02)
    w_up = nrm(ks[22], (L, D_MODEL, 2 * D_FF), D_MODEL ** -0.5)
    conv_w = nrm(ks[23], (L, CONV_WIDTH, 2 * D_FF), CONV_WIDTH ** -0.5)
    conv_b = nrm(ks[24], (L, 2 * D_FF), 0.02)
    w_down = nrm(ks[25], (L, D_FF, D_MODEL), BETA * D_FF ** -0.5)
    ln2_g = 1.0 + nrm(ks[26], (L, D_MODEL), 0.02)
    ln2_b = nrm(ks[27], (L, D_MODEL), 0.02)
    return {'x': x, 'meta_tokens': meta_tokens, 'ln_in_g': ln_in_g, 'ln_in_b': ln_in_b, 'w_in': w_in,
            'ssm_lam_re': ssm_lam_re, 'ssm_lam_im': ssm_lam_im, 'ssm_log_dt': ssm_log_dt,
            'ssm_b_re': ssm_b_re, 'ssm_b_im': ssm_b_im, 'ssm_c_re': ssm_c_re, 'ssm_c_im': ssm_c_im,
            'ssm_d': ssm_d, 'ssm_glu_w': ssm_glu_w, 'ssm_glu_b': ssm_glu_b, 'fox_f_bias': fox_f_bias,
            'kv_norm_g': kv_norm_g, 'w_kv_up': w_kv_up, 'mix_norm_g': mix_norm_g, 'w_out': w_out,
            'ln1_g': ln1_g, 'ln1_b': ln1_b, 'w_up': w_up, 'conv_w': conv_w, 'conv_b': conv_b,
            'w_down': w_down, 'ln2_g': ln2_g, 'ln2_b': ln2_b}

def reference(x, meta_tokens, ln_in_g, ln_in_b, w_in, ssm_lam_re, ssm_lam_im, ssm_log_dt,
              ssm_b_re, ssm_b_im, ssm_c_re, ssm_c_im, ssm_d, ssm_glu_w, ssm_glu_b, fox_f_bias,
              kv_norm_g, w_kv_up, mix_norm_g, w_out, ln1_g, ln1_b, w_up, conv_w, conv_b,
              w_down, ln2_g, ln2_b):
    bsz, seq, _ = x.shape
    topk = min(TOPK_MAX, seq // 4)
    meta = jnp.broadcast_to(meta_tokens[None].astype(x.dtype), (bsz, N_META, D_MODEL))
    h = _layer_norm(jnp.concatenate([meta, x], axis=1), ln_in_g, ln_in_b)
    cos, sin = _rope_tables(seq + N_META)
    for l in range(DEPTH):
        m = _mixer(h, cos, sin, topk, w_in[l], ssm_lam_re[l], ssm_lam_im[l], ssm_log_dt[l],
                   ssm_b_re[l], ssm_b_im[l], ssm_c_re[l], ssm_c_im[l], ssm_d[l], ssm_glu_w[l],
                   ssm_glu_b[l], fox_f_bias[l], kv_norm_g[l], w_kv_up[l], mix_norm_g[l], w_out[l])
        h = _layer_norm(ALPHA * h + m, ln1_g[l], ln1_b[l])
        f = _conv_ffn(h, w_up[l], conv_w[l], conv_b[l], w_down[l])
        h = _layer_norm(ALPHA * h + f, ln2_g[l], ln2_b[l])
    return h[:, N_META:, :]


_drawn_inputs = setup_inputs


def setup_inputs(seed=0):
    import zlib

    import numpy as np

    out = dict(_drawn_inputs(seed))
    spreads = {}
    factors = {'ssm_lam_re': 8.0,
     'ssm_glu_b': 8.0,
     'kv_norm_g': 4.913,
     'mix_norm_g': 3.784,
     'conv_b': 4.173}
    for name, (base, spread) in spreads.items():
        noise = np.random.default_rng([zlib.crc32(name.encode()), seed]).standard_normal(out[name].shape)
        drawn = base * np.exp(spread * noise) if base else spread * noise
        out[name] = jnp.asarray(drawn.astype(out[name].dtype))
    for name, factor in factors.items():
        out[name] = (out[name] * factor).astype(out[name].dtype)
    return out
```

```python
from contextlib import ExitStack

import concourse.bass as bass
import numpy as np
from concourse import mybir

F32 = mybir.dt.float32
F32R = mybir.dt.float32r
ALU = mybir.AluOpType
ACT = mybir.ActivationFunctionType
AX_X = mybir.AxisListType.X

P = 128
D_MODEL, SEQ, N_META, DEPTH = 2048, 256, 16, 2
NT = SEQ + N_META
HEAD = 64
SSM_W, GROUP, STATE = D_MODEL // 2, 16, 64
HEADS = 8
KV_RANK = 128
IDX_HEADS = 16
TOPK = min(256, SEQ // 4)
D_FF = 11 * D_MODEL // 4
ALPHA = (2.0 * DEPTH) ** 0.25
LN_EPS, RMS_EPS = 1e-5, 1e-6
NEG = -1e30
HALF_PI = 1.5707963
TAKEN = -3e38
SCALE = HEAD ** -0.5
TWO_PI_LOW = 6.283185
ROUND = 12582912.0

DT = D_MODEL // P
FT = D_FF // P
UT = SSM_W // P
ST = SSM_W // GROUP * STATE // P
MASK_T = 96
QT = [(s, min(MASK_T, NT - s)) for s in range(0, NT, MASK_T)]
NQ = len(QT)

KB = 4
SLOTS = 4
PHASES = {"in": (18, DT // KB, 2), "glu": (4, UT // KB, 4), "out": (8, DT // KB, 2),
          "up": (FT, DT // KB, 2), "down": (8, FT // KB, 4)}
SPLIT = ("out", "up", "down")
BLOCKS_PER_LAYER = sum(g * b for g, b, _ in PHASES.values())
GROUPS_PER_LAYER = sum(g for g, _, _ in PHASES.values())
SPLIT_PER_LAYER = sum(PHASES[p][0] * PHASES[p][1] for p in SPLIT)


def first_block(layer, phase):
    names = list(PHASES)
    return layer * BLOCKS_PER_LAYER + sum(PHASES[n][0] * PHASES[n][1] for n in names[:names.index(phase)])


def first_group(layer, phase):
    names = list(PHASES)
    return layer * GROUPS_PER_LAYER + sum(PHASES[n][0] for n in names[:names.index(phase)])


def first_split(layer, phase):
    return layer * SPLIT_PER_LAYER + sum(PHASES[n][0] * PHASES[n][1] for n in SPLIT[:SPLIT.index(phase)])


U0, FQ0, FK0, FV0, DQ0, IQ0, CKV, FFIW, IK, PADT = 0, 8, 12, 16, 20, 24, 32, 33, 34, 35

CONST = {}
_at = 0
for _name, _cols in (("ident", P), ("ones", P), ("perm", P), ("rope_c", NT), ("rope_s", NT), ("time", NT),
                     ("causal", MASK_T), ("sel8", HEADS)):
    CONST[_name] = (_at, _cols)
    _at += _cols
CONST_COLS = _at

PARAM = {}
_at = 0
for _name, _cols in (("ln_in_g", DT), ("ln_in_b", DT), ("ln1_g", DEPTH * DT), ("ln1_b", DEPTH * DT),
                     ("ln2_g", DEPTH * DT), ("ln2_b", DEPTH * DT), ("mix_g", DEPTH * DT),
                     ("conv", DEPTH * FT * 8), ("glu_b", DEPTH * UT),
                     ("d_skip", DEPTH * UT), ("kv_g", DEPTH), ("f_bias", DEPTH),
                     ("lam_re", DEPTH * ST), ("lam_im", DEPTH * ST), ("log_dt", DEPTH * ST)):
    PARAM[_name] = (_at, _cols)
    _at += _cols
PARAM_COLS = _at


def hybrid_trunk(nc, x, stream, consts, params, ssm_b, ssm_c, w_kv, out):
    with ExitStack() as ctx:
        def sem(name):
            return ctx.enter_context(nc.semaphore(name))

        base = (nc.sbuf_base + 63) // 64 * 64
        cursor = {"at": base}

        def place(name, shape, dt=F32, at=None):
            size = 4 * int(np.prod(shape[1:]))
            where = cursor["at"] if at is None else at
            t = nc.alloc_sbuf_tensor_at(name, shape, dt, offset=where)
            if at is None:
                cursor["at"] += (size + 31) // 32 * 32
            return t, where + (size + 31) // 32 * 32

        h, _ = place("h", [P, DT, NT])
        raw, _ = place("raw", [P, SLOTS, KB, 2 * P])
        w_hi, _ = place("w_hi", [P, SLOTS, KB, 2 * P], F32R)
        w_lo, _ = place("w_lo", [P, SLOTS, KB, 2 * P], F32R)
        par, _ = place("par", [P, PARAM_COLS])
        ones, _ = place("ones_p", [P, P])
        rstd, _ = place("rstd", [P, NT])
        low = cursor["at"]
        x_hi, e = place("x_hi", [P, DT, NT], F32R, at=low)
        x_lo, high = place("x_lo", [P, DT, NT], F32R, at=e)
        g_hi, e = place("g_hi", [P, FT, NT], F32R, at=high)
        g_lo, ffn_end = place("g_lo", [P, FT, NT], F32R, at=e)
        squares, _ = place("squares", [P, DT, NT], at=high)
        conv, e = place("conv", [P, 2, 2, NT], at=ffn_end)
        gate, e = place("gate", [P, 2, NT], at=e)
        prod, e = place("prod", [P, 2, NT], at=e)
        cpar, e = place("cpar", [P, 2, 8], at=e)
        assert e <= nc.sbuf_usable_end, (e, nc.sbuf_usable_end)
        end = nc.sbuf_usable_end
        proj, e = place("proj", [P, 36, NT], at=high)
        kv, e = place("kv", [P, 8, NT], at=e)
        yssm, e = place("yssm", [P, UT, NT], at=e)
        wkv, e = place("wkv", [P, 1024], at=e)
        cst, e = place("cst", [P, CONST_COLS], at=e)
        small, e = place("small", [P, 20, ST], at=e)
        mixer_end = e
        v_tok, e = place("v_tok", [P, 2, NQ, 512], at=mixer_end)
        y_tok, e = place("y_tok", [P, 2, NQ, 512], at=low)
        work, e2 = place("work", [P, 2, NQ, NT], at=e)
        probs, e2 = place("probs", [P, 2, NT], at=e2)
        pt, e2 = place("pt", [P, 2, NQ, MASK_T], at=e2)
        relu, e2 = place("relu", [P, 4, NT], at=e2)
        rope_t, e2 = place("rope_t", [P, 4, NT], at=e2)
        assert e2 <= high, (e2, high)
        dsa_bias, e = place("dsa_bias", [P, NQ, NT], at=mixer_end + 2 * NQ * 512 * 4)
        top8, e = place("top8", [P, NQ, 8], at=e)
        iw_tok, e = place("iw_tok", [P, NQ, 32], at=e)
        stat, e = place("stat", [P, 4, 8], at=e)
        ltmp, e = place("ltmp", [P, 5, NT], at=e)
        assert e <= end, (e, end)
        table, e = place("table", [P, 2, 4, 2, NT], at=low)
        turns, e = place("turns", [P, 3, 2, NT], at=e)
        states, e = place("states", [P, 2, 2, 2, NT], at=e)
        assert e <= high, (e, high)
        rot, e = place("rot", [P, 4, 2, 2, NT], at=mixer_end)
        b_st, e = place("b_st", [P, 2, UT, P], at=e)
        c_st, e = place("c_st", [P, 2, ST, 32], at=e)
        assert e <= end, (e, end)

        ps = ctx.enter_context(nc.psum_tensor("ps", [P, 8, 512], F32))

        def const(name, rows=P, cols=None):
            at, n = CONST[name]
            return cst[0:rows, at:at + (cols or n)]

        def param(name, at, n=1, rows=P):
            o = PARAM[name][0] + at
            return par[0:rows, o:o + n]

        w_loaded = [sem(f"w_loaded{s}") for s in range(SLOTS)]
        block_used = sem("block_used")
        hi_made, lo_made = sem("hi_made"), sem("lo_made")
        psum_free = sem("psum_free")
        x_loaded, par_loaded, mix_loaded, ones_made = sem("x_loaded"), sem("par_loaded"), sem("mix_loaded"), sem("ones_made")
        mean_made, centered, squared, var_made, dev_made = (sem(n) for n in (
            "mean_made", "centered", "squared", "var_made", "dev_made"))
        h_made, xhi_made, xlo_made = sem("h_made"), sem("xhi_made"), sem("xlo_made")
        dt_made, freq_made, trig_made, c_made = (sem(n) for n in ("dt_made", "freq_made", "trig_made", "c_made"))
        turns_made, table_made, bu_made, bu_read, s_made, s_used, abs_made, y_read = (sem(n) for n in (
            "turns_made", "table_made", "bu_made", "bu_read", "s_made", "s_used", "abs_made", "y_read"))
        gelu_made, sig_made, glu_made, glu_sq, glu_ms, glu_sd, ymul = (sem(n) for n in (
            "gelu_made", "sig_made", "glu_made", "glu_sq", "glu_ms", "glu_sd", "ymul"))
        rot_made, roped = sem("rot_made"), sem("roped")
        ckv_sq, ckv_ms, ckv_sd, ckv_normed, kv_mm, kv_made = (sem(n) for n in (
            "ckv_sq", "ckv_ms", "ckv_sd", "ckv_normed", "kv_mm", "kv_made"))
        f_neg, f_exp, f_ln, cum_made = sem("f_neg"), sem("f_exp"), sem("f_ln"), sem("cum_made")
        vt_made, v_made = sem("vt_made"), sem("v_made")
        iwt_made, iw_made = sem("iwt_made"), sem("iw_made")
        idx_mm, idx_relu, idx_used, bias_made = sem("idx_mm"), sem("idx_relu"), sem("idx_used"), sem("bias_made")
        score_made, max_made, prob_made, ptr_made, pt_made, o_made, den_made, o_read = (sem(n) for n in (
            "score_made", "max_made", "prob_made", "ptr_made", "pt_made", "o_made", "den_made", "o_read"))
        ysq, ysd, ynorm, yt_mm, yt_made = (sem(n) for n in ("ysq", "ysd", "ynorm", "yt_mm", "yt_made"))
        yhi_made, ylo_made = sem("yhi_made"), sem("ylo_made")
        cpar_made, conv_a, conv1_made, gate_made = sem("cpar_made"), sem("conv_a"), sem("conv1_made"), sem("gate_made")
        prod_made, ghi_made, g_made = sem("prod_made"), sem("ghi_made"), sem("g_made")
        dve_step = sem("dve_step")
        stored = sem("stored")

        block = ctx.enter_context(nc.Block())

        @block.sync
        def _(sp):
            sp.dma_start(h[:, :, :], x).then_inc(x_loaded, 16)
            sp.dma_start(par[:, :], params).then_inc(par_loaded, 16)
            for b in range(SLOTS):
                sp.dma_start(raw[:, b, :, :], stream[b].rearrange("p (k m) -> p k m", k=KB)).then_inc(w_loaded[b], 16)
            with sp.Fori(1, DEPTH * BLOCKS_PER_LAYER // SLOTS) as it:
                for b in range(SLOTS):
                    n = it * SLOTS + b
                    src = stream[bass.ds(n, 1), :, :].rearrange("a p (k m) -> p (a k) m", k=KB)
                    sp.wait_ge(block_used, n - (SLOTS - 1))
                    sp.dma_start(raw[:, b, :, :], src).then_inc(w_loaded[b], 16)
            sp.wait_ge(h_made, 4 * (2 * DEPTH + 1))
            sp.dma_start(out, h[:, :, :]).then_inc(stored, 16)
            sp.wait_ge(stored, 16)

        @block.gpsimd
        def _(pool):
            nc.gpsimd.memset(ones[:, :], 1.0).then_inc(ones_made, 1)
            for l in range(DEPTH):
                if l:
                    pool.wait_ge(h_made, 4 * (2 * l + 1))
                else:
                    pool.wait_ge(h_made, 4)
                pool.dma_start(cst[:, :], consts).then_inc(mix_loaded, 16)
                pool.dma_start(wkv[:, :], w_kv[l]).then_inc(mix_loaded, 16)
                pool.dma_start(b_st[:, :, :, :], ssm_b[l]).then_inc(mix_loaded, 16)
                pool.dma_start(c_st[:, :, :, :], ssm_c[l]).then_inc(mix_loaded, 16)

        @block.tensor
        def _(pe):
            def products(l, phase, rhs, ready=None):
                groups, blocks, body = PHASES[phase]
                b0, g0 = first_block(l, phase), first_group(l, phase)
                split = phase in SPLIT
                s0 = first_split(l, phase) if split else 0
                with pe.Fori(0, groups // body) as it:
                    for g in range(body):
                        pe.wait_ge(psum_free, it * body + g0 + g + 1)
                        for b in range(blocks):
                            n = g * blocks + b
                            slot = n % SLOTS
                            if split:
                                pe.wait_ge(lo_made, it * (body * blocks) + (s0 + n + 1))
                            else:
                                pe.wait_ge(w_loaded[slot], it * (body * blocks // SLOTS * 16) + ((b0 + n) // SLOTS + 1) * 16)
                            for kk in range(KB):
                                k = b * KB + kk
                                for j in range(2):
                                    acc = ps[:, 2 * (g % 2) + j, 0:NT]
                                    cols = slice(j * P, j * P + P)
                                    first, last = k == 0, k == blocks * KB - 1
                                    if split:
                                        hi, lo = rhs(k)
                                        pe.matmul(acc, w_lo[:, slot, kk, cols], hi, start=first, stop=False)
                                        pe.matmul(acc, w_hi[:, slot, kk, cols], lo, start=False, stop=False)
                                        mm = pe.matmul(acc, w_hi[:, slot, kk, cols], hi, start=False, stop=last)
                                    else:
                                        mm = pe.matmul(acc, raw[:, slot, kk, cols], rhs(k), start=first, stop=last)
                            mm.then_inc(block_used, 1)

            def layer_norm_sums(n):
                for k in range(DT):
                    mm = pe.matmul(ps[:, 4, 0:NT], ones[:, :], h[:, k, :], start=k == 0, stop=k == DT - 1)
                mm.then_inc(mean_made, 1)
                for k in range(DT):
                    if k % 4 == 0:
                        pe.wait_ge(squared, 4 * n + k // 4 + 1)
                    mm = pe.matmul(ps[:, 5, 0:NT], ones[:, :], squares[:, k, :], start=k == 0, stop=k == DT - 1)
                mm.then_inc(var_made, 1)

            def state_inputs(l, pr):
                for e in range(2):
                    t = 2 * pr + e
                    rows = slice(32 * (t % 4), 32 * (t % 4) + 32)
                    for c in range(2):
                        mm = pe.matmul(ps[:, 4 + 2 * e + c, 0:NT], b_st[rows, c, t // 4, :],
                                       proj[rows, U0 + t // 4, :], start=True, stop=True)
                mm.then_inc(bu_made, 1)

            def state_outputs(l, pr):
                m = pr // 2
                if pr % 2 == 0 and l * UT + m >= 2:
                    pe.wait_ge(y_read, l * UT + m - 1)
                pe.wait_ge(s_made, l * 16 + pr + 1)
                for e in range(2):
                    t = 2 * pr + e
                    rows = slice(32 * (t % 4), 32 * (t % 4) + 32)
                    for c in range(2):
                        mm = pe.matmul(ps[rows, m % 2, 0:NT], c_st[:, c, t, :], states[:, pr % 2, e, c, :],
                                       start=c == 0, stop=c == 1)
                mm.then_inc(s_used, 1)

            def scores(l, n):
                kind, hd, q = n // (HEADS * NQ), n // NQ % HEADS, n % NQ
                qs, qn = QT[q]
                ke = qs + qn
                b = slice(64 * (hd % 2), 64 * (hd % 2) + 64)
                s = ps[0:qn, 4 + n % 2, 0:ke]
                if n >= 2:
                    pe.wait_ge(prob_made, l * 48 + n - 1)
                if kind == 0:
                    pe.matmul(s, proj[b, FQ0 + hd // 2, qs:ke], proj[b, FK0 + hd // 2, 0:ke], start=True, stop=False)
                    pe.matmul(s, const("sel8", 8)[:, hd:hd + 1].to_broadcast([8, qn]), ltmp[0:8, 4, 0:ke],
                              start=False, stop=False)
                    pe.matmul(s[:, qs:ke], const("ident", qn, qn), const("causal", qn, qn), start=False, stop=False)
                    mm = pe.matmul(s, ltmp[0:8, 3, qs:ke], const("sel8", 8)[:, hd:hd + 1].to_broadcast([8, ke]),
                                   start=False, stop=True)
                else:
                    pe.matmul(s, proj[b, DQ0 + hd // 2, qs:ke], kv[b, hd // 2, 0:ke], start=True, stop=False)
                    mm = pe.matmul(s, const("ident", qn, qn), dsa_bias[0:qn, q, 0:ke], start=False, stop=True)
                mm.then_inc(score_made, 1)

            def prob_transposes(l, n):
                q = n % NQ
                qs, qn = QT[q]
                pe.wait_ge(prob_made, l * 48 + n + 1)
                if n >= 1:
                    pe.wait_ge(pt_made, l * 48 + n)
                for c in range(q + 1):
                    ks, kn = QT[c]
                    at = (q - c) * MASK_T
                    mm = pe.transpose(ps[0:kn, 6, at:at + qn], probs[0:qn, n % 2, ks:ks + kn], const("ident", qn, qn))
                mm.then_inc(ptr_made, 1)

            def weighted_values(l, n):
                kind, hd, q = n // (HEADS * NQ), n // NQ % HEADS, n % NQ
                qs, qn = QT[q]
                pe.wait_ge(pt_made, l * 48 + n + 1)
                if n >= 1:
                    pe.wait_ge(o_read, l * 48 + n)
                for c in range(q + 1):
                    ks, kn = QT[c]
                    mm = pe.matmul(ps[0:qn, 7, 0:HEAD], pt[0:kn, n % 2, q - c, 0:qn],
                                   v_tok[0:kn, kind, c, hd * HEAD:hd * HEAD + HEAD], start=c == 0, stop=c == q)
                mm.then_inc(o_made, 1)

            def transpose_values(l, kind):
                for c, (ks, kn) in enumerate(QT):
                    n = kind * NQ + c
                    pe.wait_ge(v_made, l * 6 + n) if n else None
                    for t in range(4):
                        src = proj[:, FV0 + t, ks:ks + kn] if kind == 0 else kv[:, 4 + t, ks:ks + kn]
                        mm = pe.transpose(ps[0:kn, 7, t * P:t * P + P], src, const("ident"))
                    mm.then_inc(vt_made, 1)

            pe.wait_ge(ones_made, 1)
            pe.wait_ge(x_loaded, 16)
            layer_norm_sums(0)
            for l in range(DEPTH):
                ln = 2 * l + 1
                pe.wait_ge(h_made, 4 * ln)
                products(l, "in", lambda k: h[:, k, :])
                pe.wait_ge(psum_free, first_group(l, "in") + 18 + 2)
                pe.wait_ge(mix_loaded, 64 * (l + 1))
                state_inputs(l, 0)
                pe.wait_ge(c_made, l + 1)
                for pr in range(16):
                    if pr < 15:
                        pe.wait_ge(bu_read, 2 * (l * 16 + pr + 1))
                        state_inputs(l, pr + 1)
                    state_outputs(l, pr)
                for r, (t0, tn) in enumerate(((DQ0, 4), (IQ0, 4), (IQ0 + 4, 4), (IK, 1))):
                    if r:
                        pe.wait_ge(roped, 5 * l + r)
                    else:
                        pe.wait_ge(bu_read, 32 * (l + 1))
                    for t in range(tn):
                        mm = pe.matmul(ps[:, 4 + t, 0:NT], const("perm"), proj[:, t0 + t, :], start=True, stop=True)
                    mm.then_inc(rot_made, 1)
                pe.wait_ge(ckv_sq, l + 1)
                pe.wait_ge(roped, 5 * l + 4)
                pe.matmul(ps[:, 4, 0:NT], ones[:, :], ltmp[:, 0, :], start=True, stop=True).then_inc(ckv_ms, 1)
                pe.wait_ge(ckv_normed, l + 1)
                for r in range(2):
                    if r:
                        pe.wait_ge(kv_made, 2 * l + 1)
                    for t in range(4):
                        mm = pe.matmul(ps[:, 4 + t, 0:NT], wkv[:, (4 * r + t) * P:(4 * r + t + 1) * P], proj[:, PADT, :],
                                       start=True, stop=True)
                    mm.then_inc(kv_mm, 1)
                pe.wait_ge(kv_made, 2 * l + 2)
                for t in range(4):
                    mm = pe.matmul(ps[:, 4 + t, 0:NT], const("perm"), kv[:, t, :], start=True, stop=True)
                mm.then_inc(rot_made, 1)
                pe.wait_ge(roped, 5 * l + 5)
                for q, (qs, qn) in enumerate(QT):
                    mm = pe.transpose(ps[0:qn, 6, 32 * q:32 * q + 24], proj[0:24, FFIW, qs:qs + qn], const("ident", 24, 24))
                mm.then_inc(iwt_made, 1)
                transpose_values(l, 0)
                transpose_values(l, 1)
                pe.wait_ge(v_made, 6 * (l + 1))
                pe.wait_ge(iw_made, l + 1)
                for n in range(IDX_HEADS * NQ):
                    j, q = n // NQ, n % NQ
                    qs, qn = QT[q]
                    b = slice(64 * (j % 2), 64 * (j % 2) + 64)
                    if n >= 4:
                        pe.wait_ge(idx_relu, l * 48 + n - 3)
                    pe.matmul(ps[0:qn, 4 + n % 4, 0:qs + qn], proj[b, IQ0 + j // 2, qs:qs + qn],
                              proj[b, IK, 0:qs + qn], start=True, stop=True).then_inc(idx_mm, 1)
                pe.wait_ge(idx_relu, 48 * (l + 1))
                pe.wait_ge(cum_made, l + 1)
                for n in range(48 + 2):
                    if n == 24:
                        pe.wait_ge(bias_made, l + 1)
                    if n < 48:
                        scores(l, n)
                    if 1 <= n < 49:
                        prob_transposes(l, n - 1)
                    if n >= 2:
                        weighted_values(l, n - 2)
                pe.wait_ge(gelu_made, l + 1)
                g0, b0 = first_group(l, "glu"), first_block(l, "glu")
                for g in range(4):
                    pe.wait_ge(psum_free, g0 + g + 1)
                    for b in range(2):
                        n = 2 * g + b
                        pe.wait_ge(w_loaded[n % SLOTS], ((b0 + n) // SLOTS + 1) * 16)
                        for kk in range(KB):
                            for j in range(2):
                                k = b * KB + kk
                                mm = pe.matmul(ps[:, 2 * (g % 2) + j, 0:NT], raw[:, n % SLOTS, kk, j * P:j * P + P],
                                               yssm[:, k, :], start=k == 0, stop=k == 7)
                        mm.then_inc(block_used, 1)
                for g in range(4):
                    pe.wait_ge(glu_sq, 4 * l + g + 1)
                    for j in range(2):
                        mm = pe.matmul(ps[:, 4, 0:NT], ones[:, :], proj[:, 8 + 2 * g + j, :],
                                       start=g + j == 0, stop=g == 3 and j == 1)
                mm.then_inc(glu_ms, 1)
                for n in range(6):
                    kind, q = n // NQ, n % NQ
                    qs, qn = QT[q]
                    pe.wait_ge(ynorm, 6 * l + n + 1)
                    if n >= 2:
                        pe.wait_ge(yt_made, 6 * l + n - 1)
                    for t in range(4):
                        mm = pe.transpose(ps[:, 5 + n % 2, t * MASK_T:t * MASK_T + qn],
                                          y_tok[0:qn, kind, q, t * P:t * P + P], const("ident", qn, qn))
                    mm.then_inc(yt_mm, 1)
                pe.wait_ge(ylo_made, 2 * (l + 1))
                products(l, "out", lambda k: (x_hi[:, k, :], x_lo[:, k, :]))
                pe.wait_ge(psum_free, first_group(l, "out") + 8 + 2)
                layer_norm_sums(ln)
                pe.wait_ge(xlo_made, 4 * (l + 1))
                products(l, "up", lambda k: (x_hi[:, k, :], x_lo[:, k, :]))
                pe.wait_ge(g_made, FT * (l + 1))
                products(l, "down", lambda k: (g_hi[:, k, :], g_lo[:, k, :]))
                pe.wait_ge(psum_free, first_group(l, "down") + 8 + 2)
                layer_norm_sums(ln + 1)

        @block.scalar
        def _(act):
            def cast(l, phase, n, loop=0):
                b = first_block(l, phase) + n
                slot = b % SLOTS
                act.wait_ge(w_loaded[slot], loop + (b // SLOTS + 1) * 16)
                act.activation(w_hi[:, slot, :, :], raw[:, slot, :, :], ACT.Copy).then_inc(hi_made, 1)

            def layer_norm(n):
                for c in range(4):
                    act.wait_ge(centered, 4 * n + c + 1)
                    act.activation(squares[:, 4 * c:4 * c + 4, :], h[:, 4 * c:4 * c + 4, :], ACT.Square).then_inc(squared, 1)
                act.wait_ge(var_made, n + 1)
                act.activation(rstd[:, :], ps[:, 5, 0:NT], ACT.Sqrt, bias=LN_EPS, scale=1.0 / D_MODEL).then_inc(dev_made, 1)

            act.wait_ge(x_loaded, 16)
            layer_norm(0)
            for l in range(DEPTH):
                ln = 2 * l + 1
                act.wait_ge(mix_loaded, 64 * (l + 1))
                act.wait_ge(par_loaded, 16)
                act.activation(small[:, 0, :], param("log_dt", l * ST, ST), ACT.Exp).then_inc(dt_made, 1)
                act.wait_ge(freq_made, l + 1)
                act.activation(small[:, 4, :], small[:, 1, :], ACT.Exp).then_inc(trig_made, 1)
                act.activation(small[:, 5, :], small[:, 3, :], ACT.Sin, scale=TWO_PI_LOW).then_inc(trig_made, 1)
                act.activation(small[:, 6, :], small[:, 7, :], ACT.Sin, bias=HALF_PI, scale=-TWO_PI_LOW).then_inc(trig_made, 1)
                for pr in range(16):
                    r = l * 16 + pr
                    act.wait_ge(turns_made, r + 1)
                    if pr >= 2:
                        act.wait_ge(s_made, r - 1)
                    tb = table[:, pr % 2, :, :, :]
                    tr = turns[:, 0, :, :]
                    act.activation(turns[:, 2, :, :], tr, ACT.Abs).then_inc(abs_made, 1)
                    act.activation(tb[:, 1, :, :], tr, ACT.Sin, scale=TWO_PI_LOW)
                    act.activation(tb[:, 2, :, :], tr, ACT.Sin, scale=-TWO_PI_LOW)
                    act.activation(tb[:, 3, :, :], tr, ACT.Sin, scale=TWO_PI_LOW)
                    act.wait_ge(abs_made, r + 1)
                    act.activation(tb[:, 0, :, :], turns[:, 2, :, :], ACT.Sin, bias=HALF_PI, scale=-TWO_PI_LOW).then_inc(table_made, 1)
                act.wait_ge(y_read, UT * (l + 1))
                act.activation(yssm[:, :, :], yssm[:, :, :], ACT.Gelu_apprx_tanh).then_inc(gelu_made, 1)
                act.wait_ge(f_neg, l + 1)
                act.activation(ltmp[0:8, 1, :], ltmp[0:8, 1, :], ACT.Exp).then_inc(f_exp, 1)
                act.wait_ge(f_exp, l + 1)
                act.activation(ltmp[0:8, 1, :], ltmp[0:8, 1, :], ACT.Ln, bias=1.0).then_inc(f_ln, 1)
                act.wait_ge(ckv_ms, l + 1)
                act.activation(rstd[:, :], ps[:, 4, 0:NT], ACT.Sqrt, bias=RMS_EPS, scale=1.0 / KV_RANK).then_inc(ckv_sd, 1)
                for r in range(2):
                    act.wait_ge(kv_mm, 2 * l + r + 1)
                    act.activation(kv[:, 4 * r:4 * r + 4, :], ps[:, 4:8, 0:NT], ACT.Copy).then_inc(kv_made, 1)
                for n in range(6):
                    kn = QT[n % NQ][1]
                    act.wait_ge(vt_made, 6 * l + n + 1)
                    act.activation(v_tok[0:kn, n // NQ, n % NQ, :], ps[0:kn, 7, :], ACT.Copy).then_inc(v_made, 1)
                for n in range(48):
                    qs, qn = QT[n % NQ]
                    act.wait_ge(idx_mm, l * 48 + n + 1)
                    if n >= 4:
                        act.wait_ge(idx_used, l * 48 + n - 3)
                    act.activation(relu[0:qn, n % 4, 0:qs + qn], ps[0:qn, 4 + n % 4, 0:qs + qn], ACT.Relu,
                                   scale=SCALE).then_inc(idx_relu, 1)
                for n in range(48 + 2):
                    if n < 48:
                        qs, qn = QT[n % NQ]
                        act.wait_ge(max_made, l * 48 + n + 1)
                        if n >= 2:
                            act.wait_ge(ptr_made, l * 48 + n - 1)
                        act.activation(probs[0:qn, n % 2, 0:qs + qn], ps[0:qn, 4 + n % 2, 0:qs + qn], ACT.Exp,
                                       bias=stat[0:qn, 0, n % 4:n % 4 + 1], scale=SCALE,
                                       accum_out=stat[0:qn, 1, n % 4:n % 4 + 1]).then_inc(prob_made, 1)
                    if n >= 2:
                        m = n - 2
                        kind, hd, q = m // (HEADS * NQ), m // NQ % HEADS, m % NQ
                        qn = QT[q][1]
                        act.wait_ge(den_made, l * 48 + m + 1)
                        act.wait_ge(o_made, l * 48 + m + 1)
                        act.activation(y_tok[0:qn, kind, q, hd * HEAD:(hd + 1) * HEAD], ps[0:qn, 7, 0:HEAD], ACT.Copy,
                                       scale=stat[0:qn, 2, m % 4:m % 4 + 1]).then_inc(o_read, 1)
                g0, b0 = first_group(l, "glu"), first_block(l, "glu")
                for g in range(4):
                    act.wait_ge(block_used, b0 + 2 * (g + 1))
                    for j in range(2):
                        sg = act.activation(proj[:, 2 * g + j, :], ps[:, 2 * (g % 2) + j, 0:NT], ACT.Sigmoid,
                                            bias=param("glu_b", l * UT + 2 * g + j))
                    sg.then_inc(psum_free, 1)
                for g in range(4):
                    act.wait_ge(glu_made, 4 * l + g + 1)
                    act.activation(proj[:, 8 + 2 * g:10 + 2 * g, :], proj[:, 2 * g:2 * g + 2, :], ACT.Square).then_inc(glu_sq, 1)
                act.wait_ge(o_read, 48 * (l + 1))
                for n in range(6):
                    kind, q = n // NQ, n % NQ
                    qn = QT[q][1]
                    if n:
                        act.wait_ge(ysq, 6 * l + n)
                    act.activation(relu[0:qn, 0:2, 0:256], y_tok[0:qn, kind, q, :].rearrange("p (a b) -> p a b", a=2), ACT.Square,
                                   accum_out=stat[0:qn, 3, n:n + 1]).then_inc(ysq, 1)
                act.wait_ge(ysq, 6 * (l + 1))
                for n in range(6):
                    qn = QT[n % NQ][1]
                    act.activation(stat[0:qn, 2, n:n + 1], stat[0:qn, 3, n:n + 1], ACT.Sqrt, bias=RMS_EPS,
                                   scale=1.0 / 512).then_inc(ysd, 1)
                act.wait_ge(glu_ms, l + 1)
                act.activation(rstd[:, :], ps[:, 4, 0:NT], ACT.Sqrt, bias=RMS_EPS, scale=1.0 / SSM_W).then_inc(glu_sd, 1)
                act.wait_ge(ymul, 2 * l + 2)
                for c in range(2):
                    src = proj[:, 0:8, :] if c == 0 else yssm[:, :, :]
                    act.activation(x_hi[:, 8 * c:8 * c + 8, :], src, ACT.Copy).then_inc(yhi_made, 1)
                for n in range(PHASES["out"][0] * PHASES["out"][1]):
                    cast(l, "out", n)
                for n in range(4):
                    cast(l, "up", n)
                layer_norm(ln)
                for c in range(4):
                    act.wait_ge(h_made, 4 * ln + c + 1)
                    act.activation(x_hi[:, 4 * c:4 * c + 4, :], h[:, 4 * c:4 * c + 4, :], ACT.Copy).then_inc(xhi_made, 1)

                def convolve(g, odd, i=0):
                    n = FT * l + g
                    conv_at = PARAM["conv"][0] + n * 8
                    if isinstance(i, int):
                        src = par_t(conv_at + 8 * i)
                    else:
                        src = par[:, bass.ds(i * 8 + conv_at, 8)]
                    act.activation(cpar[:, odd, :], src, ACT.Copy).then_inc(cpar_made, 1)
                    act.wait_ge(cpar_made, i + n + 1)
                    act.wait_ge(block_used, i * 4 + (first_block(l, "up") + 4 * (g + 1)))
                    for j in range(2):
                        act.activation(conv[:, odd, j, :], ps[:, 2 * odd + j, 0:NT], ACT.Identity,
                                       bias=cpar[:, odd, j:j + 1], scale=cpar[:, odd, 2 + j:3 + j]).then_inc(conv_a, 1)
                    act.wait_ge(psum_free, i + (first_group(l, "up") + g + 3))
                    act.activation(gate[:, odd, :], conv[:, odd, 1, :], ACT.Silu).then_inc(gate_made, 1)

                def par_t(at):
                    return par[:, at:at + 8]

                with act.Fori(0, FT - 2, 2) as i:
                    for e in range(2):
                        for n in range(4):
                            cast(l, "up", 4 * (e + 1) + n, loop=i * 16)
                        convolve(e, e, i)
                for n in range(4):
                    cast(l, "up", 4 * (FT - 1) + n)
                convolve(FT - 2, 0)
                for n in range(4):
                    cast(l, "down", n)
                convolve(FT - 1, 1)
                for n in range(4, PHASES["down"][0] * PHASES["down"][1]):
                    cast(l, "down", n)
                layer_norm(ln + 1)

        @block.vector
        def _(dve):
            step = {"n": 0}

            def mark(ins):
                step["n"] += 1
                ins.then_inc(dve_step, 1)
                return step["n"]

            def after(n=None):
                dve.wait_ge(dve_step, step["n"] if n is None else n)

            def spread(ap, n):
                return ap.unsqueeze(1).to_broadcast([ap.shape[0], n, ap.shape[1]])

            def low_part(l, phase, n, loop=0):
                b = first_block(l, phase) + n
                slot = b % SLOTS
                dve.wait_ge(hi_made, loop + (first_split(l, phase) + n + 1))
                dve.tensor_tensor(w_lo[:, slot, :, :], raw[:, slot, :, :], w_hi[:, slot, :, :].bitcast(F32),
                                  ALU.subtract).then_inc(lo_made, 1)

            def layer_norm(n, gain, shift, l=None):
                dve.wait_ge(mean_made, n + 1)
                for c in range(4):
                    h4 = h[:, 4 * c:4 * c + 4, :]
                    dve.scalar_tensor_tensor(out=h4, in0=spread(ps[:, 4, 0:NT], 4), scalar=-1.0 / D_MODEL, in1=h4,
                                             op0=ALU.mult, op1=ALU.add).then_inc(centered, 1)
                dve.wait_ge(dev_made, n + 1)
                mark(dve.reciprocal(rstd[:, :], rstd[:, :]))
                after()
                marks = []
                for c in range(5):
                    if c < 4:
                        h4 = h[:, 4 * c:4 * c + 4, :]
                        marks.append(mark(dve.tensor_tensor(h4, h4, spread(rstd[:, :], 4), ALU.mult)))
                    if c:
                        after(marks[c - 1])
                        for k in range(4 * c - 4, 4 * c):
                            last = dve.tensor_scalar(h[:, k, :], h[:, k, :], param(gain[0], gain[1] + k),
                                                     param(shift[0], shift[1] + k), ALU.mult, ALU.add)
                        last.then_inc(h_made, 1)
                if l is not None:
                    for c in range(4):
                        dve.wait_ge(xhi_made, 4 * l + c + 1)
                        t = slice(4 * c, 4 * c + 4)
                        dve.tensor_tensor(x_lo[:, t, :], h[:, t, :], x_hi[:, t, :].bitcast(F32),
                                          ALU.subtract).then_inc(xlo_made, 1)

            def residual(l, phase, g):
                blocks = PHASES[phase][1]
                dve.wait_ge(block_used, first_block(l, phase) + blocks * (g + 1))
                h2 = h[:, 2 * g:2 * g + 2, :]
                dve.scalar_tensor_tensor(out=h2, in0=h2, scalar=ALPHA, in1=ps[:, 2 * (g % 2):2 * (g % 2) + 2, 0:NT],
                                         op0=ALU.mult, op1=ALU.add).then_inc(psum_free, 1)

            def turns_of(l, pr):
                r = l * 16 + pr
                if r >= 1:
                    dve.wait_ge(table_made, r)
                for e in range(2):
                    mark(dve.tensor_scalar(turns[:, 0, e, :], const("time"), small[:, 3, 2 * pr + e:2 * pr + e + 1],
                                           None, ALU.mult))
                after()
                mark(dve.tensor_scalar(turns[:, 1, :, :], turns[:, 0, :, :], ROUND, ROUND, ALU.add, ALU.subtract))
                after()
                dve.tensor_tensor(turns[:, 0, :, :], turns[:, 0, :, :], turns[:, 1, :, :], ALU.subtract).then_inc(turns_made, 1)

            def scan_pair(l, pr):
                r = l * 16 + pr
                t1, t2, w, z = (rot[:, c, :, :, :] for c in range(4))
                tb = table[:, pr % 2, :, :, :]
                if r:
                    dve.wait_ge(s_made, r)
                dve.wait_ge(bu_made, r + 1)
                dve.wait_ge(table_made, r + 1)
                for e in range(2):
                    bu = ps[:, 4 + 2 * e:6 + 2 * e, 0:NT]
                    dve.tensor_tensor(t1[:, e, :, :], bu, spread(tb[:, 0, e, :], 2), ALU.mult)
                    dve.tensor_tensor(t2[:, e, ::-1, :], bu, tb[:, 2:4, e, :], ALU.mult).then_inc(bu_read, 1)
                turned = []
                for e in range(2):
                    dve.wait_ge(bu_read, 2 * r + 1 + e)
                    turned.append(mark(dve.tensor_tensor(w[:, e, :, :], t1[:, e, :, :], t2[:, e, :, :], ALU.add)))
                summed = []
                for e in range(2):
                    after(turned[e])
                    decay = small[:, 4, 2 * pr + e:2 * pr + e + 1].to_broadcast([P, NT])
                    for c in range(2):
                        last = dve.tensor_tensor_scan(z[:, e, c, :], decay, w[:, e, c, :], 0.0, ALU.mult, ALU.add)
                    summed.append(mark(last))
                back = []
                for e in range(2):
                    after(summed[e])
                    dve.tensor_tensor(t1[:, e, :, :], z[:, e, :, :], spread(tb[:, 0, e, :], 2), ALU.mult)
                    back.append(mark(dve.tensor_tensor(t2[:, e, ::-1, :], z[:, e, :, :], tb[:, 1:3, e, :], ALU.mult)))
                if r >= 2:
                    dve.wait_ge(s_used, r - 1)
                for e in range(2):
                    after(back[e])
                    last = dve.tensor_tensor(states[:, pr % 2, e, :, :], t1[:, e, :, :], t2[:, e, :, :], ALU.add)
                last.then_inc(s_made, 1)

            def read_state_output(l, m):
                dve.wait_ge(s_used, l * 16 + 2 * m + 2)
                dve.scalar_tensor_tensor(out=yssm[:, m, :], in0=proj[:, U0 + m, :], scalar=param("d_skip", l * UT + m),
                                         in1=ps[:, m % 2, 0:NT], op0=ALU.mult, op1=ALU.add).then_inc(y_read, 1)

            dve.memset(rstd[:, :], 0.0).then_inc(psum_free, 2)
            dve.wait_ge(x_loaded, 16)
            dve.wait_ge(par_loaded, 16)
            layer_norm(0, ("ln_in_g", 0), ("ln_in_b", 0))
            for l in range(DEPTH):
                ln = 2 * l + 1
                with dve.Fori(0, 9) as it:
                    for g in range(2):
                        dve.wait_ge(block_used, it * 8 + (first_block(l, "in") + 4 * (g + 1)))
                        dve.tensor_scalar(proj[:, bass.ds(it * 4 + 2 * g, 2), :], ps[:, 2 * g:2 * g + 2, 0:NT], 1.0, None,
                                          ALU.mult).then_inc(psum_free, 1)
                dve.wait_ge(psum_free, first_group(l, "in") + 18 + 2)
                dve.wait_ge(mix_loaded, 64 * (l + 1))
                sm = [small[:, c, :] for c in range(20)]
                lr, li = param("lam_re", l * ST, ST), param("lam_im", l * ST, ST)
                dve.wait_ge(dt_made, l + 1)
                mark(dve.tensor_tensor(sm[1], lr, sm[0], ALU.mult))
                mark(dve.tensor_tensor(sm[2], li, sm[0], ALU.mult))
                after()
                mark(dve.tensor_scalar(sm[8], sm[2], 1.0 / (2.0 * np.pi), None, ALU.mult))
                after()
                mark(dve.tensor_scalar(sm[9], sm[8], ROUND, ROUND, ALU.add, ALU.subtract))
                after()
                mark(dve.tensor_tensor(sm[3], sm[8], sm[9], ALU.subtract))
                after()
                mark(dve.scalar_tensor_tensor(out=sm[7], in0=sm[3], scalar=-1.0, in1=sm[3], op0=ALU.mult, op1=ALU.max))
                after()
                dve.tensor_tensor(sm[13], lr, lr, ALU.mult).then_inc(freq_made, 1)
                mark(dve.tensor_tensor(sm[14], li, li, ALU.mult))
                turns_of(l, 0)
                dve.wait_ge(trig_made, 3 * (l + 1))
                dve.wait_ge(freq_made, l + 1)
                mark(dve.tensor_tensor(sm[10], sm[4], sm[6], ALU.mult))
                mark(dve.tensor_tensor(sm[11], sm[4], sm[5], ALU.mult))
                mark(dve.tensor_tensor(sm[13], sm[13], sm[14], ALU.add))
                after()
                mark(dve.tensor_scalar(sm[10], sm[10], 1.0, None, ALU.subtract))
                mark(dve.reciprocal(sm[13], sm[13]))
                after()
                mark(dve.tensor_tensor(sm[15], sm[10], lr, ALU.mult))
                mark(dve.tensor_tensor(sm[16], sm[11], li, ALU.mult))
                mark(dve.tensor_tensor(sm[17], sm[11], lr, ALU.mult))
                mark(dve.tensor_tensor(sm[18], sm[10], li, ALU.mult))
                after()
                mark(dve.tensor_tensor(sm[15], sm[15], sm[16], ALU.add))
                mark(dve.tensor_tensor(sm[17], sm[17], sm[18], ALU.subtract))
                after()
                mark(dve.tensor_tensor(sm[15], sm[15], sm[13], ALU.mult))
                mark(dve.tensor_tensor(sm[17], sm[17], sm[13], ALU.mult))
                after()
                tmp = [rot[:, c, :, :, :].rearrange("p a b t -> p (a b t)")[:, 0:ST * 32].rearrange("p (s c) -> p s c", c=32)
                       for c in range(4)]
                zr, zi = (sm[c].unsqueeze(2).to_broadcast([P, ST, 32]) for c in (15, 17))
                c_re, c_im = c_st[:, 0, :, :], c_st[:, 1, :, :]
                mark(dve.tensor_tensor(tmp[0], c_re, zr, ALU.mult))
                mark(dve.tensor_tensor(tmp[1], c_im, zi, ALU.mult))
                mark(dve.tensor_tensor(tmp[2], c_re, zi, ALU.mult))
                mark(dve.tensor_tensor(tmp[3], c_im, zr, ALU.mult))
                after()
                mark(dve.tensor_tensor(c_re, tmp[0], tmp[1], ALU.subtract))
                dve.scalar_tensor_tensor(out=c_im, in0=tmp[2], scalar=-1.0, in1=tmp[3], op0=ALU.mult,
                                         op1=ALU.subtract).then_inc(c_made, 1)
                for pr in range(16):
                    if pr < 15:
                        turns_of(l, pr + 1)
                    scan_pair(l, pr)
                    if pr >= 2 and pr % 2 == 0:
                        read_state_output(l, pr // 2 - 1)
                read_state_output(l, UT - 1)
                x, e_, c, nc_ = (ltmp[0:8, k, :] for k in (2, 1, 3, 4))
                mark(dve.tensor_scalar(x, proj[0:8, FFIW, :], param("f_bias", l, rows=8), None, ALU.add))
                after()
                dve.scalar_tensor_tensor(out=e_, in0=x, scalar=-1.0, in1=x, op0=ALU.mult, op1=ALU.min).then_inc(f_neg, 1)
                dve.tensor_tensor(ltmp[:, 0, :], proj[:, CKV, :], proj[:, CKV, :], ALU.mult).then_inc(ckv_sq, 1)

                def rope(r, tile, tn):
                    dve.wait_ge(rot_made, 5 * l + r + 1)
                    mark(dve.tensor_tensor(rope_t[:, 0:tn, :], ps[:, 4:4 + tn, 0:NT], spread(const("rope_s"), tn), ALU.mult))
                    mark(dve.tensor_tensor(tile, tile, spread(const("rope_c"), tn), ALU.mult))
                    after()
                    dve.tensor_tensor(tile, tile, rope_t[:, 0:tn, :], ALU.add).then_inc(roped, 1)

                for r, (t0, tn) in enumerate(((DQ0, 4), (IQ0, 4), (IQ0 + 4, 4), (IK, 1))):
                    rope(r, proj[:, t0:t0 + tn, :], tn)
                dve.wait_ge(ckv_sd, l + 1)
                mark(dve.reciprocal(rstd[:, :], rstd[:, :]))
                after()
                dve.scalar_tensor_tensor(out=proj[:, PADT, :], in0=proj[:, CKV, :], scalar=param("kv_g", l), in1=rstd[:, :],
                                         op0=ALU.mult, op1=ALU.mult).then_inc(ckv_normed, 1)
                dve.wait_ge(f_ln, l + 1)
                mark(dve.scalar_tensor_tensor(out=x, in0=x, scalar=0.0, in1=e_, op0=ALU.min, op1=ALU.subtract))
                after()
                mark(dve.tensor_tensor_scan(c, ones[0:8, 0:1].to_broadcast([8, NT]), x, 0.0, ALU.mult, ALU.add))
                after()
                dve.tensor_scalar(nc_, c, -1.0, None, ALU.mult).then_inc(cum_made, 1)
                dve.wait_ge(kv_made, 2 * l + 1)
                rope(4, kv[:, 0:4, :], 4)
                dve.wait_ge(iwt_made, l + 1)
                for q, (qs, qn) in enumerate(QT):
                    last = dve.tensor_scalar(iw_tok[0:qn, q, 0:24], ps[0:qn, 6, 32 * q:32 * q + 24], IDX_HEADS ** -0.5, None,
                                             ALU.mult)
                last.then_inc(iw_made, 1)
                dve.wait_ge(iw_made, l + 1)
                for n in range(IDX_HEADS * NQ):
                    j, q = n // NQ, n % NQ
                    qs, qn = QT[q]
                    acc = work[0:qn, 0, q, 0:qs + qn]
                    src, wt = relu[0:qn, n % 4, 0:qs + qn], iw_tok[0:qn, q, 8 + j:9 + j]
                    dve.wait_ge(idx_relu, l * 48 + n + 1)
                    if j == 0:
                        dve.tensor_scalar(acc, src, wt, None, ALU.mult).then_inc(idx_used, 1)
                    else:
                        dve.wait_ge(idx_used, l * 48 + n - 2)
                        dve.scalar_tensor_tensor(out=acc, in0=src, scalar=wt, in1=acc, op0=ALU.mult,
                                                 op1=ALU.add).then_inc(idx_used, 1)
                dve.wait_ge(idx_used, 48 * (l + 1))
                marks = []
                for q, (qs, qn) in enumerate(QT):
                    d = work[0:qn, 0, q, qs:qs + qn]
                    marks.append(mark(dve.tensor_tensor(d, d, const("causal", qn, qn), ALU.add)))
                for rnd in range(TOPK // 8):
                    for q, (qs, qn) in enumerate(QT):
                        after(marks[q])
                        marks[q] = mark(dve.max(top8[0:qn, q, :], work[0:qn, rnd % 2, q, 0:qs + qn]))
                    for q, (qs, qn) in enumerate(QT):
                        after(marks[q])
                        marks[q] = mark(dve.match_replace(work[0:qn, 1 - rnd % 2, q, 0:qs + qn], top8[0:qn, q, :],
                                                          work[0:qn, rnd % 2, q, 0:qs + qn], TAKEN))
                for q, (qs, qn) in enumerate(QT):
                    after(marks[q])
                    marks[q] = mark(dve.tensor_scalar(dsa_bias[0:qn, q, 0:qs + qn], work[0:qn, 0, q, 0:qs + qn], TAKEN, 1.0,
                                                      ALU.is_equal, ALU.subtract))
                for q, (qs, qn) in enumerate(QT):
                    after(marks[q])
                    marks[q] = mark(dve.tensor_scalar(dsa_bias[0:qn, q, 0:qs + qn], dsa_bias[0:qn, q, 0:qs + qn], -NEG, None,
                                                      ALU.mult))
                for q, (qs, qn) in enumerate(QT):
                    after(marks[q])
                    d = dsa_bias[0:qn, q, qs:qs + qn]
                    last = dve.tensor_tensor(d, d, const("causal", qn, qn), ALU.add)
                last.then_inc(bias_made, 1)
                for n in range(48 + 1):
                    if n < 48:
                        qs, qn = QT[n % NQ]
                        dve.wait_ge(score_made, l * 48 + n + 1)
                        mark(dve.reduce_max(stat[0:qn, 0, 4 + n % 4:5 + n % 4], ps[0:qn, 4 + n % 2, 0:qs + qn], AX_X))
                        after()
                        dve.tensor_scalar(stat[0:qn, 0, n % 4:n % 4 + 1], stat[0:qn, 0, 4 + n % 4:5 + n % 4], -SCALE, None,
                                          ALU.mult).then_inc(max_made, 1)
                    if n:
                        m = n - 1
                        q = m % NQ
                        qn = QT[q][1]
                        dve.wait_ge(ptr_made, l * 48 + m + 1)
                        if m >= 2:
                            dve.wait_ge(o_made, l * 48 + m - 1)
                        dve.tensor_copy(pt[0:MASK_T, m % 2, 0:q + 1, 0:qn],
                                        ps[0:MASK_T, 6, 0:NQ * MASK_T].rearrange("p (c t) -> p c t", c=NQ)[:, 0:q + 1, 0:qn]
                                        ).then_inc(pt_made, 1)
                        dve.reciprocal(stat[0:qn, 2, m % 4:m % 4 + 1], stat[0:qn, 1, m % 4:m % 4 + 1]).then_inc(den_made, 1)
                for g in range(4):
                    dve.wait_ge(psum_free, first_group(l, "glu") + g + 3)
                    y2 = proj[:, 2 * g:2 * g + 2, :]
                    dve.tensor_tensor(y2, y2, yssm[:, 2 * g:2 * g + 2, :], ALU.mult).then_inc(glu_made, 1)
                for n in range(6):
                    kind, q = n // NQ, n % NQ
                    qn = QT[q][1]
                    dve.wait_ge(ysd, 6 * l + n + 1)
                    mark(dve.reciprocal(stat[0:qn, 2, n:n + 1], stat[0:qn, 2, n:n + 1]))
                    after()
                    y = y_tok[0:qn, kind, q, :]
                    dve.tensor_scalar(y, y, stat[0:qn, 2, n:n + 1], None, ALU.mult).then_inc(ynorm, 1)
                dve.wait_ge(glu_sd, l + 1)
                mark(dve.reciprocal(rstd[:, :], rstd[:, :]))
                after()
                mark(dve.tensor_tensor(proj[:, 0:8, :], proj[:, 0:8, :], spread(rstd[:, :], 8), ALU.mult))
                for n in range(6):
                    kind, q = n // NQ, n % NQ
                    qs, qn = QT[q]
                    dve.wait_ge(yt_mm, 6 * l + n + 1)
                    dve.tensor_copy(yssm[:, 4 * kind:4 * kind + 4, qs:qs + qn],
                                    ps[:, 5 + n % 2, 0:4 * MASK_T].rearrange("p (c t) -> p c t", c=4)[:, :, 0:qn]
                                    ).then_inc(yt_made, 1)
                after()
                dve.wait_ge(yt_made, 6 * (l + 1))
                for c in range(2):
                    for k in range(8):
                        y = proj[:, k, :] if c == 0 else yssm[:, k, :]
                        last = dve.tensor_scalar(y, y, param("mix_g", l * DT + 8 * c + k), None, ALU.mult)
                    last.then_inc(ymul, 1)
                for c in range(2):
                    dve.wait_ge(yhi_made, 2 * l + c + 1)
                    src = proj[:, 0:8, :] if c == 0 else yssm[:, :, :]
                    dve.tensor_tensor(x_lo[:, 8 * c:8 * c + 8, :], src, x_hi[:, 8 * c:8 * c + 8, :].bitcast(F32),
                                      ALU.subtract).then_inc(ylo_made, 1)
                for g in range(8):
                    for n in range(4):
                        low_part(l, "out", 4 * g + n)
                    if g:
                        residual(l, "out", g - 1)
                for n in range(4):
                    low_part(l, "up", n)
                residual(l, "out", 7)
                layer_norm(ln, ("ln1_g", l * DT), ("ln1_b", l * DT), l)

                def convolve(g, odd, i=0):
                    n = FT * l + g
                    cv = conv[:, odd, :, :]
                    dve.wait_ge(conv_a, i * 2 + 2 * n + 2)
                    for tap in (1, 2):
                        if tap == 2:
                            dve.wait_ge(conv1_made, i * 2 + 2 * n + 2)
                        for j in range(2):
                            last = dve.scalar_tensor_tensor(
                                out=cv[:, j, tap:NT], in0=ps[:, 2 * odd + j, 0:NT - tap],
                                scalar=cpar[:, odd, 2 + 2 * tap + j:3 + 2 * tap + j], in1=cv[:, j, tap:NT],
                                op0=ALU.mult, op1=ALU.add)
                            if tap == 1:
                                last.then_inc(conv1_made, 1)
                    last.then_inc(psum_free, 1)
                    dve.wait_ge(gate_made, i + n + 1)
                    hi = g_hi[:, g:g + 1, :] if isinstance(i, int) else g_hi[:, bass.ds(i + g, 1), :]
                    lo = g_lo[:, g:g + 1, :] if isinstance(i, int) else g_lo[:, bass.ds(i + g, 1), :]
                    pr_ = prod[:, odd:odd + 1, :]
                    dve.tensor_tensor(pr_, gate[:, odd:odd + 1, :], cv[:, 0:1, :], ALU.mult).then_inc(prod_made, 1)
                    dve.tensor_tensor(hi, gate[:, odd:odd + 1, :], cv[:, 0:1, :], ALU.mult).then_inc(ghi_made, 1)
                    dve.wait_ge(prod_made, i + n + 1)
                    dve.wait_ge(ghi_made, i + n + 1)
                    dve.tensor_tensor(lo, pr_, hi.bitcast(F32), ALU.subtract).then_inc(g_made, 1)

                with dve.Fori(0, FT - 2, 2) as i:
                    for e in range(2):
                        for n in range(4):
                            low_part(l, "up", 4 * (e + 1) + n, loop=i * 4)
                        convolve(e, e, i)
                for n in range(4):
                    low_part(l, "up", 4 * (FT - 1) + n)
                convolve(FT - 2, 0)
                for n in range(4):
                    low_part(l, "down", n)
                convolve(FT - 1, 1)
                blocks = PHASES["down"][1]
                for g in range(8):
                    for n in range(4, blocks + 4):
                        if g * blocks + n < 8 * blocks:
                            low_part(l, "down", g * blocks + n)
                    residual(l, "down", g)
                layer_norm(ln + 1, ("ln2_g", l * DT), ("ln2_b", l * DT))


def feature_major(a):
    t, f = a.shape
    return a.T.reshape(f // P, P, t).transpose(1, 0, 2)


def blocks_of(w):
    k, m = w.shape
    return w.reshape(k // (KB * P), KB, P, m // (2 * P), 2 * P).transpose(3, 0, 2, 1, 4).reshape(-1, P, KB * 2 * P)


def constants():
    c = np.zeros((P, CONST_COLS), np.float32)

    def put(name, a):
        at, n = CONST[name]
        c[:a.shape[0], at:at + n] = a

    put("ident", np.eye(P))
    put("ones", np.ones((P, P)))
    rot = HEAD // 4
    perm = np.zeros((P, P))
    freq = np.float32(500000.0) ** (-np.arange(0, rot, 2, dtype=np.float32) / np.float32(rot))
    ang = np.arange(NT, dtype=np.float32)[None, :] * freq[:, None]
    cos, sin = np.ones((P, NT)), np.zeros((P, NT))
    for m in range(P):
        d = m % HEAD
        if d < rot:
            perm[m + rot // 2 if d < rot // 2 else m - rot // 2, m] = 1.0
            cos[m] = np.cos(ang[d % (rot // 2)])
            sin[m] = np.sin(ang[d % (rot // 2)]) * (-1 if d < rot // 2 else 1)
    put("perm", perm)
    put("rope_c", cos)
    put("rope_s", sin)
    put("time", np.tile(np.arange(NT) - NT // 2, (P, 1)))
    put("causal", np.where(np.arange(MASK_T)[None, :] <= np.arange(MASK_T)[:, None], 0.0, NEG))
    put("sel8", np.eye(HEADS) / SCALE)
    return c


def lay_out(i):
    z = np.zeros
    x = feature_major(np.concatenate([i["meta_tokens"], i["x"][0]], 0))
    stream = []
    for l in range(DEPTH):
        w = i["w_in"][l]
        at = np.cumsum([0, 1024, 512, 512, 512, 8, 512, 128, 1024, 64, 16])
        u, fq, fk, fv, ff, dq, ckv, iq, ik, iw = (w[:, at[n]:at[n + 1]] for n in range(10))
        pad = z((D_MODEL, P - 24), np.float32)
        stream.append(blocks_of(np.concatenate([u, fq, fk, fv, dq, iq, ckv, ff, iw, pad, ik, ik,
                                                z((D_MODEL, P), np.float32)], 1)))
        stream.append(blocks_of(i["ssm_glu_w"][l]))
        stream.append(blocks_of(i["w_out"][l]))
        stream.append(blocks_of(i["w_up"][l].reshape(D_MODEL, 2, FT, P).transpose(0, 2, 1, 3).reshape(D_MODEL, -1)))
        stream.append(blocks_of(i["w_down"][l]))
    params = z((P, PARAM_COLS), np.float32)

    def put(name, a):
        o, n = PARAM[name]
        params[:a.shape[0], o:o + n] = a

    def tiles(a):
        return a.reshape(-1, P).T

    for name, key in (("ln_in_g", "ln_in_g"), ("ln_in_b", "ln_in_b"), ("ln1_g", "ln1_g"), ("ln1_b", "ln1_b"),
                      ("ln2_g", "ln2_g"), ("ln2_b", "ln2_b"), ("mix_g", "mix_norm_g"), ("glu_b", "ssm_glu_b"),
                      ("d_skip", "ssm_d"), ("kv_g", "kv_norm_g")):
        put(name, tiles(i[key]))
    put("f_bias", i["fox_f_bias"].T)
    taps = np.concatenate([i["conv_b"][:, None], i["conv_w"][:, ::-1]], 1)
    put("conv", taps.reshape(DEPTH, 4, 2, FT, P).transpose(4, 0, 3, 1, 2).reshape(P, -1))
    for name in ("lam_re", "lam_im"):
        put(name, i["ssm_" + name].reshape(DEPTH, ST, 2, STATE).transpose(2, 3, 0, 1).reshape(P, -1))
    put("log_dt", np.broadcast_to(i["ssm_log_dt"].reshape(DEPTH, ST, 2, 1), (DEPTH, ST, 2, STATE)
                                  ).transpose(2, 3, 0, 1).reshape(P, -1))
    b = z((DEPTH, 4, 2, GROUP, 2, UT, 2, STATE), np.float32)
    c = z((DEPTH, 2, STATE, 2, ST, 2, GROUP), np.float32)
    for part, (bk, ck) in enumerate((("ssm_b_re", "ssm_c_re"), ("ssm_b_im", "ssm_c_im"))):
        bb = i[bk].reshape(DEPTH, UT, 4, 2, STATE, GROUP)
        cc = i[ck].reshape(DEPTH, ST, 2, GROUP, STATE)
        for half in range(2):
            b[:, :, half, :, part, :, half, :] = bb[:, :, :, half].transpose(0, 2, 4, 1, 3)
            c[:, half, :, part, :, half, :] = cc[:, :, half].transpose(0, 3, 1, 2)
    return {"x": np.ascontiguousarray(x), "stream": np.concatenate(stream, 0), "consts": constants(), "params": params,
            "ssm_b": b.reshape(DEPTH, P, 2, UT, P), "ssm_c": c.reshape(DEPTH, P, 2, ST, 32),
            "w_kv": np.ascontiguousarray(i["w_kv_up"])}


def kernel(**inputs):
    import concourse.bacc as bacc
    from concourse.bass_utils import run_bass_kernel_spmd

    arrays = lay_out({n: np.asarray(a) for n, a in inputs.items()})
    nc = bacc.Bacc("TRN2", target_bir_lowering=False, num_devices=1)
    aps = {n: nc.dram_tensor(n, a.shape, F32, kind="ExternalInput").ap() for n, a in arrays.items()}
    out = nc.dram_tensor("out", (P, DT, NT), F32, kind="ExternalOutput").ap()
    hybrid_trunk(nc, **aps, out=out)
    r = run_bass_kernel_spmd(nc, [arrays], core_ids=[0])
    tokens = np.asarray(r.results[0]["out"]).transpose(2, 1, 0).reshape(NT, D_MODEL)
    return tokens[N_META:][None]
```

```python
from contextlib import ExitStack

import concourse.bass as bass
import numpy as np
from concourse import mybir

F32 = mybir.dt.float32
F32R = mybir.dt.float32r
ALU = mybir.AluOpType
ACT = mybir.ActivationFunctionType
AX_X = mybir.AxisListType.X

P = 128
D_MODEL, SEQ, N_META, DEPTH = 2048, 256, 16, 2
NT = SEQ + N_META
HEAD = 64
SSM_W, GROUP, STATE = D_MODEL // 2, 16, 64
HEADS = 8
KV_RANK = 128
IDX_HEADS = 16
TOPK = min(256, SEQ // 4)
D_FF = 11 * D_MODEL // 4
ALPHA = (2.0 * DEPTH) ** 0.25
LN_EPS, RMS_EPS = 1e-5, 1e-6
NEG = -1e30
HALF_PI = 1.5707963
TAKEN = -3e38
SCALE = HEAD ** -0.5
TWO_PI_LOW = 6.283185
ROUND = 12582912.0

DT = D_MODEL // P
FT = D_FF // P
UT = SSM_W // P
ST = SSM_W // GROUP * STATE // P
MASK_T = 96
QT = [(s, min(MASK_T, NT - s)) for s in range(0, NT, MASK_T)]
NQ = len(QT)

KB = 4
SLOTS = 4
PHASES = {"in": (18, DT // KB, 1), "glu": (4, UT // KB, 4), "out": (8, DT // KB, 2),
          "up": (FT, DT // KB, 2), "down": (8, FT // KB, 4)}
SPLIT = ("in", "out", "up", "down")
BLOCKS_PER_LAYER = sum(g * b for g, b, _ in PHASES.values())
GROUPS_PER_LAYER = sum(g for g, _, _ in PHASES.values())
SPLIT_PER_LAYER = sum(PHASES[p][0] * PHASES[p][1] for p in SPLIT)


def first_block(layer, phase):
    names = list(PHASES)
    return layer * BLOCKS_PER_LAYER + sum(PHASES[n][0] * PHASES[n][1] for n in names[:names.index(phase)])


def first_group(layer, phase):
    names = list(PHASES)
    return layer * GROUPS_PER_LAYER + sum(PHASES[n][0] for n in names[:names.index(phase)])


def first_split(layer, phase):
    return layer * SPLIT_PER_LAYER + sum(PHASES[n][0] * PHASES[n][1] for n in SPLIT[:SPLIT.index(phase)])


def first_low(layer, phase):
    mine = ("in",) if phase == "in" else ("out", "up", "down")
    size = {p: PHASES[p][0] * PHASES[p][1] for p in mine}
    return layer * sum(size.values()) + sum(size[p] for p in mine[:mine.index(phase)])


U0, IQ0, CKV, FFIW, IK, PADT, DQ0, FK0, FV0, FQ0 = 0, 8, 16, 17, 18, 19, 20, 24, 28, 32

PAIRS = ST // 2
GROUPS_IN = PHASES["in"][0]
STEPS = GROUPS_IN
ROPE_STEPS = {4: (0, 1), 5: (2, 3), 6: (4, 5), 7: (6, 7), 9: (8,), 10: (9, 10), 11: (11, 12), 16: (13, 14), 17: (15, 16)}
ROPES = 17
MS_STEP = 8
KV_STEPS = {12: (0, 1), 13: (2, 3), 14: (4, 5), 15: (6, 7)}
GATE_STEP = 10
IN_BLOCKS = PHASES["in"][0] * PHASES["in"][1]
CHUNKS = DT // 2
LAST_T0 = (N_META - 2, N_META)

UNITS = 2 * HEADS * NQ
V_BANKS = (4, 5, 7, 0, 1, 3)
GATE_NORM = 3
FOX_NORM = UNITS // 2 + 2

CONST = {}
_at = 0
for _name, _cols in (("ident", P), ("ones", P), ("perm", P), ("rope_c", NT), ("rope_s", NT), ("time", NT),
                     ("causal", MASK_T), ("sel", 2 * HEADS)):
    CONST[_name] = (_at, _cols)
    _at += _cols
CONST_COLS = _at

PARAM = {}
_at = 0
for _name, _cols in (("ln_in_g", DT), ("ln_in_b", DT), ("ln1_g", DEPTH * DT), ("ln1_b", DEPTH * DT),
                     ("ln2_g", DEPTH * DT), ("ln2_b", DEPTH * DT), ("mix_g", DEPTH * DT),
                     ("conv", DEPTH * FT * 8), ("glu_b", DEPTH * UT),
                     ("d_skip", DEPTH * UT), ("kv_g", DEPTH), ("f_bias", DEPTH),
                     ("lam_re", DEPTH * ST), ("lam_im", DEPTH * ST), ("log_dt", DEPTH * ST)):
    PARAM[_name] = (_at, _cols)
    _at += _cols
PARAM_COLS = _at


def hybrid_trunk(nc, x, stream, consts, params, ssm_b, ssm_c, w_kv, out):
    with ExitStack() as ctx:
        def sem(name):
            return ctx.enter_context(nc.semaphore(name))

        base = (nc.sbuf_base + 63) // 64 * 64
        cursor = {"at": base}

        def place(name, shape, dt=F32, at=None):
            size = 4 * int(np.prod(shape[1:]))
            where = cursor["at"] if at is None else at
            t = nc.alloc_sbuf_tensor_at(name, shape, dt, offset=where)
            if at is None:
                cursor["at"] += (size + 31) // 32 * 32
            return t, where + (size + 31) // 32 * 32

        h, _ = place("h", [P, DT, NT])
        x_lo, _ = place("x_lo", [P, DT, NT], F32R, at=base)
        raw_at = cursor["at"]
        raw, _ = place("raw", [P, SLOTS, KB, 2 * P])
        in_lo, _ = place("in_lo", [P, SLOTS, KB, 2 * P], F32R, at=raw_at)
        w_hi, _ = place("w_hi", [P, SLOTS, KB, 2 * P], F32R)
        par, _ = place("par", [P, PARAM_COLS])
        ones, _ = place("ones_p", [P, P])
        rstd, _ = place("rstd", [P, NT])
        low = cursor["at"]
        x_hi, e = place("x_hi", [P, DT, NT], F32R, at=low)
        high = e
        g_hi, e = place("g_hi", [P, FT, NT], F32R, at=high)
        g_lo, ffn_end = place("g_lo", [P, FT, NT], F32R, at=e)
        squares, _ = place("squares", [P, DT, NT], at=high)
        conv, e = place("conv", [P, 2, 2, NT], at=ffn_end)
        gate, e = place("gate", [P, 2, NT], at=e)
        prod, e = place("prod", [P, 2, NT], at=e)
        cpar, e = place("cpar", [P, 2, 8], at=e)
        w_lo, e = place("w_lo", [P, SLOTS, KB, 2 * P], F32R, at=e)
        w_lo_end = e
        hsum, _ = place("hsum", [P, 2, NT], at=ffn_end)
        assert e <= nc.sbuf_usable_end, (e, nc.sbuf_usable_end)
        end = nc.sbuf_usable_end
        proj, e = place("proj", [P, 36, NT], at=high)
        kv, e = place("kv", [P, 8, NT], at=e)
        y_lo = [place("gated_lo", [P, UT, NT], F32R, at=high)[0], place("attended_lo", [P, UT, NT], F32R, at=e)[0]]
        yssm, e = place("yssm", [P, UT, NT], at=e)
        wkv, e = place("wkv", [P, 1024], at=e)
        cst, e = place("cst", [P, CONST_COLS], at=e)
        small, e = place("small", [P, 20, ST], at=e)
        ident_r, e = place("ident_r", [P, MASK_T], F32R, at=e)
        causal_r, e = place("causal_r", [P, MASK_T], F32R, at=e)
        sel_r, e = place("sel_r", [P, 2 * HEADS], F32R, at=e)
        mixer_end = e
        v_tok, e = place("v_tok", [P, 2, NQ, 512], at=mixer_end)
        y_tok, e = place("y_tok", [P, 2, NQ, 512], at=e)
        gate_sq, _ = place("gate_sq", [P, UT, NT], at=e - UT * NT * 4)
        work, e2 = place("work", [P, 2, NQ, NT], at=e)
        probs, e2 = place("probs", [P, 2, NT], at=e2)
        pt, e2 = place("pt", [P, 2, NQ, MASK_T], at=e2)
        relu, e2 = place("relu", [P, 4, NT], at=e2)
        dsa_bias, e = place("dsa_bias", [P, NQ, NT], F32R, at=e2)
        top8, e = place("top8", [P, NQ, 8], at=e)
        iw_tok, e = place("iw_tok", [P, NQ, 32], at=e)
        stat, e = place("stat", [P, 5, 8], at=e)
        attention_end = e
        y_at = (end - DT * NT * 4) // 32 * 32
        assert e <= y_at and w_lo_end <= y_at
        y_hi, e = place("y_hi", [P, DT, NT], F32R, at=y_at)
        table, e = place("table", [P, 2, 4, 2, NT], at=mixer_end)
        turns, e = place("turns", [P, 2, 2, NT], at=e)
        states, e = place("states", [P, 2, 2, 2, NT], at=e)
        side, e = place("side", [P, 2, NT], at=e)
        rot, e = place("rot", [P, 4, 2, 2, NT], at=e)
        b_st, e = place("b_st", [P, 2, UT, P], at=e)
        c_st, e = place("c_st", [P, 2, ST, 32], at=e)
        fgate, e = place("fgate", [8, 2, NT], at=e)
        cum, e = place("cum", [P, NT], F32R, at=e)
        assert y_at + UT * NT * 4 <= e - NT * 4 and e <= end, (e, end)

        ps = ctx.enter_context(nc.psum_tensor("ps", [P, 8, 512], F32))

        def const(name, rows=P, cols=None):
            at, n = CONST[name]
            return cst[0:rows, at:at + (cols or n)]

        def rope_tile(r):
            if r < 9:
                return proj[:, IQ0 + r if r < 8 else IK, :]
            return proj[:, DQ0 + r - 9, :] if r < 13 else kv[:, r - 13, :]

        def w_low(phase, slot):
            return (in_lo if phase == "in" else w_lo)[:, slot, :, :]

        def param(name, at, n=1, rows=P):
            o = PARAM[name][0] + at
            return par[0:rows, o:o + n]

        w_loaded = [sem(f"w_loaded{s}") for s in range(SLOTS)]
        block_used = sem("block_used")
        hi_made, in_lo_made, lo_made = sem("hi_made"), sem("in_lo_made"), sem("lo_made")
        psum_free = sem("psum_free")
        x_loaded, par_loaded, mix_loaded, ones_made = sem("x_loaded"), sem("par_loaded"), sem("mix_loaded"), sem("ones_made")
        mean_made, centered, squared, var_made, dev_made = (sem(n) for n in (
            "mean_made", "centered", "squared", "var_made", "dev_made"))
        h_summed, sq_summed, scaled = sem("h_summed"), sem("sq_summed"), sem("scaled")
        h_made, xhi_made, xlo_made = sem("h_made"), sem("xhi_made"), sem("xlo_made")
        dt_made, freq_made, trig_made, c_made = (sem(n) for n in ("dt_made", "freq_made", "trig_made", "c_made"))
        turns_made, table_made, bu_made, bu_read, s_made, s_used, abs_made, y_read = (sem(n) for n in (
            "turns_made", "table_made", "bu_made", "bu_read", "s_made", "s_used", "abs_made", "y_read"))
        gelu_made, sig_made, glu_made, glu_sq, glu_ms, glu_sd, ymul = (sem(n) for n in (
            "gelu_made", "sig_made", "glu_made", "glu_sq", "glu_ms", "glu_sd", "ymul"))
        glu_summed = sem("glu_summed")
        rot_made, roped = sem("rot_made"), sem("roped")
        ckv_sq, ckv_ms, ckv_sd, ckv_normed, kv_mm, kv_made = (sem(n) for n in (
            "ckv_sq", "ckv_ms", "ckv_sd", "ckv_normed", "kv_mm", "kv_made"))
        f_neg, f_exp, f_ln, cum_made = sem("f_neg"), sem("f_exp"), sem("f_ln"), sem("cum_made")
        vt_made, v_made = sem("vt_made"), sem("v_made")
        iwt_made, iw_made = sem("iwt_made"), sem("iw_made")
        idx_mm, idx_relu, idx_used, bias_made = sem("idx_mm"), sem("idx_relu"), sem("idx_used"), sem("bias_made")
        score_made, max_made, prob_made, ptr_made, pt_made, o_made, den_made, o_read = (sem(n) for n in (
            "score_made", "max_made", "prob_made", "ptr_made", "pt_made", "o_made", "den_made", "o_read"))
        ysq, ysd, ynorm, yt_mm, yt_made = (sem(n) for n in ("ysq", "ysd", "ynorm", "yt_mm", "yt_made"))
        yhi_made, ylo_made = sem("yhi_made"), sem("ylo_made")
        cpar_made, conv_a, conv1_made, gate_made = sem("cpar_made"), sem("conv_a"), sem("conv1_made"), sem("gate_made")
        prod_made, ghi_made, g_made = sem("prod_made"), sem("ghi_made"), sem("g_made")
        dve_step = sem("dve_step")
        stored = sem("stored")

        block = ctx.enter_context(nc.Block())

        @block.sync
        def _(sp):
            sp.dma_start(h[:, :, :], x).then_inc(x_loaded, 16)
            sp.dma_start(par[:, :], params).then_inc(par_loaded, 16)
            for b in range(SLOTS):
                sp.dma_start(raw[:, b, :, :], stream[b].rearrange("p (k m) -> p k m", k=KB)).then_inc(w_loaded[b], 16)
            for l in range(DEPTH):
                mixer, ffn = first_block(l, "in") + SLOTS, first_block(l, "out") + SLOTS
                end_at = min(first_block(l + 1, "in") + SLOTS, DEPTH * BLOCKS_PER_LAYER)
                for first, last, free, count in ((mixer, ffn, block_used, mixer - SLOTS),
                                                 (ffn, end_at, lo_made, first_low(l, "out"))):
                    with sp.Fori(0, (last - first) // SLOTS) as it:
                        for b in range(SLOTS):
                            src = stream[bass.ds(it * SLOTS + (first + b), 1), :, :].rearrange("a p (k m) -> p (a k) m", k=KB)
                            sp.wait_ge(free, it * SLOTS + (count + b + 1))
                            sp.dma_start(raw[:, b, :, :], src).then_inc(w_loaded[b], 16)
            sp.wait_ge(h_made, CHUNKS * (2 * DEPTH + 1))
            sp.dma_start(out, h[:, :, :]).then_inc(stored, 16)
            sp.wait_ge(stored, 16)

        @block.gpsimd
        def _(pool):
            def low_part(l, n, loop=0):
                b = first_block(l, "in") + n
                slot = b % SLOTS
                pool.wait_ge(hi_made, loop + (first_split(l, "in") + n + 1))
                nc.gpsimd.tensor_tensor(w_low("in", slot), raw[:, slot, :, :], w_hi[:, slot, :, :].bitcast(F32),
                                        ALU.subtract).then_inc(in_lo_made, 1)

            nc.gpsimd.memset(ones[:, :], 1.0).then_inc(ones_made, 1)
            for l in range(DEPTH):
                for n in range(SLOTS):
                    low_part(l, n)
                if l:
                    pool.wait_ge(mean_made, 2 * l + 1)
                pool.dma_start(cst[:, :], consts).then_inc(mix_loaded, 16)
                pool.dma_start(wkv[:, :], w_kv[l]).then_inc(mix_loaded, 16)
                pool.dma_start(b_st[:, :, :, :], ssm_b[l]).then_inc(mix_loaded, 16)
                pool.dma_start(c_st[:, :, :, :], ssm_c[l]).then_inc(mix_loaded, 16)
                with pool.Fori(0, IN_BLOCKS - SLOTS, SLOTS) as it:
                    for n in range(SLOTS):
                        low_part(l, SLOTS + n, loop=it)

        @block.tensor
        def _(pe):
            def products(l, phase, rhs, ready, t0=0):
                groups, blocks, body = PHASES[phase]
                b0, g0 = first_block(l, phase), first_group(l, phase)
                s0 = first_low(l, phase)
                with pe.Fori(0, groups // body) as it:
                    for g in range(body):
                        pe.wait_ge(psum_free, it * body + g0 + g + 1)
                        for b in range(blocks):
                            n = g * blocks + b
                            slot = (b0 + n) % SLOTS
                            pe.wait_ge(lo_made, it * (body * blocks) + (s0 + n + 1))
                            split_block(phase, slot, b, 2 * (g % 2), blocks * KB, rhs, ready if g == 0 else None, t0)

            def split_block(phase, slot, b, bank, tiles, rhs, ready=None, t0=0):
                lo_w = w_low(phase, slot)
                for kk in range(KB):
                    k = b * KB + kk
                    if ready and k % 2 == 0:
                        pe.wait_ge(*ready(k))
                    hi, lo = (part[:, t0:NT] for part in rhs(k))
                    for j in range(2):
                        acc = ps[:, bank + j, t0:NT]
                        cols = slice(j * P, j * P + P)
                        pe.matmul(acc, lo_w[:, kk, cols], hi, start=k == 0, stop=False)
                        pe.matmul(acc, w_hi[:, slot, kk, cols], lo, start=False, stop=False)
                        mm = pe.matmul(acc, w_hi[:, slot, kk, cols], hi, start=False, stop=k == tiles - 1)
                mm.then_inc(block_used, 1)

            def x_parts(k):
                return x_hi[:, k, :], x_lo[:, k, :]

            def layer_norm_sums(n):
                tiles = [hsum[:, k, :] for k in range(2)] if n else [h[:, k, :] for k in range(DT)]
                if n:
                    pe.wait_ge(h_summed, 8 * (n + 1))
                for k, tile in enumerate(tiles):
                    mm = pe.matmul(ps[:, 4, 0:NT], ones[:, :], tile, start=k == 0, stop=k == len(tiles) - 1)
                mm.then_inc(mean_made, 1)
                pe.wait_ge(sq_summed, n + 1)
                for k in range(2):
                    mm = pe.matmul(ps[:, 5, 0:NT], ones[:, :], squares[:, k, :], start=k == 0, stop=k == 1)
                mm.then_inc(var_made, 1)

            def state_inputs(l, pr):
                for e in range(2):
                    t = 2 * pr + e
                    rows = slice(32 * (t % 4), 32 * (t % 4) + 32)
                    for c in range(2):
                        mm = pe.matmul(ps[:, 4 + 2 * e + c, 0:NT], b_st[rows, c, t // 4, :],
                                       proj[rows, U0 + t // 4, :], start=True, stop=True)
                mm.then_inc(bu_made, 1)

            def state_outputs(l, pr):
                m = pr // 2
                if pr % 2 == 0 and l * UT + m:
                    pe.wait_ge(y_read, l * UT + m)
                pe.wait_ge(s_made, l * PAIRS + pr + 1)
                for e in range(2):
                    t = 2 * pr + e
                    rows = slice(32 * (t % 4), 32 * (t % 4) + 32)
                    for c in range(2):
                        mm = pe.matmul(ps[rows, 2, 0:NT], c_st[:, c, t, :], states[:, pr % 2, e, c, :],
                                       start=c == 0, stop=c == 1)
                mm.then_inc(s_used, 1)

            def in_blocks(l, g, blocks):
                if blocks[0] == 0:
                    pe.wait_ge(psum_free, first_group(l, "in") + g + 2)
                for b in blocks:
                    pe.wait_ge(in_lo_made, first_low(l, "in") + 4 * g + b + 1)
                    split_block("in", (first_block(l, "in") + 4 * g + b) % SLOTS, b, 0, DT, x_parts,
                                (lambda k: (xlo_made, CHUNKS * 2 * l + k // 2 + 1)) if g == 0 else None)

            def side_products(l, step, half):
                ropes, kvs = ROPE_STEPS.get(step, ()), KV_STEPS.get(step, ())
                if half < len(ropes):
                    r = ropes[half]
                    if r == 8:
                        pe.wait_ge(ckv_sd, l + 1)
                    elif r == 13:
                        pe.wait_ge(kv_made, 8 * (l + 1))
                    if l * ROPES + r:
                        pe.wait_ge(roped, l * ROPES + r)
                    pe.matmul(ps[:, 3, 0:NT], const("perm"), rope_tile(r), start=True, stop=True).then_inc(rot_made, 1)
                if step == MS_STEP and half == 1:
                    pe.wait_ge(roped, l * ROPES + 8)
                    pe.wait_ge(ckv_sq, l + 1)
                    pe.matmul(ps[:, 3, 0:NT], ones[:, :], side[:, 1, :], start=True, stop=True).then_inc(ckv_ms, 1)
                if half < len(kvs):
                    t = kvs[half]
                    pe.wait_ge(roped, l * ROPES + 13)
                    pe.wait_ge(ckv_normed, l + 1)
                    if l * 8 + t:
                        pe.wait_ge(kv_made, l * 8 + t)
                    pe.matmul(ps[:, 3, 0:NT], wkv[:, t * P:(t + 1) * P], proj[:, PADT, :],
                              start=True, stop=True).then_inc(kv_mm, 1)

            def scores(l, n):
                kind, hd, q = n // (HEADS * NQ), n // NQ % HEADS, n % NQ
                qs, qn = QT[q]
                ke = qs + qn
                b = slice(64 * (hd % 2), 64 * (hd % 2) + 64)
                s = ps[0:qn, 4 + n % 2, 0:ke]
                if n >= 2:
                    pe.wait_ge(prob_made, l * 48 + n - 1)
                if kind == 0:
                    pe.matmul(s, proj[b, FQ0 + hd // 2, qs:ke], proj[b, FK0 + hd // 2, 0:ke], start=True, stop=False)
                    pe.matmul(s, cum[:, qs:ke], sel_r[:, hd:hd + 1].to_broadcast([P, ke]), start=False, stop=False)
                    pe.matmul(s, sel_r[:, HEADS + hd:HEADS + hd + 1].to_broadcast([P, qn]), cum[:, 0:ke],
                              start=False, stop=False)
                    mm = pe.matmul(s[:, qs:ke], ident_r[0:qn, 0:qn], causal_r[0:qn, 0:qn],
                                   start=False, stop=True)
                else:
                    pe.matmul(s, proj[b, DQ0 + hd // 2, qs:ke], kv[b, hd // 2, 0:ke], start=True, stop=False)
                    mm = pe.matmul(s, ident_r[0:qn, 0:qn], dsa_bias[0:qn, q, 0:ke], start=False, stop=True)
                mm.then_inc(score_made, 1)

            def prob_transposes(l, n):
                q = n % NQ
                qs, qn = QT[q]
                pe.wait_ge(prob_made, l * 48 + n + 1)
                if n >= 1:
                    pe.wait_ge(pt_made, l * 48 + n)
                for c in range(q + 1):
                    ks, kn = QT[c]
                    at = (q - c) * MASK_T
                    mm = pe.transpose(ps[0:kn, 6, at:at + qn], probs[0:qn, n % 2, ks:ks + kn], const("ident", qn, qn))
                mm.then_inc(ptr_made, 1)

            def weighted_values(l, n):
                kind, hd, q = n // (HEADS * NQ), n // NQ % HEADS, n % NQ
                qs, qn = QT[q]
                pe.wait_ge(pt_made, l * 48 + n + 1)
                if n >= 1:
                    pe.wait_ge(o_read, l * 48 + n)
                for c in range(q + 1):
                    ks, kn = QT[c]
                    mm = pe.matmul(ps[0:qn, 7, 0:HEAD], pt[0:kn, n % 2, q - c, 0:qn],
                                   v_tok[0:kn, kind, c, hd * HEAD:hd * HEAD + HEAD], start=c == 0, stop=c == q)
                mm.then_inc(o_made, 1)

            def transpose_values(l):
                for n in range(2 * NQ):
                    ks, kn = QT[n % NQ]
                    for t in range(4):
                        src = proj[:, FV0 + t, ks:ks + kn] if n < NQ else kv[:, 4 + t, ks:ks + kn]
                        mm = pe.transpose(ps[0:kn, V_BANKS[n], t * P:t * P + P], src, const("ident"))
                    mm.then_inc(vt_made, 1)

            def index_scores(l, n):
                j, q = n // NQ, n % NQ
                qs, qn = QT[q]
                b = slice(64 * (j % 2), 64 * (j % 2) + 64)
                if n >= 4:
                    pe.wait_ge(idx_relu, l * 48 + n - 3)
                pe.matmul(ps[0:qn, 4 + n % 4, 0:qs + qn], proj[b, IQ0 + j // 2, qs:qs + qn],
                          proj[b, IK, 0:qs + qn], start=True, stop=True).then_inc(idx_mm, 1)

            def gate_group(l, g):
                pe.wait_ge(psum_free, first_group(l, "glu") + g + 1)
                for b in range(2):
                    n = 2 * g + b
                    pe.wait_ge(w_loaded[n % SLOTS], ((first_block(l, "glu") + n) // SLOTS + 1) * 16)
                    for kk in range(KB):
                        for j in range(2):
                            k = b * KB + kk
                            mm = pe.matmul(ps[:, 2 * (g % 2) + j, 0:NT], raw[:, n % SLOTS, kk, j * P:j * P + P],
                                           yssm[:, k, :], start=k == 0, stop=k == 7)
                    mm.then_inc(block_used, 1)

            def output_transposes(l, kind, q):
                n = kind * NQ + q
                qs, qn = QT[q]
                pe.wait_ge(ynorm, 6 * l + n + 1)
                if n >= 2:
                    pe.wait_ge(yt_made, 6 * l + n - 1)
                for t in range(4):
                    mm = pe.transpose(ps[:, 1 + 3 * kind + n % 2, t * MASK_T:t * MASK_T + qn],
                                      y_tok[0:qn, kind, q, t * P:t * P + P], const("ident", qn, qn))
                mm.then_inc(yt_mm, 1)

            pe.wait_ge(ones_made, 1)
            pe.wait_ge(x_loaded, 16)
            layer_norm_sums(0)
            for l in range(DEPTH):
                ln = 2 * l + 1
                in_blocks(l, 0, range(4))
                pe.wait_ge(psum_free, first_group(l, "in") + 1 + 2)
                pe.wait_ge(mix_loaded, 64 * (l + 1))
                if l:
                    pe.wait_ge(bu_read, 32 * l)
                state_inputs(l, 0)
                for step in range(STEPS):
                    if step + 1 < PAIRS:
                        pe.wait_ge(bu_read, 2 * (l * PAIRS + step + 1))
                        state_inputs(l, step + 1)
                    pe.wait_ge(psum_free, first_group(l, "in") + step + 1 + 2)
                    side_products(l, step, 0)
                    if step + 1 < GROUPS_IN:
                        in_blocks(l, step + 1, (0, 1, 2))
                    side_products(l, step, 1)
                    if step + 1 < GROUPS_IN:
                        in_blocks(l, step + 1, (3,))
                    if step == 0:
                        pe.wait_ge(c_made, l + 1)
                    if step < PAIRS:
                        state_outputs(l, step)
                pe.wait_ge(bu_read, 32 * (l + 1))
                pe.wait_ge(roped, ROPES * (l + 1))
                for q, (qs, qn) in enumerate(QT):
                    mm = pe.transpose(ps[0:qn, 6, 32 * q:32 * q + 24], proj[0:24, FFIW, qs:qs + qn], const("ident", 24, 24))
                mm.then_inc(iwt_made, 1)
                transpose_values(l)
                pe.wait_ge(v_made, 6 * (l + 1))
                pe.wait_ge(iw_made, l + 1)
                pe.wait_ge(gelu_made, l + 1)
                for g in range(4):
                    for n in range(12 * g, 12 * g + 12):
                        index_scores(l, n)
                    gate_group(l, g)
                pe.wait_ge(idx_relu, 48 * (l + 1))
                pe.wait_ge(cum_made, l + 1)
                pe.wait_ge(psum_free, first_group(l, "glu") + 4 + 2)
                for n in range(UNITS + 2):
                    if n == UNITS // 2:
                        pe.wait_ge(bias_made, l + 1)
                    if n < UNITS:
                        scores(l, n)
                    if 1 <= n < UNITS + 1:
                        prob_transposes(l, n - 1)
                    if n >= 2:
                        weighted_values(l, n - 2)
                    if n == GATE_NORM:
                        pe.wait_ge(glu_summed, l + 1)
                        for j in range(2):
                            mm = pe.matmul(ps[:, 0, 0:NT], ones[:, :], gate_sq[:, 6 + j, :], start=j == 0, stop=j == 1)
                        mm.then_inc(glu_ms, 1)
                    if FOX_NORM + 8 <= n < FOX_NORM + 11:
                        output_transposes(l, 0, n - FOX_NORM - 8)
                for q in range(NQ):
                    output_transposes(l, 1, q)
                products(l, "out", lambda k: (y_hi[:, k, :], y_lo[k // UT][:, k % UT, :]), lambda k: (ylo_made, 4 * l + k // 4 + 1), LAST_T0[0] if l == DEPTH - 1 else 0)
                pe.wait_ge(psum_free, first_group(l, "out") + 8 + 2)
                layer_norm_sums(ln)
                products(l, "up", x_parts, lambda k: (xlo_made, CHUNKS * ln + k // 2 + 1), LAST_T0[0] if l == DEPTH - 1 else 0)
                products(l, "down", lambda k: (g_hi[:, k, :], g_lo[:, k, :]), lambda k: (g_made, FT * l + k + 2),
                         LAST_T0[1] if l == DEPTH - 1 else 0)
                pe.wait_ge(psum_free, first_group(l, "down") + 8 + 2)
                layer_norm_sums(ln + 1)

        @block.scalar
        def _(act):
            def cast(l, phase, n, loop=0):
                b = first_block(l, phase) + n
                slot = b % SLOTS
                act.wait_ge(w_loaded[slot], loop * (16 // SLOTS) + (b // SLOTS + 1) * 16)
                if b >= SLOTS:
                    act.wait_ge(block_used, loop + (b - SLOTS + 1))
                act.activation(w_hi[:, slot, :, :], raw[:, slot, :, :], ACT.Copy).then_inc(hi_made, 1)

            def layer_norm(n, gain, shift):
                for c in range(4):
                    act.wait_ge(centered, 4 * n + c + 1)
                    act.activation(squares[:, 4 * c:4 * c + 4, :], h[:, 4 * c:4 * c + 4, :], ACT.Square).then_inc(squared, 1)
                act.wait_ge(var_made, n + 1)
                act.activation(rstd[:, :], ps[:, 5, 0:NT], ACT.Sqrt, bias=LN_EPS, scale=1.0 / D_MODEL).then_inc(dev_made, 1)
                for c in range(CHUNKS):
                    act.wait_ge(scaled, CHUNKS * n + c + 1)
                    for k in range(2 * c, 2 * c + 2):
                        last = act.activation(h[:, k, :], h[:, k, :], ACT.Identity, bias=param(shift[0], shift[1] + k),
                                              scale=param(gain[0], gain[1] + k))
                    last.then_inc(h_made, 1)
                    if n < 2 * DEPTH:
                        act.wait_ge(h_made, CHUNKS * n + c + 1)
                        act.activation(x_hi[:, 2 * c:2 * c + 2, :], h[:, 2 * c:2 * c + 2, :], ACT.Copy).then_inc(xhi_made, 1)

            act.wait_ge(x_loaded, 16)
            for n in range(SLOTS):
                cast(0, "in", n)
            act.wait_ge(par_loaded, 16)
            layer_norm(0, ("ln_in_g", 0), ("ln_in_b", 0))
            for l in range(DEPTH):
                ln = 2 * l + 1
                act.activation(small[:, 0, :], param("log_dt", l * ST, ST), ACT.Exp).then_inc(dt_made, 1)
                cast(l, "in", 4)
                act.wait_ge(freq_made, l + 1)
                act.activation(small[:, 4, :], small[:, 1, :], ACT.Exp).then_inc(trig_made, 1)
                act.activation(small[:, 5, :], small[:, 3, :], ACT.Sin, scale=TWO_PI_LOW).then_inc(trig_made, 1)
                act.activation(small[:, 6, :], small[:, 7, :], ACT.Sin, bias=HALF_PI, scale=-TWO_PI_LOW).then_inc(trig_made, 1)

                def read_group(g):
                    act.wait_ge(block_used, first_block(l, "in") + 4 * (g + 1))
                    act.activation(proj[:, 2 * g:2 * g + 2, :], ps[:, 0:2, 0:NT], ACT.Copy).then_inc(psum_free, 1)

                def wave_table(pr):
                    r = l * PAIRS + pr
                    act.wait_ge(turns_made, r + 1)
                    if pr >= 2:
                        act.wait_ge(s_made, r - 1)
                    tb = table[:, pr % 2, :, :, :]
                    tr = turns[:, 0, :, :]
                    act.activation(turns[:, 1, :, :], tr, ACT.Abs).then_inc(abs_made, 1)
                    act.activation(tb[:, 1, :, :], tr, ACT.Sin, scale=TWO_PI_LOW)
                    act.activation(tb[:, 2, :, :], tr, ACT.Sin, scale=-TWO_PI_LOW)
                    act.activation(tb[:, 3, :, :], tr, ACT.Sin, scale=TWO_PI_LOW)
                    act.wait_ge(abs_made, r + 1)
                    act.activation(tb[:, 0, :, :], turns[:, 1, :, :], ACT.Sin, bias=HALF_PI, scale=-TWO_PI_LOW).then_inc(table_made, 1)

                cast(l, "in", 5)
                cast(l, "in", 6)
                wave_table(0)
                read_group(0)
                cast(l, "in", 7)
                wave_table(1)
                for step in range(STEPS):
                    if step + 2 < PAIRS:
                        wave_table(step + 2)
                    if step == MS_STEP:
                        act.wait_ge(ckv_ms, l + 1)
                        act.activation(rstd[:, :], ps[:, 3, 0:NT], ACT.Sqrt, bias=RMS_EPS, scale=1.0 / KV_RANK).then_inc(ckv_sd, 1)
                    if step == GATE_STEP:
                        act.wait_ge(f_neg, l + 1)
                        act.activation(fgate[:, 1, :], fgate[:, 1, :], ACT.Exp).then_inc(f_exp, 1)
                        act.wait_ge(f_exp, l + 1)
                        act.activation(fgate[:, 1, :], fgate[:, 1, :], ACT.Ln, bias=1.0).then_inc(f_ln, 1)
                    kvs = KV_STEPS.get(step, ())
                    for i in range(4):
                        if i % 3 == 0 and kvs:
                            t = kvs[i // 3]
                            act.wait_ge(kv_mm, l * 8 + t + 1)
                            act.activation(kv[:, t, :], ps[:, 3, 0:NT], ACT.Copy).then_inc(kv_made, 1)
                        if step + 1 < GROUPS_IN:
                            if i == 3:
                                read_group(step + 1)
                            if step + 2 < GROUPS_IN:
                                cast(l, "in", 4 * (step + 2) + i)
                for n in range(6):
                    kn = QT[n % NQ][1]
                    act.wait_ge(vt_made, 6 * l + n + 1)
                    act.activation(v_tok[0:kn, n // NQ, n % NQ, :], ps[0:kn, V_BANKS[n], :], ACT.Copy).then_inc(v_made, 1)
                act.wait_ge(y_read, UT * (l + 1))
                act.activation(yssm[:, :, :], yssm[:, :, :], ACT.Gelu_apprx_tanh).then_inc(gelu_made, 1)

                def gate_out(g):
                    if g < 4:
                        act.wait_ge(block_used, first_block(l, "glu") + 2 * (g + 1))
                        for j in range(2):
                            sg = act.activation(proj[:, 2 * g + j, :], ps[:, 2 * (g % 2) + j, 0:NT], ACT.Sigmoid,
                                                bias=param("glu_b", l * UT + 2 * g + j))
                        sg.then_inc(psum_free, 1)
                    if g:
                        act.wait_ge(glu_made, 4 * l + g)
                        act.activation(gate_sq[:, 2 * g - 2:2 * g, :], proj[:, 2 * g - 2:2 * g, :], ACT.Square).then_inc(glu_sq, 1)

                for g in range(4):
                    for n in range(12 * g, 12 * g + 12):
                        qs, qn = QT[n % NQ]
                        act.wait_ge(idx_mm, l * 48 + n + 1)
                        if n >= 4:
                            act.wait_ge(idx_used, l * 48 + n - 3)
                        act.activation(relu[0:qn, n % 4, 0:qs + qn], ps[0:qn, 4 + n % 4, 0:qs + qn], ACT.Relu,
                                       scale=SCALE).then_inc(idx_relu, 1)
                    gate_out(g)
                gate_out(4)

                def output_squares(kind, q):
                    n = 6 * l + NQ * kind + q
                    qn = QT[q][1]
                    act.wait_ge(o_read, l * UNITS + (kind + 1) * UNITS // 2)
                    if n:
                        act.wait_ge(ysq, n)
                    act.activation(relu[0:qn, 0:2, 0:256], y_tok[0:qn, kind, q, :].rearrange("p (a b) -> p a b", a=2), ACT.Square,
                                   accum_out=stat[0:qn, 3, NQ * kind + q:NQ * kind + q + 1]).then_inc(ysq, 1)

                def output_deviations(kind):
                    act.wait_ge(ysq, 6 * l + NQ * (kind + 1))
                    for q in range(NQ):
                        n = NQ * kind + q
                        qn = QT[q][1]
                        act.activation(stat[0:qn, 4, n:n + 1], stat[0:qn, 3, n:n + 1], ACT.Sqrt, bias=RMS_EPS,
                                       scale=1.0 / 512).then_inc(ysd, 1)

                def high_part(c):
                    if c < 2:
                        act.wait_ge(ymul, 2 * l + c + 1)
                    else:
                        act.wait_ge(yt_made, 6 * l + NQ * (c - 1))
                    src = proj[:, 4 * c:4 * c + 4, :] if c < 2 else yssm[:, 4 * c - 8:4 * c - 4, :]
                    act.activation(y_hi[:, 4 * c:4 * c + 4, :], src, ACT.Copy).then_inc(yhi_made, 1)

                for n in range(UNITS + 2):
                    if n < UNITS:
                        qs, qn = QT[n % NQ]
                        act.wait_ge(max_made, l * UNITS + n + 1)
                        if n >= 2:
                            act.wait_ge(ptr_made, l * UNITS + n - 1)
                        act.activation(probs[0:qn, n % 2, 0:qs + qn], ps[0:qn, 4 + n % 2, 0:qs + qn], ACT.Exp,
                                       bias=stat[0:qn, 0, n % 4:n % 4 + 1], scale=SCALE,
                                       accum_out=stat[0:qn, 1, n % 4:n % 4 + 1]).then_inc(prob_made, 1)
                    if n >= 2:
                        m = n - 2
                        kind, hd, q = m // (HEADS * NQ), m // NQ % HEADS, m % NQ
                        qn = QT[q][1]
                        act.wait_ge(den_made, l * UNITS + m + 1)
                        act.wait_ge(o_made, l * UNITS + m + 1)
                        act.activation(y_tok[0:qn, kind, q, hd * HEAD:(hd + 1) * HEAD], ps[0:qn, 7, 0:HEAD], ACT.Copy,
                                       scale=stat[0:qn, 2, m % 4:m % 4 + 1]).then_inc(o_read, 1)
                    if n == GATE_NORM + 2:
                        act.wait_ge(glu_ms, l + 1)
                        act.activation(rstd[:, :], ps[:, 0, 0:NT], ACT.Sqrt, bias=RMS_EPS, scale=1.0 / SSM_W).then_inc(glu_sd, 1)
                    if n in (GATE_NORM + 9, GATE_NORM + 13):
                        high_part((n - GATE_NORM - 9) // 4)
                    if FOX_NORM <= n < FOX_NORM + NQ:
                        output_squares(0, n - FOX_NORM)
                    if n == FOX_NORM + 4:
                        output_deviations(0)
                    if n == FOX_NORM + 13:
                        high_part(2)
                for q in range(NQ):
                    output_squares(1, q)
                output_deviations(1)
                for n in range(SLOTS):
                    cast(l, "out", n)
                high_part(3)
                for n in range(SLOTS, PHASES["out"][0] * PHASES["out"][1]):
                    cast(l, "out", n)
                for n in range(4):
                    cast(l, "up", n)
                layer_norm(ln, ("ln1_g", l * DT), ("ln1_b", l * DT))

                def convolve(g, odd, i=0):
                    n = FT * l + g
                    conv_at = PARAM["conv"][0] + n * 8
                    if isinstance(i, int):
                        src = par_t(conv_at + 8 * i)
                    else:
                        src = par[:, bass.ds(i * 8 + conv_at, 8)]
                    act.activation(cpar[:, odd, :], src, ACT.Copy).then_inc(cpar_made, 1)
                    act.wait_ge(cpar_made, i + n + 1)
                    act.wait_ge(block_used, i * 4 + (first_block(l, "up") + 4 * (g + 1)))
                    for j in range(2):
                        act.activation(conv[:, odd, j, :], ps[:, 2 * odd + j, 0:NT], ACT.Identity,
                                       bias=cpar[:, odd, j:j + 1], scale=cpar[:, odd, 2 + j:3 + j]).then_inc(conv_a, 1)
                    act.wait_ge(psum_free, i + (first_group(l, "up") + g + 3))
                    act.activation(gate[:, odd, :], conv[:, odd, 1, :], ACT.Silu).then_inc(gate_made, 1)

                def par_t(at):
                    return par[:, at:at + 8]

                with act.Fori(0, FT - 2, 2) as i:
                    for e in range(2):
                        for n in range(4):
                            cast(l, "up", 4 * (e + 1) + n, loop=i * 4)
                        convolve(e, e, i)
                for n in range(4):
                    cast(l, "up", 4 * (FT - 1) + n)
                convolve(FT - 2, 0)
                for n in range(4):
                    cast(l, "down", n)
                convolve(FT - 1, 1)
                for n in range(4, PHASES["down"][0] * PHASES["down"][1]):
                    cast(l, "down", n)
                if l + 1 < DEPTH:
                    for n in range(SLOTS):
                        cast(l + 1, "in", n)
                layer_norm(ln + 1, ("ln2_g", l * DT), ("ln2_b", l * DT))

        @block.vector
        def _(dve):
            steps = {"n": 0}

            def mark(ins):
                steps["n"] += 1
                ins.then_inc(dve_step, 1)
                return steps["n"]

            def after(n=None):
                dve.wait_ge(dve_step, steps["n"] if n is None else n)

            def spread(ap, n):
                return ap.unsqueeze(1).to_broadcast([ap.shape[0], n, ap.shape[1]])

            def low_part(l, phase, n, loop=0):
                b = first_block(l, phase) + n
                slot = b % SLOTS
                dve.wait_ge(hi_made, loop + (first_split(l, phase) + n + 1))
                dve.tensor_tensor(w_lo[:, slot, :, :], raw[:, slot, :, :], w_hi[:, slot, :, :].bitcast(F32),
                                  ALU.subtract).then_inc(lo_made, 1)

            def layer_norm(n):
                dve.wait_ge(mean_made, n + 1)
                for c in range(4):
                    h4 = h[:, 4 * c:4 * c + 4, :]
                    dve.scalar_tensor_tensor(out=h4, in0=spread(ps[:, 4, 0:NT], 4), scalar=-1.0 / D_MODEL, in1=h4,
                                             op0=ALU.mult, op1=ALU.add).then_inc(centered, 1)
                for c in range(1, 4):
                    dve.wait_ge(squared, 4 * n + c + 1)
                    if c > 1:
                        after()
                    mark(dve.tensor_tensor(squares[:, 0:4, :], squares[:, 0:4, :], squares[:, 4 * c:4 * c + 4, :], ALU.add))
                after()
                dve.tensor_tensor(squares[:, 0:2, :], squares[:, 0:2, :], squares[:, 2:4, :], ALU.add).then_inc(sq_summed, 1)
                dve.wait_ge(dev_made, n + 1)
                mark(dve.reciprocal(rstd[:, :], rstd[:, :]))
                after()

                def scale(c):
                    h2 = h[:, 2 * c:2 * c + 2, :]
                    dve.tensor_tensor(h2, h2, spread(rstd[:, :], 2), ALU.mult).then_inc(scaled, 1)

                for c in range(CHUNKS + 2):
                    if c < CHUNKS:
                        scale(c)
                    if c >= 2 and n < 2 * DEPTH:
                        dve.wait_ge(xhi_made, CHUNKS * n + c - 1)
                        t = slice(2 * c - 4, 2 * c - 2)
                        dve.tensor_tensor(x_lo[:, t, :], h[:, t, :], x_hi[:, t, :].bitcast(F32),
                                          ALU.subtract).then_inc(xlo_made, 1)

            def residual(l, phase, g):
                blocks = PHASES[phase][1]
                dve.wait_ge(block_used, first_block(l, phase) + blocks * (g + 1))
                h2 = h[:, 2 * g:2 * g + 2, :]
                dve.scalar_tensor_tensor(out=h2, in0=x_lo[:, 2 * g:2 * g + 2, :].bitcast(F32), scalar=ALPHA, in1=ps[:, 2 * (g % 2):2 * (g % 2) + 2, 0:NT],
                                         op0=ALU.mult, op1=ALU.add).then_inc(psum_free, 1)
                dve.wait_ge(psum_free, first_group(l, phase) + g + 3)
                mark(dve.scalar_tensor_tensor(out=h2, in0=x_hi[:, 2 * g:2 * g + 2, :].bitcast(F32), scalar=ALPHA, in1=h2,
                                              op0=ALU.mult, op1=ALU.add))
                after()
                n = 8 * (2 * l + 1 + (phase == "down")) + g
                dve.wait_ge(h_summed, n)
                if g == 0:
                    dve.tensor_copy(hsum[:, :, :], h2).then_inc(h_summed, 1)
                else:
                    dve.tensor_tensor(hsum[:, :, :], hsum[:, :, :], h2, ALU.add).then_inc(h_summed, 1)

            def turns_of(l, pr):
                r = l * 16 + pr
                if r >= 1:
                    dve.wait_ge(table_made, r)
                for e in range(2):
                    mark(dve.tensor_scalar(turns[:, 0, e, :], const("time"), small[:, 3, 2 * pr + e:2 * pr + e + 1],
                                           None, ALU.mult))
                after()
                mark(dve.tensor_scalar(turns[:, 1, :, :], turns[:, 0, :, :], ROUND, ROUND, ALU.add, ALU.subtract))
                after()
                dve.tensor_tensor(turns[:, 0, :, :], turns[:, 0, :, :], turns[:, 1, :, :], ALU.subtract).then_inc(turns_made, 1)

            def scan_pair(l, pr):
                r = l * 16 + pr
                t1, t2, w, z = (rot[:, c, :, :, :] for c in range(4))
                tb = table[:, pr % 2, :, :, :]
                if r:
                    dve.wait_ge(s_made, r)
                dve.wait_ge(bu_made, r + 1)
                dve.wait_ge(table_made, r + 1)
                for e in range(2):
                    bu = ps[:, 4 + 2 * e:6 + 2 * e, 0:NT]
                    dve.tensor_tensor(t1[:, e, :, :], bu, spread(tb[:, 0, e, :], 2), ALU.mult)
                    dve.tensor_tensor(t2[:, e, ::-1, :], bu, tb[:, 2:4, e, :], ALU.mult).then_inc(bu_read, 1)
                turned = []
                for e in range(2):
                    dve.wait_ge(bu_read, 2 * r + 1 + e)
                    turned.append(mark(dve.tensor_tensor(w[:, e, :, :], t1[:, e, :, :], t2[:, e, :, :], ALU.add)))
                summed = []
                for e in range(2):
                    after(turned[e])
                    decay = small[:, 4, 2 * pr + e:2 * pr + e + 1].to_broadcast([P, NT])
                    for c in range(2):
                        last = dve.tensor_tensor_scan(z[:, e, c, :], decay, w[:, e, c, :], 0.0, ALU.mult, ALU.add)
                    summed.append(mark(last))
                back = []
                for e in range(2):
                    after(summed[e])
                    dve.tensor_tensor(t1[:, e, :, :], z[:, e, :, :], spread(tb[:, 0, e, :], 2), ALU.mult)
                    back.append(mark(dve.tensor_tensor(t2[:, e, ::-1, :], z[:, e, :, :], tb[:, 1:3, e, :], ALU.mult)))
                if r >= 2:
                    dve.wait_ge(s_used, r - 1)
                for e in range(2):
                    after(back[e])
                    last = dve.tensor_tensor(states[:, pr % 2, e, :, :], t1[:, e, :, :], t2[:, e, :, :], ALU.add)
                last.then_inc(s_made, 1)

            def read_state_output(l, m):
                dve.wait_ge(s_used, l * 16 + 2 * m + 2)
                dve.scalar_tensor_tensor(out=yssm[:, m, :], in0=proj[:, U0 + m, :], scalar=param("d_skip", l * UT + m),
                                         in1=ps[:, 2, 0:NT], op0=ALU.mult, op1=ALU.add).then_inc(y_read, 1)

            dve.memset(hsum[:, :, :], 0.0).then_inc(h_summed, 8)
            dve.memset(rstd[:, :], 0.0).then_inc(psum_free, 2)
            dve.wait_ge(x_loaded, 16)
            dve.wait_ge(par_loaded, 16)
            layer_norm(0)
            for l in range(DEPTH):
                ln = 2 * l + 1
                sm = [small[:, c, :] for c in range(20)]
                lr, li = param("lam_re", l * ST, ST), param("lam_im", l * ST, ST)
                dve.wait_ge(dt_made, l + 1)
                mark(dve.tensor_tensor(sm[1], lr, sm[0], ALU.mult))
                mark(dve.tensor_tensor(sm[2], li, sm[0], ALU.mult))
                after()
                mark(dve.tensor_scalar(sm[8], sm[2], 1.0 / (2.0 * np.pi), None, ALU.mult))
                after()
                mark(dve.tensor_scalar(sm[9], sm[8], ROUND, ROUND, ALU.add, ALU.subtract))
                after()
                mark(dve.tensor_tensor(sm[3], sm[8], sm[9], ALU.subtract))
                after()
                mark(dve.scalar_tensor_tensor(out=sm[7], in0=sm[3], scalar=-1.0, in1=sm[3], op0=ALU.mult, op1=ALU.max))
                after()
                dve.tensor_tensor(sm[13], lr, lr, ALU.mult).then_inc(freq_made, 1)
                mark(dve.tensor_tensor(sm[14], li, li, ALU.mult))
                dve.wait_ge(mix_loaded, 64 * (l + 1))
                turns_of(l, 0)
                dve.wait_ge(trig_made, 3 * (l + 1))
                dve.wait_ge(freq_made, l + 1)
                mark(dve.tensor_tensor(sm[10], sm[4], sm[6], ALU.mult))
                mark(dve.tensor_tensor(sm[11], sm[4], sm[5], ALU.mult))
                mark(dve.tensor_tensor(sm[13], sm[13], sm[14], ALU.add))
                after()
                mark(dve.tensor_scalar(sm[10], sm[10], 1.0, None, ALU.subtract))
                mark(dve.reciprocal(sm[13], sm[13]))
                after()
                mark(dve.tensor_tensor(sm[15], sm[10], lr, ALU.mult))
                mark(dve.tensor_tensor(sm[16], sm[11], li, ALU.mult))
                mark(dve.tensor_tensor(sm[17], sm[11], lr, ALU.mult))
                mark(dve.tensor_tensor(sm[18], sm[10], li, ALU.mult))
                after()
                mark(dve.tensor_tensor(sm[15], sm[15], sm[16], ALU.add))
                mark(dve.tensor_tensor(sm[17], sm[17], sm[18], ALU.subtract))
                after()
                mark(dve.tensor_tensor(sm[15], sm[15], sm[13], ALU.mult))
                mark(dve.tensor_tensor(sm[17], sm[17], sm[13], ALU.mult))
                after()
                tmp = [rot[:, c, :, :, :].rearrange("p a b t -> p (a b t)")[:, 0:ST * 32].rearrange("p (s c) -> p s c", c=32)
                       for c in range(4)]
                zr, zi = (sm[c].unsqueeze(2).to_broadcast([P, ST, 32]) for c in (15, 17))
                c_re, c_im = c_st[:, 0, :, :], c_st[:, 1, :, :]
                mark(dve.tensor_tensor(tmp[0], c_re, zr, ALU.mult))
                mark(dve.tensor_tensor(tmp[1], c_im, zi, ALU.mult))
                mark(dve.tensor_tensor(tmp[2], c_re, zi, ALU.mult))
                mark(dve.tensor_tensor(tmp[3], c_im, zr, ALU.mult))
                after()
                mark(dve.tensor_tensor(c_re, tmp[0], tmp[1], ALU.subtract))
                dve.scalar_tensor_tensor(out=c_im, in0=tmp[2], scalar=-1.0, in1=tmp[3], op0=ALU.mult,
                                         op1=ALU.subtract).then_inc(c_made, 1)
                fx, fe = fgate[:, 0, :], fgate[:, 1, :]

                def rope(r):
                    dve.wait_ge(rot_made, l * ROPES + r + 1)
                    mark(dve.tensor_tensor(side[:, 0, :], ps[:, 3, 0:NT], const("rope_s"), ALU.mult))
                    mark(dve.tensor_tensor(rope_tile(r), rope_tile(r), const("rope_c"), ALU.mult))
                    after()
                    dve.tensor_tensor(rope_tile(r), rope_tile(r), side[:, 0, :], ALU.add).then_inc(roped, 1)

                def side_work(step, half):
                    ropes = ROPE_STEPS.get(step, ())
                    if half < len(ropes):
                        if ropes[half]:
                            dve.wait_ge(roped, l * ROPES + ropes[half])
                        rope(ropes[half])
                    if step == MS_STEP and half == 0:
                        dve.wait_ge(psum_free, first_group(l, "in") + CKV // 2 + 1 + 2)
                        dve.tensor_tensor(side[:, 1, :], proj[:, CKV, :], proj[:, CKV, :], ALU.mult).then_inc(ckv_sq, 1)
                    if step == MS_STEP + 1 and half == 1:
                        dve.wait_ge(ckv_sd, l + 1)
                        mark(dve.reciprocal(rstd[:, :], rstd[:, :]))
                        after()
                        dve.scalar_tensor_tensor(out=proj[:, PADT, :], in0=proj[:, CKV, :], scalar=param("kv_g", l), in1=rstd[:, :],
                                                 op0=ALU.mult, op1=ALU.mult).then_inc(ckv_normed, 1)
                    if step == GATE_STEP and half == 0:
                        mark(dve.tensor_scalar(cum[:, :], const("time"), 0.0, None, ALU.mult))
                        mark(dve.tensor_copy(ident_r[:, :], const("ident", cols=MASK_T)))
                        mark(dve.tensor_copy(causal_r[:, :], const("causal")))
                        mark(dve.tensor_copy(sel_r[:, :], const("sel")))
                        mark(dve.tensor_scalar(fx, proj[0:8, FFIW, :], param("f_bias", l, rows=8), None, ALU.add))
                        after()
                        dve.scalar_tensor_tensor(out=fe, in0=fx, scalar=-1.0, in1=fx, op0=ALU.mult, op1=ALU.min).then_inc(f_neg, 1)
                    if step == GATE_STEP and half == 1:
                        dve.wait_ge(f_ln, l + 1)
                        mark(dve.scalar_tensor_tensor(out=fx, in0=fx, scalar=0.0, in1=fe, op0=ALU.min, op1=ALU.subtract))
                        after()
                        mark(dve.tensor_tensor_scan(fe, ones[0:8, 0:1].to_broadcast([8, NT]), fx, 0.0, ALU.mult, ALU.add))
                        after()
                        mark(dve.tensor_copy(cum[0:8, :], fe))
                        after()
                        dve.tensor_tensor(cum[32:40, :], fe, cum[0:8, :].bitcast(F32), ALU.subtract).then_inc(cum_made, 1)

                turns_of(l, 1)
                scan_pair(l, 0)
                for step in range(STEPS):
                    side_work(step, 0)
                    if step >= 2 and step % 2 == 0 and step <= PAIRS:
                        read_state_output(l, step // 2 - 1)
                    if step + 2 < PAIRS:
                        turns_of(l, step + 2)
                    if step + 1 < PAIRS:
                        scan_pair(l, step + 1)
                    side_work(step, 1)
                dve.wait_ge(iwt_made, l + 1)
                for q, (qs, qn) in enumerate(QT):
                    last = dve.tensor_scalar(iw_tok[0:qn, q, 0:24], ps[0:qn, 6, 32 * q:32 * q + 24], IDX_HEADS ** -0.5, None,
                                             ALU.mult)
                last.then_inc(iw_made, 1)
                dve.wait_ge(iw_made, l + 1)
                def gate_apply(g):
                    dve.wait_ge(psum_free, first_group(l, "glu") + g + 3)
                    y2 = proj[:, 2 * g:2 * g + 2, :]
                    dve.tensor_tensor(y2, y2, yssm[:, 2 * g:2 * g + 2, :], ALU.mult).then_inc(glu_made, 1)

                for n in range(IDX_HEADS * NQ):
                    j, q = n // NQ, n % NQ
                    qs, qn = QT[q]
                    acc = work[0:qn, 0, q, 0:qs + qn]
                    src, wt = relu[0:qn, n % 4, 0:qs + qn], iw_tok[0:qn, q, 8 + j:9 + j]
                    dve.wait_ge(idx_relu, l * 48 + n + 1)
                    if j == 0:
                        dve.tensor_scalar(acc, src, wt, None, ALU.mult).then_inc(idx_used, 1)
                    else:
                        dve.wait_ge(idx_used, l * 48 + n - 2)
                        dve.scalar_tensor_tensor(out=acc, in0=src, scalar=wt, in1=acc, op0=ALU.mult,
                                                 op1=ALU.add).then_inc(idx_used, 1)
                    if n % 12 == 11:
                        gate_apply(n // 12)
                dve.wait_ge(idx_used, 48 * (l + 1))
                marks = []
                for q, (qs, qn) in enumerate(QT):
                    d = work[0:qn, 0, q, qs:qs + qn]
                    marks.append(mark(dve.tensor_tensor(d, d, const("causal", qn, qn), ALU.add)))
                dve.wait_ge(glu_sq, 4 * (l + 1))
                mark(dve.tensor_tensor(gate_sq[:, 4:8, :], gate_sq[:, 4:8, :], gate_sq[:, 0:4, :], ALU.add))
                after()
                dve.tensor_tensor(gate_sq[:, 6:8, :], gate_sq[:, 6:8, :], gate_sq[:, 4:6, :], ALU.add).then_inc(glu_summed, 1)

                def top_scores(rnd):
                    for q, (qs, qn) in enumerate(QT):
                        after(marks[q])
                        marks[q] = mark(dve.max(top8[0:qn, q, :], work[0:qn, rnd % 2, q, 0:qs + qn]))
                    for q, (qs, qn) in enumerate(QT):
                        after(marks[q])
                        marks[q] = mark(dve.match_replace(work[0:qn, 1 - rnd % 2, q, 0:qs + qn], top8[0:qn, q, :],
                                                          work[0:qn, rnd % 2, q, 0:qs + qn], TAKEN))

                def sparse_bias():
                    for q, (qs, qn) in enumerate(QT):
                        after(marks[q])
                        marks[q] = mark(dve.tensor_scalar(work[0:qn, 1, q, 0:qs + qn], work[0:qn, 0, q, 0:qs + qn], TAKEN, 1.0,
                                                          ALU.is_equal, ALU.subtract))
                    for q, (qs, qn) in enumerate(QT):
                        after(marks[q])
                        if q:
                            dve.tensor_scalar(dsa_bias[0:qn, q, 0:qs], work[0:qn, 1, q, 0:qs], -NEG, None, ALU.mult)
                        last = dve.scalar_tensor_tensor(out=dsa_bias[0:qn, q, qs:qs + qn], in0=work[0:qn, 1, q, qs:qs + qn],
                                                        scalar=-NEG, in1=const("causal", qn, qn), op0=ALU.mult, op1=ALU.add)
                    last.then_inc(bias_made, 1)

                def output_scale(kind, q):
                    n = kind * NQ + q
                    qn = QT[q][1]
                    dve.wait_ge(ysd, 6 * l + n + 1)
                    mark(dve.reciprocal(stat[0:qn, 4, n:n + 1], stat[0:qn, 4, n:n + 1]))
                    after()
                    y = y_tok[0:qn, kind, q, :]
                    dve.tensor_scalar(y, y, stat[0:qn, 4, n:n + 1], None, ALU.mult).then_inc(ynorm, 1)

                def output_read(kind, q):
                    n = kind * NQ + q
                    qs, qn = QT[q]
                    dve.wait_ge(yt_mm, 6 * l + n + 1)
                    for t in range(4):
                        last = dve.tensor_scalar(yssm[:, 4 * kind + t, qs:qs + qn], ps[:, 1 + 3 * kind + n % 2, t * MASK_T:t * MASK_T + qn],
                                                 param("mix_g", l * DT + UT + 4 * kind + t), None, ALU.mult)
                        if t == 3:
                            last.then_inc(yt_made, 1)

                def low_y(c):
                    dve.wait_ge(yhi_made, 4 * l + c + 1)
                    src = proj[:, 4 * c:4 * c + 4, :] if c < 2 else yssm[:, 4 * c - 8:4 * c - 4, :]
                    dve.tensor_tensor(y_lo[c // 2][:, 4 * (c % 2):4 * (c % 2) + 4, :], src, y_hi[:, 4 * c:4 * c + 4, :].bitcast(F32),
                                      ALU.subtract).then_inc(ylo_made, 1)

                for n in range(UNITS + 1):
                    if n < UNITS:
                        qs, qn = QT[n % NQ]
                        dve.wait_ge(score_made, l * UNITS + n + 1)
                        mark(dve.reduce_max(stat[0:qn, 0, 4 + n % 4:5 + n % 4], ps[0:qn, 4 + n % 2, 0:qs + qn], AX_X))
                        after()
                        dve.tensor_scalar(stat[0:qn, 0, n % 4:n % 4 + 1], stat[0:qn, 0, 4 + n % 4:5 + n % 4], -SCALE, None,
                                          ALU.mult).then_inc(max_made, 1)
                    if n:
                        m = n - 1
                        q = m % NQ
                        qn = QT[q][1]
                        dve.wait_ge(ptr_made, l * UNITS + m + 1)
                        if m >= 2:
                            dve.wait_ge(o_made, l * UNITS + m - 1)
                        dve.tensor_copy(pt[0:MASK_T, m % 2, 0:q + 1, 0:qn],
                                        ps[0:MASK_T, 6, 0:NQ * MASK_T].rearrange("p (c t) -> p c t", c=NQ)[:, 0:q + 1, 0:qn]
                                        ).then_inc(pt_made, 1)
                        dve.reciprocal(stat[0:qn, 2, m % 4:m % 4 + 1], stat[0:qn, 1, m % 4:m % 4 + 1]).then_inc(den_made, 1)
                    if n % 3 == 0 and n // 3 < TOPK // 8:
                        top_scores(n // 3)
                    if n == 3 * (TOPK // 8) - 2:
                        sparse_bias()
                    if n == GATE_NORM + 3:
                        dve.wait_ge(glu_sd, l + 1)
                        mark(dve.reciprocal(rstd[:, :], rstd[:, :]))
                        after()
                    if GATE_NORM + 4 <= n < GATE_NORM + 12:
                        k = n - GATE_NORM - 4
                        last = dve.scalar_tensor_tensor(out=proj[:, k, :], in0=proj[:, k, :], scalar=param("mix_g", l * DT + k),
                                                        in1=rstd[:, :], op0=ALU.mult, op1=ALU.mult)
                        if k % 4 == 3:
                            last.then_inc(ymul, 1)
                    if n in (GATE_NORM + 13, GATE_NORM + 17):
                        low_y((n - GATE_NORM - 13) // 4)
                    if FOX_NORM + 6 <= n < FOX_NORM + 9:
                        output_scale(0, n - FOX_NORM - 6)
                    if FOX_NORM + 9 <= n < FOX_NORM + 12:
                        output_read(0, n - FOX_NORM - 9)
                    if n == FOX_NORM + 15:
                        low_y(2)
                for q in range(NQ):
                    output_scale(1, q)
                dve.wait_ge(ynorm, 6 * (l + 1))
                for n in range(SLOTS - 1):
                    low_part(l, "out", n)
                for q in range(NQ):
                    output_read(1, q)
                low_y(3)
                low_part(l, "out", SLOTS - 1)
                for g in range(8):
                    for n in range(4):
                        if g:
                            low_part(l, "out", 4 * g + n)
                    if g:
                        residual(l, "out", g - 1)
                for n in range(4):
                    low_part(l, "up", n)
                residual(l, "out", 7)
                layer_norm(ln)

                def convolve(g, odd, i=0):
                    n = FT * l + g
                    cv = conv[:, odd, :, :]
                    dve.wait_ge(conv_a, i * 2 + 2 * n + 2)
                    for tap in (1, 2):
                        if tap == 2:
                            dve.wait_ge(conv1_made, i * 2 + 2 * n + 2)
                        for j in range(2):
                            last = dve.scalar_tensor_tensor(
                                out=cv[:, j, tap:NT], in0=ps[:, 2 * odd + j, 0:NT - tap],
                                scalar=cpar[:, odd, 2 + 2 * tap + j:3 + 2 * tap + j], in1=cv[:, j, tap:NT],
                                op0=ALU.mult, op1=ALU.add)
                            if tap == 1:
                                last.then_inc(conv1_made, 1)
                    last.then_inc(psum_free, 1)
                    dve.wait_ge(gate_made, i + n + 1)
                    hi = g_hi[:, g:g + 1, :] if isinstance(i, int) else g_hi[:, bass.ds(i + g, 1), :]
                    lo = g_lo[:, g:g + 1, :] if isinstance(i, int) else g_lo[:, bass.ds(i + g, 1), :]
                    pr_ = prod[:, odd:odd + 1, :]
                    dve.tensor_tensor(pr_, gate[:, odd:odd + 1, :], cv[:, 0:1, :], ALU.mult).then_inc(prod_made, 1)
                    dve.tensor_tensor(hi, gate[:, odd:odd + 1, :], cv[:, 0:1, :], ALU.mult).then_inc(ghi_made, 1)
                    dve.wait_ge(prod_made, i + n + 1)
                    dve.wait_ge(ghi_made, i + n + 1)
                    dve.tensor_tensor(lo, pr_, hi.bitcast(F32), ALU.subtract).then_inc(g_made, 1)

                with dve.Fori(0, FT - 2, 2) as i:
                    for e in range(2):
                        for n in range(4):
                            low_part(l, "up", 4 * (e + 1) + n, loop=i * 4)
                        convolve(e, e, i)
                for n in range(4):
                    low_part(l, "up", 4 * (FT - 1) + n)
                convolve(FT - 2, 0)
                for n in range(4):
                    low_part(l, "down", n)
                convolve(FT - 1, 1)
                blocks = PHASES["down"][1]
                for g in range(8):
                    for n in range(4, blocks + 4):
                        if g * blocks + n < 8 * blocks:
                            low_part(l, "down", g * blocks + n)
                    residual(l, "down", g)
                layer_norm(ln + 1)


def feature_major(a):
    t, f = a.shape
    return a.T.reshape(f // P, P, t).transpose(1, 0, 2)


def blocks_of(w):
    k, m = w.shape
    return w.reshape(k // (KB * P), KB, P, m // (2 * P), 2 * P).transpose(3, 0, 2, 1, 4).reshape(-1, P, KB * 2 * P)


def constants():
    c = np.zeros((P, CONST_COLS), np.float32)

    def put(name, a):
        at, n = CONST[name]
        c[:a.shape[0], at:at + n] = a

    put("ident", np.eye(P))
    put("ones", np.ones((P, P)))
    rot = HEAD // 4
    perm = np.zeros((P, P))
    freq = np.float32(500000.0) ** (-np.arange(0, rot, 2, dtype=np.float32) / np.float32(rot))
    ang = np.arange(NT, dtype=np.float32)[None, :] * freq[:, None]
    cos, sin = np.ones((P, NT)), np.zeros((P, NT))
    for m in range(P):
        d = m % HEAD
        if d < rot:
            perm[m + rot // 2 if d < rot // 2 else m - rot // 2, m] = 1.0
            cos[m] = np.cos(ang[d % (rot // 2)])
            sin[m] = np.sin(ang[d % (rot // 2)]) * (-1 if d < rot // 2 else 1)
    put("perm", perm)
    put("rope_c", cos)
    put("rope_s", sin)
    put("time", np.tile(np.arange(NT) - NT // 2, (P, 1)))
    put("causal", np.where(np.arange(MASK_T)[None, :] <= np.arange(MASK_T)[:, None], 0.0, NEG))
    sel = np.zeros((40, 2 * HEADS))
    for part in (slice(0, HEADS), slice(32, 32 + HEADS)):
        sel[part] = np.concatenate([np.eye(HEADS), -np.eye(HEADS)], 1) / SCALE
    put("sel", sel)
    return c


def lay_out(i):
    z = np.zeros
    x = feature_major(np.concatenate([i["meta_tokens"], i["x"][0]], 0))
    stream = []
    for l in range(DEPTH):
        w = i["w_in"][l]
        at = np.cumsum([0, 1024, 512, 512, 512, 8, 512, 128, 1024, 64, 16])
        u, fq, fk, fv, ff, dq, ckv, iq, ik, iw = (w[:, at[n]:at[n + 1]] for n in range(10))
        pad = z((D_MODEL, P - 24), np.float32)
        stream.append(blocks_of(np.concatenate([u, iq, ckv, ff, iw, pad, ik, ik, z((D_MODEL, P), np.float32),
                                                dq, fk, fv, fq], 1)))
        stream.append(blocks_of(i["ssm_glu_w"][l]))
        stream.append(blocks_of(i["w_out"][l]))
        stream.append(blocks_of(i["w_up"][l].reshape(D_MODEL, 2, FT, P).transpose(0, 2, 1, 3).reshape(D_MODEL, -1)))
        stream.append(blocks_of(i["w_down"][l]))
    params = z((P, PARAM_COLS), np.float32)

    def put(name, a):
        o, n = PARAM[name]
        params[:a.shape[0], o:o + n] = a

    def tiles(a):
        return a.reshape(-1, P).T

    for name, key in (("ln_in_g", "ln_in_g"), ("ln_in_b", "ln_in_b"), ("ln1_g", "ln1_g"), ("ln1_b", "ln1_b"),
                      ("ln2_g", "ln2_g"), ("ln2_b", "ln2_b"), ("mix_g", "mix_norm_g"), ("glu_b", "ssm_glu_b"),
                      ("d_skip", "ssm_d"), ("kv_g", "kv_norm_g")):
        put(name, tiles(i[key]))
    put("f_bias", i["fox_f_bias"].T)
    taps = np.concatenate([i["conv_b"][:, None], i["conv_w"][:, ::-1]], 1)
    put("conv", taps.reshape(DEPTH, 4, 2, FT, P).transpose(4, 0, 3, 1, 2).reshape(P, -1))
    for name in ("lam_re", "lam_im"):
        put(name, i["ssm_" + name].reshape(DEPTH, ST, 2, STATE).transpose(2, 3, 0, 1).reshape(P, -1))
    put("log_dt", np.broadcast_to(i["ssm_log_dt"].reshape(DEPTH, ST, 2, 1), (DEPTH, ST, 2, STATE)
                                  ).transpose(2, 3, 0, 1).reshape(P, -1))
    b = z((DEPTH, 4, 2, GROUP, 2, UT, 2, STATE), np.float32)
    c = z((DEPTH, 2, STATE, 2, ST, 2, GROUP), np.float32)
    for part, (bk, ck) in enumerate((("ssm_b_re", "ssm_c_re"), ("ssm_b_im", "ssm_c_im"))):
        bb = i[bk].reshape(DEPTH, UT, 4, 2, STATE, GROUP)
        cc = i[ck].reshape(DEPTH, ST, 2, GROUP, STATE)
        for half in range(2):
            b[:, :, half, :, part, :, half, :] = bb[:, :, :, half].transpose(0, 2, 4, 1, 3)
            c[:, half, :, part, :, half, :] = cc[:, :, half].transpose(0, 3, 1, 2)
    return {"x": np.ascontiguousarray(x), "stream": np.concatenate(stream, 0), "consts": constants(), "params": params,
            "ssm_b": b.reshape(DEPTH, P, 2, UT, P), "ssm_c": c.reshape(DEPTH, P, 2, ST, 32),
            "w_kv": np.ascontiguousarray(i["w_kv_up"])}


def kernel(**inputs):
    import concourse.bacc as bacc
    from concourse.bass_utils import run_bass_kernel_spmd

    arrays = lay_out({n: np.asarray(a) for n, a in inputs.items()})
    nc = bacc.Bacc("TRN2", target_bir_lowering=False, num_devices=1)
    aps = {n: nc.dram_tensor(n, a.shape, F32, kind="ExternalInput").ap() for n, a in arrays.items()}
    out = nc.dram_tensor("out", (P, DT, NT), F32, kind="ExternalOutput").ap()
    hybrid_trunk(nc, **aps, out=out)
    r = run_bass_kernel_spmd(nc, [arrays], core_ids=[0])
    tokens = np.asarray(r.results[0]["out"]).transpose(2, 1, 0).reshape(NT, D_MODEL)
    return tokens[N_META:][None]
```

```python
from contextlib import ExitStack

import concourse.bass as bass
import numpy as np
from concourse import mybir

F32 = mybir.dt.float32
F32R = mybir.dt.float32r
ALU = mybir.AluOpType
ACT = mybir.ActivationFunctionType
AX_X = mybir.AxisListType.X

P = 128
D_MODEL, SEQ, N_META, DEPTH = 2048, 256, 16, 2
NT = SEQ + N_META
HEAD = 64
SSM_W, GROUP, STATE = D_MODEL // 2, 16, 64
HEADS = 8
KV_RANK = 128
IDX_HEADS = 16
TOPK = min(256, SEQ // 4)
D_FF = 11 * D_MODEL // 4
ALPHA = (2.0 * DEPTH) ** 0.25
LN_EPS, RMS_EPS = 1e-5, 1e-6
NEG = -1e30
HALF_PI = 1.5707963
TAKEN = -3e38
SCALE = HEAD ** -0.5
TWO_PI_LOW = 6.283185
ROUND = 12582912.0

DT = D_MODEL // P
FT = D_FF // P
UT = SSM_W // P
ST = SSM_W // GROUP * STATE // P
MASK_T = 96
QT = [(s, min(MASK_T, NT - s)) for s in range(0, NT, MASK_T)]
NQ = len(QT)

KB = 4
SLOTS = 4
PHASES = {"in": (18, DT // KB, 1), "glu": (4, UT // KB, 4), "out": (8, DT // KB, 4),
          "up": (FT, DT // KB, 2), "down": (8, FT // KB, 4)}
SPLIT = ("in", "out", "up", "down")
BLOCKS_PER_LAYER = sum(g * b for g, b, _ in PHASES.values())
GROUPS_PER_LAYER = sum(g for g, _, _ in PHASES.values())
SPLIT_PER_LAYER = sum(PHASES[p][0] * PHASES[p][1] for p in SPLIT)


def first_block(layer, phase):
    names = list(PHASES)
    return layer * BLOCKS_PER_LAYER + sum(PHASES[n][0] * PHASES[n][1] for n in names[:names.index(phase)])


def first_group(layer, phase):
    names = list(PHASES)
    return layer * GROUPS_PER_LAYER + sum(PHASES[n][0] for n in names[:names.index(phase)])


def first_split(layer, phase):
    return layer * SPLIT_PER_LAYER + sum(PHASES[n][0] * PHASES[n][1] for n in SPLIT[:SPLIT.index(phase)])


def first_low(layer, phase):
    mine = ("in",) if phase == "in" else ("out", "up", "down")
    size = {p: PHASES[p][0] * PHASES[p][1] for p in mine}
    return layer * sum(size.values()) + sum(size[p] for p in mine[:mine.index(phase)])


U0, IQ0, CKV, FFIW, IK, PADT, DQ0, FK0, FV0, FQ0 = 0, 8, 16, 17, 18, 19, 20, 24, 28, 32

PAIRS = ST // 2
GROUPS_IN = PHASES["in"][0]
STEPS = GROUPS_IN
ROPE_STEPS = {4: (0, 1), 5: (2, 3), 6: (4, 5), 7: (6, 7), 9: (8,), 10: (9, 10), 11: (11, 12), 16: (13, 14), 17: (15, 16)}
ROPES = 17
MS_STEP = 8
KV_STEPS = {12: (0, 1), 13: (2, 3), 14: (4, 5), 15: (6, 7)}
GATE_STEP = 10
IN_BLOCKS = PHASES["in"][0] * PHASES["in"][1]
CHUNKS = DT // 2
PIVOT = 3 * DT // 4
LAST_T0 = (N_META - 2, N_META)

UNITS = 2 * HEADS * NQ
S_BANKS = (4, 5, 3)
V_BANKS = (4, 5, 7, 0, 1, 3)
Y_BANKS = (1, 2, 1, 4, 5, 6)
GATE_NORM = 3
FOX_NORM = UNITS // 2 + 3

CONST = {}
_at = 0
for _name, _cols in (("ident", P), ("perm", P), ("rope_c", NT), ("rope_s", NT), ("time", NT),
                     ("causal", MASK_T), ("sel", 2 * HEADS)):
    CONST[_name] = (_at, _cols)
    _at += _cols
CONST_COLS = _at

PARAM = {}
_at = 0
for _name, _cols in (("ln_in_g", DT), ("ln_in_b", DT), ("ln1_g", DEPTH * DT), ("ln1_b", DEPTH * DT),
                     ("ln2_g", DEPTH * DT), ("ln2_b", DEPTH * DT), ("mix_g", DEPTH * DT),
                     ("conv", DEPTH * FT * 8), ("glu_b", DEPTH * UT),
                     ("d_skip", DEPTH * UT), ("kv_g", DEPTH), ("f_bias", DEPTH),
                     ("lam_re", DEPTH * ST), ("lam_im", DEPTH * ST), ("log_dt", DEPTH * ST)):
    PARAM[_name] = (_at, _cols)
    _at += _cols
PARAM_COLS = _at


def hybrid_trunk(nc, x, stream, consts, params, ssm_b, ssm_c, w_kv, out):
    with ExitStack() as ctx:
        def sem(name):
            return ctx.enter_context(nc.semaphore(name))

        base = (nc.sbuf_base + 63) // 64 * 64
        cursor = {"at": base}

        def place(name, shape, dt=F32, at=None):
            size = 4 * int(np.prod(shape[1:]))
            where = cursor["at"] if at is None else at
            t = nc.alloc_sbuf_tensor_at(name, shape, dt, offset=where)
            if at is None:
                cursor["at"] += (size + 31) // 32 * 32
            return t, where + (size + 31) // 32 * 32

        h, _ = place("h", [P, DT, NT])
        x_lo, _ = place("x_lo", [P, DT, NT], F32R, at=base)
        raw_at = cursor["at"]
        raw, _ = place("raw", [P, SLOTS, KB, 2 * P])
        in_lo, _ = place("in_lo", [P, SLOTS, KB, 2 * P], F32R, at=raw_at)
        w_hi, _ = place("w_hi", [P, SLOTS, KB, 2 * P], F32R)
        par, _ = place("par", [P, PARAM_COLS])
        ones, _ = place("ones_p", [P, P])
        rstd, _ = place("rstd", [P, NT])
        x_hi, high = place("x_hi", [P, DT, NT], F32R)
        g_hi, e = place("g_hi", [P, FT, NT], F32R, at=high)
        g_lo, ffn_end = place("g_lo", [P, FT, NT], F32R, at=e)
        conv, e = place("conv", [P, 2, 2, NT], at=ffn_end)
        gate, e = place("gate", [P, 2, NT], at=e)
        prod, e = place("prod", [P, 2, NT], at=e)
        cpar, e = place("cpar", [P, 2, 8], at=e)
        w_lo, e = place("w_lo", [P, SLOTS, KB, 2 * P], F32R, at=e)
        w_lo_end = e
        hsum, _ = place("hsum", [P, 2, NT], at=ffn_end)
        assert e <= nc.sbuf_usable_end, (e, nc.sbuf_usable_end)
        end = nc.sbuf_usable_end
        sq_first, _ = place("sq_first", [P, DT, NT], at=high)
        sq_down, e = place("sq_down", [P, DT, NT], at=w_lo_end)
        assert e <= end, (e, end)
        proj, e = place("proj", [P, 36, NT], at=high)
        kv, e = place("kv", [P, 8, NT], at=e)
        y_lo = [place("gated_lo", [P, UT, NT], F32R, at=high)[0], place("attended_lo", [P, UT, NT], F32R, at=e)[0]]
        yssm, e = place("yssm", [P, UT, NT], at=e)
        wkv, e = place("wkv", [P, 1024], at=e)
        cst, e = place("cst", [P, CONST_COLS], at=e)
        small, e = place("small", [P, 20, ST], at=e)
        ident_r, e = place("ident_r", [P, MASK_T], F32R, at=e)
        causal_r, e = place("causal_r", [P, MASK_T], F32R, at=e)
        sel_r, e = place("sel_r", [P, 2 * HEADS], F32R, at=e)
        mixer_end = e
        sq_out, _ = place("sq_out", [P, DT, NT], at=mixer_end)
        v_tok, e = place("v_tok", [P, 2, NQ, 512], at=mixer_end)
        y_tok, e = place("y_tok", [P, 2, NQ, 512], at=e)
        gate_sq, _ = place("gate_sq", [P, UT, NT], at=e - UT * NT * 4)
        work, e2 = place("work", [P, 2, NQ, NT], at=e)
        probs, e2 = place("probs", [P, 3, NT], at=e2)
        pt, e2 = place("pt", [P, 2, NQ, MASK_T], at=e2)
        relu, e2 = place("relu", [P, 4, NT], at=e2)
        dsa_bias, e = place("dsa_bias", [P, NQ, NT], F32R, at=e2)
        top8, e = place("top8", [P, NQ, 8], at=e)
        iw_tok, e = place("iw_tok", [P, NQ, 32], at=e)
        stat, e = place("stat", [P, 5, 8], at=e)
        y_at = (end - DT * NT * 4) // 32 * 32
        assert e <= y_at and w_lo_end <= y_at
        y_hi, e = place("y_hi", [P, DT, NT], F32R, at=y_at)
        b_st, e = place("b_st", [P, 2, UT, P], at=mixer_end)
        c_st, e = place("c_st", [P, 2, ST, 32], at=e)
        table, e = place("table", [P, 2, 4, 2, NT], at=e)
        turns, e = place("turns", [P, 2, 2, NT], at=e)
        states, e = place("states", [P, 2, 2, 2, NT], at=e)
        side, e = place("side", [P, 2, NT], at=e)
        rot, e = place("rot", [P, 4, 2, 2, NT], at=e)
        fgate, e = place("fgate", [8, 2, NT], at=e)
        cum, e = place("cum", [P, NT], F32R, at=e)
        assert y_at + UT * NT * 4 <= e - NT * 4 and e <= end, (e, end)

        ps = ctx.enter_context(nc.psum_tensor("ps", [P, 8, 512], F32))

        def const(name, rows=P, cols=None):
            at, n = CONST[name]
            return cst[0:rows, at:at + (cols or n)]

        def rope_tile(r):
            if r < 9:
                return proj[:, IQ0 + r if r < 8 else IK, :]
            return proj[:, DQ0 + r - 9, :] if r < 13 else kv[:, r - 13, :]

        def squares_of(n):
            return (sq_down if n % 2 == 0 else sq_out) if n else sq_first

        def chunk(c):
            return slice(4 * c, 4 * c + 4) if c < PIVOT // 4 else slice(PIVOT + 2 * c - 6, PIVOT + 2 * c - 4)

        def norm_base(n):
            return 5 * n - 1 if n else 0

        def w_low(phase, slot):
            return (in_lo if phase == "in" else w_lo)[:, slot, :, :]

        def rope_bank(r):
            return 0 if r == ROPES - 1 else 3

        def param(name, at, n=1, rows=P):
            o = PARAM[name][0] + at
            return par[0:rows, o:o + n]

        w_loaded = [sem(f"w_loaded{s}") for s in range(SLOTS)]
        block_used = sem("block_used")
        hi_made, in_lo_made, lo_made = sem("hi_made"), sem("in_lo_made"), sem("lo_made")
        psum_free = sem("psum_free")
        x_loaded = [sem(f"x_loaded{c}") for c in range(4)]
        par_loaded, mix_loaded, ones_made = sem("par_loaded"), sem("mix_loaded"), sem("ones_made")
        mean_made, centered, squared, var_made, dev_made = (sem(n) for n in (
            "mean_made", "centered", "squared", "var_made", "dev_made"))
        pivot_made, spread_made = sem("pivot_made"), sem("spread_made")
        h_summed, sq_summed, scaled = sem("h_summed"), sem("sq_summed"), sem("scaled")
        h_made, xhi_made, xlo_made = sem("h_made"), sem("xhi_made"), sem("xlo_made")
        dt_made, freq_made, trig_made, c_made = (sem(n) for n in ("dt_made", "freq_made", "trig_made", "c_made"))
        turns_made, table_made, bu_made, bu_read, s_made, s_used, abs_made, y_read = (sem(n) for n in (
            "turns_made", "table_made", "bu_made", "bu_read", "s_made", "s_used", "abs_made", "y_read"))
        gelu_made, glu_made, glu_sq, glu_ms, glu_sd, ymul = (sem(n) for n in (
            "gelu_made", "glu_made", "glu_sq", "glu_ms", "glu_sd", "ymul"))
        glu_summed = sem("glu_summed")
        rot_made, roped = sem("rot_made"), sem("roped")
        ckv_sq, ckv_ms, ckv_sd, ckv_normed, kv_mm, kv_made = (sem(n) for n in (
            "ckv_sq", "ckv_ms", "ckv_sd", "ckv_normed", "kv_mm", "kv_made"))
        f_neg, f_exp, f_ln, cum_made = sem("f_neg"), sem("f_exp"), sem("f_ln"), sem("cum_made")
        vt_made, v_made = sem("vt_made"), sem("v_made")
        iwt_made, iw_made = sem("iwt_made"), sem("iw_made")
        idx_mm, idx_relu, idx_used, bias_made = sem("idx_mm"), sem("idx_relu"), sem("idx_used"), sem("bias_made")
        score_made, max_made, prob_made, ptr_made, pt_made, o_made, den_made, o_read = (sem(n) for n in (
            "score_made", "max_made", "prob_made", "ptr_made", "pt_made", "o_made", "den_made", "o_read"))
        ysq, ysd, ynorm, yt_mm, yt_made = (sem(n) for n in ("ysq", "ysd", "ynorm", "yt_mm", "yt_made"))
        yhi_made, ylo_made = sem("yhi_made"), sem("ylo_made")
        cpar_made, conv_a, conv1_made, gate_made = sem("cpar_made"), sem("conv_a"), sem("conv1_made"), sem("gate_made")
        prod_made, ghi_made, g_made = sem("prod_made"), sem("ghi_made"), sem("g_made")
        dve_step = sem("dve_step")
        stored = sem("stored")

        block = ctx.enter_context(nc.Block())

        @block.sync
        def _(sp):
            for c in range(4):
                sp.dma_start(h[:, 4 * c:4 * c + 4, :], x[:, 4 * c:4 * c + 4, :]).then_inc(x_loaded[c], 16)
            sp.dma_start(par[:, :], params).then_inc(par_loaded, 16)
            for b in range(SLOTS):
                sp.dma_start(raw[:, b, :, :], stream[b].rearrange("p (k m) -> p k m", k=KB)).then_inc(w_loaded[b], 16)
            for l in range(DEPTH):
                mixer, ffn = first_block(l, "in") + SLOTS, first_block(l, "out") + SLOTS
                end_at = min(first_block(l + 1, "in") + SLOTS, DEPTH * BLOCKS_PER_LAYER)
                for first, last, free, count in ((mixer, ffn, block_used, mixer - SLOTS),
                                                 (ffn, end_at, lo_made, first_low(l, "out"))):
                    with sp.Fori(0, (last - first) // SLOTS) as it:
                        for b in range(SLOTS):
                            src = stream[bass.ds(it * SLOTS + (first + b), 1), :, :].rearrange("a p (k m) -> p (a k) m", k=KB)
                            sp.wait_ge(free, it * SLOTS + (count + b + 1))
                            sp.dma_start(raw[:, b, :, :], src).then_inc(w_loaded[b], 16)
            for c in range(4):
                sp.wait_ge(h_made, CHUNKS * 2 * DEPTH + 2 * (c + 1))
                sp.dma_start(out[:, 4 * c:4 * c + 4, :], h[:, 4 * c:4 * c + 4, :]).then_inc(stored, 16)
            sp.wait_ge(stored, 64)

        @block.gpsimd
        def _(pool):
            def low_part(l, n, loop=0):
                b = first_block(l, "in") + n
                slot = b % SLOTS
                pool.wait_ge(hi_made, loop + (first_split(l, "in") + n + 1))
                nc.gpsimd.tensor_tensor(w_low("in", slot), raw[:, slot, :, :], w_hi[:, slot, :, :].bitcast(F32),
                                        ALU.subtract).then_inc(in_lo_made, 1)

            nc.gpsimd.memset(ones[:, :], 1.0).then_inc(ones_made, 1)
            for l in range(DEPTH):
                for n in range(SLOTS):
                    low_part(l, n)
                if l:
                    pool.wait_ge(mean_made, 2 * l + 1)
                pool.dma_start(cst[:, :], consts).then_inc(mix_loaded, 16)
                pool.dma_start(wkv[:, :], w_kv[l]).then_inc(mix_loaded, 16)
                pool.dma_start(b_st[:, :, :, :], ssm_b[l]).then_inc(mix_loaded, 16)
                pool.dma_start(c_st[:, :, :, :], ssm_c[l]).then_inc(mix_loaded, 16)
                with pool.Fori(0, IN_BLOCKS - SLOTS, SLOTS) as it:
                    for n in range(SLOTS):
                        low_part(l, SLOTS + n, loop=it)

        @block.tensor
        def _(pe):
            def products(l, phase, rhs, ready, t0=0):
                groups, blocks, body = PHASES[phase]
                b0, g0 = first_block(l, phase), first_group(l, phase)
                s0 = first_low(l, phase)
                with pe.Fori(0, groups // body) as it:
                    for g in range(body):
                        pe.wait_ge(psum_free, it * body + g0 + g + 1)
                        for b in range(blocks):
                            n = g * blocks + b
                            slot = (b0 + n) % SLOTS
                            pe.wait_ge(lo_made, it * (body * blocks) + (s0 + n + 1))
                            split_block(phase, slot, b, 2 * (g % 2), blocks * KB, rhs, ready if g == 0 else None, t0)
                        if phase != "up" and g == 2:
                            pe.wait_ge(h_summed, it * body + (PIVOT // 2 * (2 * l + (phase == "down")) + 2))
                            for k in range(2):
                                mm = pe.matmul(ps[:, 4, 0:NT], ones[:, :], hsum[:, k, :], start=k == 0, stop=k == 1)
                            mm.then_inc(pivot_made, 1)

            def split_block(phase, slot, b, bank, tiles, rhs, ready=None, t0=0):
                lo_w = w_low(phase, slot)
                for kk in range(KB):
                    k = b * KB + kk
                    if ready and k % 2 == 0:
                        pe.wait_ge(*ready(k))
                    hi, lo = (part[:, t0:NT] for part in rhs(k))
                    for j in range(2):
                        acc = ps[:, bank + j, t0:NT]
                        cols = slice(j * P, j * P + P)
                        pe.matmul(acc, lo_w[:, kk, cols], hi, start=k == 0, stop=False)
                        pe.matmul(acc, w_hi[:, slot, kk, cols], lo, start=False, stop=False)
                        mm = pe.matmul(acc, w_hi[:, slot, kk, cols], hi, start=False, stop=k == tiles - 1)
                mm.then_inc(block_used, 1)

            def x_parts(k):
                return x_hi[:, k, :], x_lo[:, k, :]

            def first_norm_sums():
                for k in range(DT):
                    if k % 4 == 0:
                        pe.wait_ge(x_loaded[k // 4], 16)
                    mm = pe.matmul(ps[:, 4, 0:NT], ones[:, :], h[:, k, :], start=k == 0, stop=k == DT - 1)
                mm.then_inc(mean_made, 1)
                pe.wait_ge(sq_summed, 1)
                for k in range(2):
                    mm = pe.matmul(ps[:, 6, 0:NT], ones[:, :], sq_first[:, k, :], start=k == 0, stop=k == 1)
                mm.then_inc(var_made, 1)

            def layer_norm_sums(n):
                for g in range(PIVOT // 2, 8):
                    pe.wait_ge(centered, norm_base(n) + 4 + g - PIVOT // 2)
                    for k in range(2 * g, 2 * g + 2):
                        mm = pe.matmul(ps[:, 5, 0:NT], ones[:, :], h[:, k, :], start=k == PIVOT, stop=k == DT - 1)
                mm.then_inc(mean_made, 1)
                pe.wait_ge(sq_summed, n + 1)
                for k in range(4):
                    if k == 2:
                        pe.wait_ge(squared, norm_base(n) + 5)
                    tile = squares_of(n)[:, k if k < 2 else DT - 4 + k, :]
                    mm = pe.matmul(ps[:, 6, 0:NT], ones[:, :], tile, start=k == 0, stop=k == 3)
                mm.then_inc(var_made, 1)

            def state_inputs(l, pr):
                for e in range(2):
                    t = 2 * pr + e
                    rows = slice(32 * (t % 4), 32 * (t % 4) + 32)
                    for c in range(2):
                        mm = pe.matmul(ps[:, 4 + 2 * e + c, 0:NT], b_st[rows, c, t // 4, :],
                                       proj[rows, U0 + t // 4, :], start=True, stop=True)
                mm.then_inc(bu_made, 1)

            def state_outputs(l, pr):
                m = pr // 2
                if pr % 2 == 0 and l * UT + m:
                    pe.wait_ge(y_read, l * UT + m)
                pe.wait_ge(s_made, l * PAIRS + pr + 1)
                for e in range(2):
                    t = 2 * pr + e
                    rows = slice(32 * (t % 4), 32 * (t % 4) + 32)
                    for c in range(2):
                        mm = pe.matmul(ps[rows, 2, 0:NT], c_st[:, c, t, :], states[:, pr % 2, e, c, :],
                                       start=c == 0, stop=c == 1)
                mm.then_inc(s_used, 1)

            def in_blocks(l, g, blocks):
                if blocks[0] == 0:
                    pe.wait_ge(psum_free, first_group(l, "in") + g + 2)
                for b in blocks:
                    pe.wait_ge(in_lo_made, first_low(l, "in") + 4 * g + b + 1)
                    split_block("in", (first_block(l, "in") + 4 * g + b) % SLOTS, b, 0, DT, x_parts,
                                (lambda k: (xlo_made, CHUNKS * 2 * l + k // 2 + 1)) if g == 0 else None)

            def side_products(l, step, half):
                ropes, kvs = ROPE_STEPS.get(step, ()), KV_STEPS.get(step, ())
                if half < len(ropes):
                    r = ropes[half]
                    if r == 8:
                        pe.wait_ge(ckv_sd, l + 1)
                    elif r == 13:
                        pe.wait_ge(kv_made, 8 * (l + 1))
                    if l * ROPES + r and r < ROPES - 1:
                        pe.wait_ge(roped, l * ROPES + r)
                    pe.matmul(ps[:, rope_bank(r), 0:NT], const("perm"), rope_tile(r), start=True, stop=True).then_inc(rot_made, 1)
                if step == MS_STEP and half == 1:
                    pe.wait_ge(roped, l * ROPES + 8)
                    pe.wait_ge(ckv_sq, l + 1)
                    pe.matmul(ps[:, 3, 0:NT], ones[:, :], side[:, 1, :], start=True, stop=True).then_inc(ckv_ms, 1)
                if half < len(kvs):
                    t = kvs[half]
                    pe.wait_ge(roped, l * ROPES + 13)
                    pe.wait_ge(ckv_normed, l + 1)
                    if l * 8 + t:
                        pe.wait_ge(kv_made, l * 8 + t)
                    pe.matmul(ps[:, 3, 0:NT], wkv[:, t * P:(t + 1) * P], proj[:, PADT, :],
                              start=True, stop=True).then_inc(kv_mm, 1)

            def scores(l, n):
                kind, hd, q = n // (HEADS * NQ), n // NQ % HEADS, n % NQ
                qs, qn = QT[q]
                ke = qs + qn
                b = slice(64 * (hd % 2), 64 * (hd % 2) + 64)
                s = ps[0:qn, S_BANKS[n % 3], 0:ke]
                if n >= 3:
                    pe.wait_ge(prob_made, l * 48 + n - 2)
                if kind == 0:
                    pe.matmul(s, proj[b, FQ0 + hd // 2, qs:ke], proj[b, FK0 + hd // 2, 0:ke], start=True, stop=False)
                    pe.matmul(s, cum[:, qs:ke], sel_r[:, hd:hd + 1].to_broadcast([P, ke]), start=False, stop=False)
                    pe.matmul(s, sel_r[:, HEADS + hd:HEADS + hd + 1].to_broadcast([P, qn]), cum[:, 0:ke],
                              start=False, stop=False)
                    mm = pe.matmul(s[:, qs:ke], ident_r[0:qn, 0:qn], causal_r[0:qn, 0:qn],
                                   start=False, stop=True)
                else:
                    pe.matmul(s, proj[b, DQ0 + hd // 2, qs:ke], kv[b, hd // 2, 0:ke], start=True, stop=False)
                    mm = pe.matmul(s, ident_r[0:qn, 0:qn], dsa_bias[0:qn, q, 0:ke], start=False, stop=True)
                mm.then_inc(score_made, 1)

            def prob_transposes(l, n):
                q = n % NQ
                qs, qn = QT[q]
                pe.wait_ge(prob_made, l * 48 + n + 1)
                if n >= 1:
                    pe.wait_ge(pt_made, l * 48 + n)
                for c in range(q + 1):
                    ks, kn = QT[c]
                    at = (q - c) * MASK_T
                    mm = pe.transpose(ps[0:kn, 6, at:at + qn], probs[0:qn, n % 3, ks:ks + kn], const("ident", qn, qn))
                mm.then_inc(ptr_made, 1)

            def weighted_values(l, n):
                kind, hd, q = n // (HEADS * NQ), n // NQ % HEADS, n % NQ
                qs, qn = QT[q]
                pe.wait_ge(pt_made, l * 48 + n + 1)
                if n >= 1:
                    pe.wait_ge(o_read, l * 48 + n)
                for c in range(q + 1):
                    ks, kn = QT[c]
                    mm = pe.matmul(ps[0:qn, 7, 0:HEAD], pt[0:kn, n % 2, q - c, 0:qn],
                                   v_tok[0:kn, kind, c, hd * HEAD:hd * HEAD + HEAD], start=c == 0, stop=c == q)
                mm.then_inc(o_made, 1)

            def transpose_values(l):
                for n in range(2 * NQ):
                    ks, kn = QT[n % NQ]
                    if n == NQ:
                        pe.wait_ge(roped, ROPES * (l + 1))
                    for t in range(4):
                        src = proj[:, FV0 + t, ks:ks + kn] if n < NQ else kv[:, 4 + t, ks:ks + kn]
                        mm = pe.transpose(ps[0:kn, V_BANKS[n], t * P:t * P + P], src, const("ident"))
                    mm.then_inc(vt_made, 1)

            def index_scores(l, n):
                j, q = n // NQ, n % NQ
                qs, qn = QT[q]
                b = slice(64 * (j % 2), 64 * (j % 2) + 64)
                if n >= 4:
                    pe.wait_ge(idx_relu, l * 48 + n - 3)
                pe.matmul(ps[0:qn, 4 + n % 4, 0:qs + qn], proj[b, IQ0 + j // 2, qs:qs + qn],
                          proj[b, IK, 0:qs + qn], start=True, stop=True).then_inc(idx_mm, 1)

            def gate_group(l, g):
                pe.wait_ge(psum_free, first_group(l, "glu") + g + 1)
                for b in range(2):
                    n = 2 * g + b
                    pe.wait_ge(w_loaded[n % SLOTS], ((first_block(l, "glu") + n) // SLOTS + 1) * 16)
                    for kk in range(KB):
                        for j in range(2):
                            k = b * KB + kk
                            mm = pe.matmul(ps[:, 2 * (g % 2) + j, 0:NT], raw[:, n % SLOTS, kk, j * P:j * P + P],
                                           yssm[:, k, :], start=k == 0, stop=k == 7)
                    mm.then_inc(block_used, 1)

            def output_transposes(l, kind, q):
                n = kind * NQ + q
                qs, qn = QT[q]
                pe.wait_ge(ynorm, 6 * l + n + 1)
                if n == 2:
                    pe.wait_ge(yt_made, 6 * l + 1)
                for t in range(4):
                    mm = pe.transpose(ps[:, Y_BANKS[n], t * MASK_T:t * MASK_T + qn],
                                      y_tok[0:qn, kind, q, t * P:t * P + P], const("ident", qn, qn))
                mm.then_inc(yt_mm, 1)

            pe.wait_ge(ones_made, 1)
            first_norm_sums()
            for l in range(DEPTH):
                ln = 2 * l + 1
                in_blocks(l, 0, range(4))
                pe.wait_ge(psum_free, first_group(l, "in") + 1 + 2)
                pe.wait_ge(mix_loaded, 64 * (l + 1))
                if l:
                    pe.wait_ge(bu_read, 32 * l)
                state_inputs(l, 0)
                for step in range(STEPS):
                    if step == 0:
                        in_blocks(l, 1, range(4))
                    if step + 1 < PAIRS:
                        pe.wait_ge(bu_read, 2 * (l * PAIRS + step + 1))
                        state_inputs(l, step + 1)
                    pe.wait_ge(psum_free, first_group(l, "in") + step + 1 + 2)
                    side_products(l, step, 0)
                    if 1 <= step < GROUPS_IN - 1:
                        in_blocks(l, step + 1, (0, 1, 2))
                    side_products(l, step, 1)
                    if 1 <= step < GROUPS_IN - 1:
                        in_blocks(l, step + 1, (3,))
                    if step == 0:
                        pe.wait_ge(c_made, l + 1)
                    if step < PAIRS:
                        state_outputs(l, step)
                pe.wait_ge(bu_read, 32 * (l + 1))
                for q, (qs, qn) in enumerate(QT):
                    mm = pe.transpose(ps[0:qn, 6, 32 * q:32 * q + 24], proj[0:24, FFIW, qs:qs + qn], const("ident", 24, 24))
                mm.then_inc(iwt_made, 1)
                transpose_values(l)
                pe.wait_ge(iw_made, l + 1)
                for g in range(4):
                    for n in range(12 * g, 12 * g + 12):
                        if n in (0, 1, 3):
                            pe.wait_ge(v_made, 6 * l + (1, 2, 2, 3)[n])
                        index_scores(l, n)
                    if g == 0:
                        pe.wait_ge(v_made, 6 * (l + 1))
                        pe.wait_ge(gelu_made, l + 1)
                    gate_group(l, g)
                pe.wait_ge(idx_relu, 48 * (l + 1))
                pe.wait_ge(cum_made, l + 1)
                pe.wait_ge(psum_free, first_group(l, "glu") + 4 + 2)
                for n in range(UNITS + 3):
                    if n == UNITS // 2:
                        pe.wait_ge(bias_made, l + 1)
                    if n < UNITS:
                        scores(l, n)
                    if 2 <= n < UNITS + 2:
                        prob_transposes(l, n - 2)
                    if n >= 3:
                        weighted_values(l, n - 3)
                    if n == GATE_NORM:
                        pe.wait_ge(glu_summed, l + 1)
                        for j in range(2):
                            mm = pe.matmul(ps[:, 0, 0:NT], ones[:, :], gate_sq[:, 6 + j, :], start=j == 0, stop=j == 1)
                        mm.then_inc(glu_ms, 1)
                    if FOX_NORM + 8 <= n < FOX_NORM + 11:
                        output_transposes(l, 0, n - FOX_NORM - 8)
                for q in range(NQ):
                    output_transposes(l, 1, q)
                products(l, "out", lambda k: (y_hi[:, k, :], y_lo[k // UT][:, k % UT, :]), lambda k: (ylo_made, 4 * l + k // 4 + 1))
                pe.wait_ge(psum_free, first_group(l, "out") + 8 + 2)
                layer_norm_sums(ln)
                products(l, "up", x_parts, lambda k: (xlo_made, CHUNKS * ln + k // 2 + 1), LAST_T0[0] if l == DEPTH - 1 else 0)
                products(l, "down", lambda k: (g_hi[:, k, :], g_lo[:, k, :]), lambda k: (g_made, FT * l + k + 2),
                         LAST_T0[1] if l == DEPTH - 1 else 0)
                pe.wait_ge(psum_free, first_group(l, "down") + 8 + 2)
                layer_norm_sums(ln + 1)

        @block.scalar
        def _(act):
            def cast(l, phase, n, loop=0):
                b = first_block(l, phase) + n
                slot = b % SLOTS
                act.wait_ge(w_loaded[slot], loop * (16 // SLOTS) + (b // SLOTS + 1) * 16)
                if b >= SLOTS:
                    act.wait_ge(block_used, loop + (b - SLOTS + 1))
                act.activation(w_hi[:, slot, :, :], raw[:, slot, :, :], ACT.Copy).then_inc(hi_made, 1)

            def layer_norm(n, gain, shift):
                if n == 0:
                    for c in range(4):
                        act.wait_ge(centered, c + 1)
                        act.activation(sq_first[:, 4 * c:4 * c + 4, :], h[:, 4 * c:4 * c + 4, :], ACT.Square).then_inc(squared, 1)
                    act.wait_ge(var_made, 1)
                    act.activation(rstd[:, :], ps[:, 6, 0:NT], ACT.Sqrt, bias=LN_EPS, scale=1.0 / D_MODEL).then_inc(dev_made, 1)
                else:
                    pivot_square(n, 4)
                    act.wait_ge(spread_made, n)
                    act.activation(rstd[:, :], rstd[:, :], ACT.Sqrt, bias=LN_EPS).then_inc(dev_made, 1)
                for c in range(CHUNKS):
                    act.wait_ge(scaled, CHUNKS * n + c + 1)
                    for k in range(2 * c, 2 * c + 2):
                        last = act.activation(h[:, k, :], h[:, k, :], ACT.Identity, bias=param(shift[0], shift[1] + k),
                                              scale=param(gain[0], gain[1] + k))
                    last.then_inc(h_made, 1)
                    if n < 2 * DEPTH:
                        act.wait_ge(h_made, CHUNKS * n + c + 1)
                        act.activation(x_hi[:, 2 * c:2 * c + 2, :], h[:, 2 * c:2 * c + 2, :], ACT.Copy).then_inc(xhi_made, 1)

            def pivot_square(n, c):
                t = chunk(c)
                act.wait_ge(centered, norm_base(n) + c + 1)
                act.activation(squares_of(n)[:, t, :], h[:, t, :], ACT.Square).then_inc(squared, 1)

            for n in range(SLOTS):
                cast(0, "in", n)
            act.wait_ge(par_loaded, 16)
            layer_norm(0, ("ln_in_g", 0), ("ln_in_b", 0))
            for l in range(DEPTH):
                ln = 2 * l + 1
                act.activation(small[:, 0, :], param("log_dt", l * ST, ST), ACT.Exp).then_inc(dt_made, 1)
                cast(l, "in", 4)
                act.wait_ge(freq_made, l + 1)
                act.activation(small[:, 4, :], small[:, 1, :], ACT.Exp).then_inc(trig_made, 1)
                act.activation(small[:, 5, :], small[:, 3, :], ACT.Sin, scale=TWO_PI_LOW).then_inc(trig_made, 1)
                act.activation(small[:, 6, :], small[:, 7, :], ACT.Sin, bias=HALF_PI, scale=-TWO_PI_LOW).then_inc(trig_made, 1)

                def read_group(g):
                    act.wait_ge(block_used, first_block(l, "in") + 4 * (g + 1))
                    act.activation(proj[:, 2 * g:2 * g + 2, :], ps[:, 0:2, 0:NT], ACT.Copy).then_inc(psum_free, 1)

                def wave_table(pr):
                    r = l * PAIRS + pr
                    act.wait_ge(turns_made, r + 1)
                    if pr >= 2:
                        act.wait_ge(s_made, r - 1)
                    tb = table[:, pr % 2, :, :, :]
                    tr = turns[:, 0, :, :]
                    act.activation(turns[:, 1, :, :], tr, ACT.Abs).then_inc(abs_made, 1)
                    act.activation(tb[:, 1, :, :], tr, ACT.Sin, scale=TWO_PI_LOW)
                    act.activation(tb[:, 2, :, :], tr, ACT.Sin, scale=-TWO_PI_LOW)
                    act.activation(tb[:, 3, :, :], tr, ACT.Sin, scale=TWO_PI_LOW)
                    act.wait_ge(abs_made, r + 1)
                    act.activation(tb[:, 0, :, :], turns[:, 1, :, :], ACT.Sin, bias=HALF_PI, scale=-TWO_PI_LOW).then_inc(table_made, 1)

                cast(l, "in", 5)
                read_group(0)
                cast(l, "in", 6)
                cast(l, "in", 7)
                wave_table(0)
                wave_table(1)
                for step in range(STEPS):
                    if step + 2 < PAIRS:
                        wave_table(step + 2)
                    if step == STEPS - 1:
                        act.wait_ge(y_read, UT * (l + 1))
                        act.activation(yssm[:, :, :], yssm[:, :, :], ACT.Gelu_apprx_tanh).then_inc(gelu_made, 1)
                    if step == MS_STEP:
                        act.wait_ge(ckv_ms, l + 1)
                        act.activation(rstd[:, :], ps[:, 3, 0:NT], ACT.Sqrt, bias=RMS_EPS, scale=1.0 / KV_RANK).then_inc(ckv_sd, 1)
                    if step == GATE_STEP:
                        act.wait_ge(f_neg, l + 1)
                        act.activation(fgate[:, 1, :], fgate[:, 1, :], ACT.Exp).then_inc(f_exp, 1)
                        act.wait_ge(f_exp, l + 1)
                        act.activation(fgate[:, 1, :], fgate[:, 1, :], ACT.Ln, bias=1.0).then_inc(f_ln, 1)
                    kvs = KV_STEPS.get(step, ())
                    for i in range(4):
                        if i % 2 == 0 and kvs:
                            t = kvs[i // 2]
                            act.wait_ge(kv_mm, l * 8 + t + 1)
                            act.activation(kv[:, t, :], ps[:, 3, 0:NT], ACT.Copy).then_inc(kv_made, 1)
                        if step + 1 < GROUPS_IN:
                            if i == 2:
                                read_group(step + 1)
                            if step + 2 < GROUPS_IN:
                                cast(l, "in", 4 * (step + 2) + i)
                for n in range(6):
                    kn = QT[n % NQ][1]
                    act.wait_ge(vt_made, 6 * l + n + 1)
                    act.activation(v_tok[0:kn, n // NQ, n % NQ, :], ps[0:kn, V_BANKS[n], :], ACT.Copy).then_inc(v_made, 1)

                def gate_out(g):
                    if g < 4:
                        act.wait_ge(block_used, first_block(l, "glu") + 2 * (g + 1))
                        for j in range(2):
                            sg = act.activation(proj[:, 2 * g + j, :], ps[:, 2 * (g % 2) + j, 0:NT], ACT.Sigmoid,
                                                bias=param("glu_b", l * UT + 2 * g + j))
                        sg.then_inc(psum_free, 1)
                    if g:
                        act.wait_ge(glu_made, 4 * l + g)
                        act.activation(gate_sq[:, 2 * g - 2:2 * g, :], proj[:, 2 * g - 2:2 * g, :], ACT.Square).then_inc(glu_sq, 1)

                for g in range(4):
                    for n in range(12 * g, 12 * g + 12):
                        qs, qn = QT[n % NQ]
                        act.wait_ge(idx_mm, l * 48 + n + 1)
                        if n >= 4:
                            act.wait_ge(idx_used, l * 48 + n - 3)
                        act.activation(relu[0:qn, n % 4, 0:qs + qn], ps[0:qn, 4 + n % 4, 0:qs + qn], ACT.Relu,
                                       scale=SCALE).then_inc(idx_relu, 1)
                    gate_out(g)
                gate_out(4)

                def output_squares(kind, q):
                    n = 6 * l + NQ * kind + q
                    qn = QT[q][1]
                    act.wait_ge(o_read, l * UNITS + (kind + 1) * UNITS // 2 - (NQ - 1 - q))
                    if n:
                        act.wait_ge(ysq, n)
                    act.activation(relu[0:qn, 0:2, 0:256], y_tok[0:qn, kind, q, :].rearrange("p (a b) -> p a b", a=2), ACT.Square,
                                   accum_out=stat[0:qn, 3, NQ * kind + q:NQ * kind + q + 1]).then_inc(ysq, 1)

                def output_deviations(kind):
                    act.wait_ge(ysq, 6 * l + NQ * (kind + 1))
                    for q in range(NQ):
                        n = NQ * kind + q
                        qn = QT[q][1]
                        act.activation(stat[0:qn, 4, n:n + 1], stat[0:qn, 3, n:n + 1], ACT.Sqrt, bias=RMS_EPS,
                                       scale=1.0 / 512).then_inc(ysd, 1)

                def high_part(c):
                    if c < 2:
                        act.wait_ge(ymul, 2 * l + c + 1)
                    else:
                        act.wait_ge(yt_made, 6 * l + NQ * (c - 1))
                    src = proj[:, 4 * c:4 * c + 4, :] if c < 2 else yssm[:, 4 * c - 8:4 * c - 4, :]
                    act.activation(y_hi[:, 4 * c:4 * c + 4, :], src, ACT.Copy).then_inc(yhi_made, 1)

                for n in range(UNITS + 3):
                    if n < UNITS:
                        qs, qn = QT[n % NQ]
                        act.wait_ge(max_made, l * UNITS + n + 1)
                        if n >= 3:
                            act.wait_ge(ptr_made, l * UNITS + n - 2)
                        act.activation(probs[0:qn, n % 3, 0:qs + qn], ps[0:qn, S_BANKS[n % 3], 0:qs + qn], ACT.Exp,
                                       bias=stat[0:qn, 0, n % 4:n % 4 + 1], scale=SCALE,
                                       accum_out=stat[0:qn, 1, n % 4:n % 4 + 1]).then_inc(prob_made, 1)
                    if n >= 3:
                        m = n - 3
                        kind, hd, q = m // (HEADS * NQ), m // NQ % HEADS, m % NQ
                        qn = QT[q][1]
                        act.wait_ge(den_made, l * UNITS + m + 1)
                        act.wait_ge(o_made, l * UNITS + m + 1)
                        act.activation(y_tok[0:qn, kind, q, hd * HEAD:(hd + 1) * HEAD], ps[0:qn, 7, 0:HEAD], ACT.Copy,
                                       scale=stat[0:qn, 2, m % 4:m % 4 + 1]).then_inc(o_read, 1)
                    if n == GATE_NORM + 2:
                        act.wait_ge(glu_ms, l + 1)
                        act.activation(rstd[:, :], ps[:, 0, 0:NT], ACT.Sqrt, bias=RMS_EPS, scale=1.0 / SSM_W).then_inc(glu_sd, 1)
                    if n in (GATE_NORM + 9, GATE_NORM + 13):
                        high_part((n - GATE_NORM - 9) // 4)
                    if FOX_NORM <= n < FOX_NORM + NQ:
                        output_squares(0, n - FOX_NORM)
                    if n == FOX_NORM + 4:
                        output_deviations(0)
                    if n == FOX_NORM + 13:
                        high_part(2)
                    if n >= UNITS:
                        output_squares(1, n - UNITS)
                output_deviations(1)
                for n in range(SLOTS - 1):
                    cast(l, "out", n)
                high_part(3)
                cast(l, "out", SLOTS - 1)
                for n in range(SLOTS, PHASES["out"][0] * PHASES["out"][1]):
                    cast(l, "out", n)
                for c in range(4):
                    pivot_square(ln, c)
                for n in range(4):
                    cast(l, "up", n)
                layer_norm(ln, ("ln1_g", l * DT), ("ln1_b", l * DT))

                def convolve(g, odd, i=0):
                    n = FT * l + g
                    conv_at = PARAM["conv"][0] + n * 8
                    if isinstance(i, int):
                        src = par_t(conv_at + 8 * i)
                    else:
                        src = par[:, bass.ds(i * 8 + conv_at, 8)]
                    act.activation(cpar[:, odd, :], src, ACT.Copy).then_inc(cpar_made, 1)
                    act.wait_ge(cpar_made, i + n + 1)
                    act.wait_ge(block_used, i * 4 + (first_block(l, "up") + 4 * (g + 1)))
                    for j in range(2):
                        act.activation(conv[:, odd, j, :], ps[:, 2 * odd + j, 0:NT], ACT.Identity,
                                       bias=cpar[:, odd, j:j + 1], scale=cpar[:, odd, 2 + j:3 + j]).then_inc(conv_a, 1)
                    act.wait_ge(psum_free, i + (first_group(l, "up") + g + 3))
                    act.activation(gate[:, odd, :], conv[:, odd, 1, :], ACT.Silu).then_inc(gate_made, 1)

                def par_t(at):
                    return par[:, at:at + 8]

                with act.Fori(0, FT - 2, 2) as i:
                    for e in range(2):
                        for n in range(4):
                            cast(l, "up", 4 * (e + 1) + n, loop=i * 4)
                        convolve(e, e, i)
                for n in range(4):
                    cast(l, "up", 4 * (FT - 1) + n)
                convolve(FT - 2, 0)
                for n in range(4):
                    cast(l, "down", n)
                convolve(FT - 1, 1)
                blocks = PHASES["down"][1]
                for n in range(4, 8 * blocks):
                    cast(l, "down", n)
                    if 7 * blocks + 4 <= n < 7 * blocks + 8:
                        pivot_square(ln + 1, n - 7 * blocks - 4)
                if l + 1 < DEPTH:
                    for n in range(SLOTS):
                        cast(l + 1, "in", n)
                layer_norm(ln + 1, ("ln2_g", l * DT), ("ln2_b", l * DT))

        @block.vector
        def _(dve):
            steps = {"n": 0}

            def mark(ins):
                steps["n"] += 1
                ins.then_inc(dve_step, 1)
                return steps["n"]

            def after(n=None):
                dve.wait_ge(dve_step, steps["n"] if n is None else n)

            def spread(ap, n):
                return ap.unsqueeze(1).to_broadcast([ap.shape[0], n, ap.shape[1]])

            def low_part(l, phase, n, loop=0):
                b = first_block(l, phase) + n
                slot = b % SLOTS
                dve.wait_ge(hi_made, loop + (first_split(l, phase) + n + 1))
                dve.tensor_tensor(w_lo[:, slot, :, :], raw[:, slot, :, :], w_hi[:, slot, :, :].bitcast(F32),
                                  ALU.subtract).then_inc(lo_made, 1)

            def first_norm_stats():
                dve.wait_ge(mean_made, 1)
                for c in range(4):
                    h4 = h[:, 4 * c:4 * c + 4, :]
                    dve.scalar_tensor_tensor(out=h4, in0=spread(ps[:, 4, 0:NT], 4), scalar=-1.0 / D_MODEL, in1=h4,
                                             op0=ALU.mult, op1=ALU.add).then_inc(centered, 1)
                for c in range(1, 4):
                    dve.wait_ge(squared, c + 1)
                    if c > 1:
                        after()
                    mark(dve.tensor_tensor(sq_first[:, 0:4, :], sq_first[:, 0:4, :], sq_first[:, 4 * c:4 * c + 4, :], ALU.add))
                after()
                dve.tensor_tensor(sq_first[:, 0:2, :], sq_first[:, 0:2, :], sq_first[:, 2:4, :], ALU.add).then_inc(sq_summed, 1)

            def take_pivot(n, c):
                t = chunk(c)
                dve.wait_ge(pivot_made, 2 * n)
                after()
                dve.scalar_tensor_tensor(out=h[:, t, :], in0=spread(ps[:, 4, 0:NT], t.stop - t.start), scalar=-1.0 / (P * PIVOT),
                                         in1=h[:, t, :], op0=ALU.mult, op1=ALU.add).then_inc(centered, 1)

            def fold_squares(n, c):
                sq = squares_of(n)
                dve.wait_ge(squared, norm_base(n) + c + 1)
                if c > 1:
                    after()
                if c < 3:
                    mark(dve.tensor_tensor(sq[:, 0:4, :], sq[:, 0:4, :], sq[:, 4 * c:4 * c + 4, :], ALU.add))
                else:
                    mark(dve.tensor_tensor(sq[:, 0:2, :], sq[:, 0:2, :], sq[:, 2:4, :], ALU.add))
                    after()
                    dve.tensor_tensor(sq[:, 0:2, :], sq[:, 0:2, :], sq[:, PIVOT:PIVOT + 2, :], ALU.add).then_inc(sq_summed, 1)

            def layer_norm(n, low_parts=None):
                if n:
                    take_pivot(n, 4)
                    if low_parts:
                        low_part(*low_parts, 0)
                    shift, shift_sq = squares_of(n)[:, 4, :], squares_of(n)[:, 5, :]
                    dve.wait_ge(sq_summed, n + 1)
                    dve.wait_ge(mean_made, n + 1)
                    mark(dve.tensor_scalar(shift, ps[:, 5, 0:NT], -1.0 / D_MODEL, None, ALU.mult))
                    after()
                    mark(dve.tensor_tensor(shift_sq, shift, shift, ALU.mult))

                    def unshift(c):
                        h4 = h[:, 4 * c:4 * c + 4, :]
                        return mark(dve.tensor_tensor(h4, h4, spread(shift, 4), ALU.add))

                    unshifted = [unshift(0)]
                    dve.wait_ge(var_made, n + 1)
                    after()
                    dve.scalar_tensor_tensor(out=rstd[:, :], in0=ps[:, 6, 0:NT], scalar=1.0 / D_MODEL, in1=shift_sq,
                                             op0=ALU.mult, op1=ALU.subtract).then_inc(spread_made, 1)
                    if low_parts:
                        low_part(*low_parts, 1)
                else:
                    first_norm_stats()
                dve.wait_ge(dev_made, n + 1)
                mark(dve.reciprocal(rstd[:, :], rstd[:, :]))
                after()
                for c in range(CHUNKS + 2):
                    if c < CHUNKS:
                        if n and c % 2 == 0:
                            after(unshifted[c // 2])
                        h2 = h[:, 2 * c:2 * c + 2, :]
                        dve.tensor_tensor(h2, h2, spread(rstd[:, :], 2), ALU.mult).then_inc(scaled, 1)
                    if n and c in (0, 2, 4):
                        unshifted.append(unshift(c // 2 + 1))
                    if low_parts and c in (3, 5):
                        low_part(*low_parts, c // 2 + 1)
                    if c >= 2 and n < 2 * DEPTH:
                        dve.wait_ge(xhi_made, CHUNKS * n + c - 1)
                        t = slice(2 * c - 4, 2 * c - 2)
                        dve.tensor_tensor(x_lo[:, t, :], h[:, t, :], x_hi[:, t, :].bitcast(F32),
                                          ALU.subtract).then_inc(xlo_made, 1)

            def residual(l, phase, g):
                blocks = PHASES[phase][1]
                dve.wait_ge(block_used, first_block(l, phase) + blocks * (g + 1))
                h2 = h[:, 2 * g:2 * g + 2, :]
                dve.scalar_tensor_tensor(out=h2, in0=x_lo[:, 2 * g:2 * g + 2, :].bitcast(F32), scalar=ALPHA,
                                         in1=ps[:, 2 * (g % 2):2 * (g % 2) + 2, 0:NT],
                                         op0=ALU.mult, op1=ALU.add).then_inc(psum_free, 1)
                dve.wait_ge(psum_free, first_group(l, phase) + g + 3)
                mark(dve.scalar_tensor_tensor(out=h2, in0=x_hi[:, 2 * g:2 * g + 2, :].bitcast(F32), scalar=ALPHA, in1=h2,
                                              op0=ALU.mult, op1=ALU.add))
                if g < PIVOT // 2:
                    after()
                    n = PIVOT // 2 * (2 * l + (phase == "down")) + g
                    if g == 2:
                        dve.wait_ge(pivot_made, 2 * (2 * l + (phase == "down")) + 1)
                    if g == 0:
                        dve.tensor_copy(hsum[:, :, :], h2).then_inc(h_summed, 1)
                    else:
                        dve.wait_ge(h_summed, n)
                        dve.tensor_tensor(hsum[:, :, :], hsum[:, :, :], h2, ALU.add).then_inc(h_summed, 1)

            def turns_of(l, pr):
                r = l * 16 + pr
                if r >= 1:
                    dve.wait_ge(table_made, r)
                for e in range(2):
                    mark(dve.tensor_scalar(turns[:, 0, e, :], const("time"), small[:, 3, 2 * pr + e:2 * pr + e + 1],
                                           None, ALU.mult))
                after()
                mark(dve.tensor_scalar(turns[:, 1, :, :], turns[:, 0, :, :], ROUND, ROUND, ALU.add, ALU.subtract))
                after()
                dve.tensor_tensor(turns[:, 0, :, :], turns[:, 0, :, :], turns[:, 1, :, :], ALU.subtract).then_inc(turns_made, 1)

            def scan_pair(l, pr):
                r = l * 16 + pr
                t1, t2, w, z = (rot[:, c, :, :, :] for c in range(4))
                tb = table[:, pr % 2, :, :, :]
                if r:
                    dve.wait_ge(s_made, r)
                dve.wait_ge(bu_made, r + 1)
                dve.wait_ge(table_made, r + 1)
                for e in range(2):
                    bu = ps[:, 4 + 2 * e:6 + 2 * e, 0:NT]
                    dve.tensor_tensor(t1[:, e, :, :], bu, spread(tb[:, 0, e, :], 2), ALU.mult)
                    dve.tensor_tensor(t2[:, e, ::-1, :], bu, tb[:, 2:4, e, :], ALU.mult).then_inc(bu_read, 1)
                turned = []
                for e in range(2):
                    dve.wait_ge(bu_read, 2 * r + 1 + e)
                    turned.append(mark(dve.tensor_tensor(w[:, e, :, :], t1[:, e, :, :], t2[:, e, :, :], ALU.add)))
                summed = []
                for e in range(2):
                    after(turned[e])
                    decay = small[:, 4, 2 * pr + e:2 * pr + e + 1].to_broadcast([P, NT])
                    for c in range(2):
                        last = dve.tensor_tensor_scan(z[:, e, c, :], decay, w[:, e, c, :], 0.0, ALU.mult, ALU.add)
                    summed.append(mark(last))
                back = []
                for e in range(2):
                    after(summed[e])
                    dve.tensor_tensor(t1[:, e, :, :], z[:, e, :, :], spread(tb[:, 0, e, :], 2), ALU.mult)
                    back.append(mark(dve.tensor_tensor(t2[:, e, ::-1, :], z[:, e, :, :], tb[:, 1:3, e, :], ALU.mult)))
                if r >= 2:
                    dve.wait_ge(s_used, r - 1)
                for e in range(2):
                    after(back[e])
                    last = dve.tensor_tensor(states[:, pr % 2, e, :, :], t1[:, e, :, :], t2[:, e, :, :], ALU.add)
                last.then_inc(s_made, 1)

            def read_state_output(l, m):
                dve.wait_ge(s_used, l * 16 + 2 * m + 2)
                dve.scalar_tensor_tensor(out=yssm[:, m, :], in0=proj[:, U0 + m, :], scalar=param("d_skip", l * UT + m),
                                         in1=ps[:, 2, 0:NT], op0=ALU.mult, op1=ALU.add).then_inc(y_read, 1)

            dve.memset(rstd[:, :], 0.0).then_inc(psum_free, 2)
            dve.wait_ge(par_loaded, 16)
            layer_norm(0)
            for l in range(DEPTH):
                ln = 2 * l + 1
                sm = [small[:, c, :] for c in range(20)]
                lr, li = param("lam_re", l * ST, ST), param("lam_im", l * ST, ST)
                dve.wait_ge(dt_made, l + 1)
                mark(dve.tensor_tensor(sm[1], lr, sm[0], ALU.mult))
                mark(dve.tensor_tensor(sm[2], li, sm[0], ALU.mult))
                after()
                mark(dve.tensor_scalar(sm[8], sm[2], 1.0 / (2.0 * np.pi), None, ALU.mult))
                after()
                mark(dve.tensor_scalar(sm[9], sm[8], ROUND, ROUND, ALU.add, ALU.subtract))
                after()
                mark(dve.tensor_tensor(sm[3], sm[8], sm[9], ALU.subtract))
                after()
                mark(dve.scalar_tensor_tensor(out=sm[7], in0=sm[3], scalar=-1.0, in1=sm[3], op0=ALU.mult, op1=ALU.max))
                after()
                dve.tensor_tensor(sm[13], lr, lr, ALU.mult).then_inc(freq_made, 1)
                mark(dve.tensor_tensor(sm[14], li, li, ALU.mult))
                dve.wait_ge(mix_loaded, 64 * (l + 1))
                turns_of(l, 0)
                dve.wait_ge(trig_made, 3 * (l + 1))
                dve.wait_ge(freq_made, l + 1)
                mark(dve.tensor_tensor(sm[10], sm[4], sm[6], ALU.mult))
                mark(dve.tensor_tensor(sm[11], sm[4], sm[5], ALU.mult))
                mark(dve.tensor_tensor(sm[13], sm[13], sm[14], ALU.add))
                after()
                mark(dve.tensor_scalar(sm[10], sm[10], 1.0, None, ALU.subtract))
                mark(dve.reciprocal(sm[13], sm[13]))
                after()
                mark(dve.tensor_tensor(sm[15], sm[10], lr, ALU.mult))
                mark(dve.tensor_tensor(sm[16], sm[11], li, ALU.mult))
                mark(dve.tensor_tensor(sm[17], sm[11], lr, ALU.mult))
                mark(dve.tensor_tensor(sm[18], sm[10], li, ALU.mult))
                after()
                mark(dve.tensor_tensor(sm[15], sm[15], sm[16], ALU.add))
                mark(dve.tensor_tensor(sm[17], sm[17], sm[18], ALU.subtract))
                after()
                mark(dve.tensor_tensor(sm[15], sm[15], sm[13], ALU.mult))
                mark(dve.tensor_tensor(sm[17], sm[17], sm[13], ALU.mult))
                after()
                tmp = [rot[:, c, :, :, :].rearrange("p a b t -> p (a b t)")[:, 0:ST * 32].rearrange("p (s c) -> p s c", c=32)
                       for c in range(4)]
                zr, zi = (sm[c].unsqueeze(2).to_broadcast([P, ST, 32]) for c in (15, 17))
                c_re, c_im = c_st[:, 0, :, :], c_st[:, 1, :, :]
                mark(dve.tensor_tensor(tmp[0], c_re, zr, ALU.mult))
                mark(dve.tensor_tensor(tmp[1], c_im, zi, ALU.mult))
                mark(dve.tensor_tensor(tmp[2], c_re, zi, ALU.mult))
                mark(dve.tensor_tensor(tmp[3], c_im, zr, ALU.mult))
                after()
                mark(dve.tensor_tensor(c_re, tmp[0], tmp[1], ALU.subtract))
                dve.scalar_tensor_tensor(out=c_im, in0=tmp[2], scalar=-1.0, in1=tmp[3], op0=ALU.mult,
                                         op1=ALU.subtract).then_inc(c_made, 1)
                fx, fe = fgate[:, 0, :], fgate[:, 1, :]

                def rope(r):
                    dve.wait_ge(rot_made, l * ROPES + r + 1)
                    mark(dve.tensor_tensor(side[:, 0, :], ps[:, rope_bank(r), 0:NT], const("rope_s"), ALU.mult))
                    mark(dve.tensor_tensor(rope_tile(r), rope_tile(r), const("rope_c"), ALU.mult))
                    after()
                    dve.tensor_tensor(rope_tile(r), rope_tile(r), side[:, 0, :], ALU.add).then_inc(roped, 1)

                def side_work(step, half):
                    ropes = ROPE_STEPS.get(step, ())
                    if half < len(ropes):
                        if ropes[half]:
                            dve.wait_ge(roped, l * ROPES + ropes[half])
                        rope(ropes[half])
                    if step == MS_STEP and half == 0:
                        dve.wait_ge(psum_free, first_group(l, "in") + CKV // 2 + 1 + 2)
                        dve.tensor_tensor(side[:, 1, :], proj[:, CKV, :], proj[:, CKV, :], ALU.mult).then_inc(ckv_sq, 1)
                    if step == MS_STEP + 1 and half == 1:
                        dve.wait_ge(ckv_sd, l + 1)
                        mark(dve.reciprocal(rstd[:, :], rstd[:, :]))
                        after()
                        dve.scalar_tensor_tensor(out=proj[:, PADT, :], in0=proj[:, CKV, :], scalar=param("kv_g", l), in1=rstd[:, :],
                                                 op0=ALU.mult, op1=ALU.mult).then_inc(ckv_normed, 1)
                    if step == GATE_STEP and half == 0:
                        mark(dve.tensor_scalar(cum[:, :], const("time"), 0.0, None, ALU.mult))
                        mark(dve.tensor_copy(ident_r[:, :], const("ident", cols=MASK_T)))
                        mark(dve.tensor_copy(causal_r[:, :], const("causal")))
                        mark(dve.tensor_copy(sel_r[:, :], const("sel")))
                        mark(dve.tensor_scalar(fx, proj[0:8, FFIW, :], param("f_bias", l, rows=8), None, ALU.add))
                        after()
                        dve.scalar_tensor_tensor(out=fe, in0=fx, scalar=-1.0, in1=fx, op0=ALU.mult, op1=ALU.min).then_inc(f_neg, 1)
                    if step == GATE_STEP and half == 1:
                        dve.wait_ge(f_ln, l + 1)
                        mark(dve.scalar_tensor_tensor(out=fx, in0=fx, scalar=0.0, in1=fe, op0=ALU.min, op1=ALU.subtract))
                        after()
                        mark(dve.tensor_tensor_scan(fe, ones[0:8, 0:1].to_broadcast([8, NT]), fx, 0.0, ALU.mult, ALU.add))
                        after()
                        mark(dve.tensor_copy(cum[0:8, :], fe))
                        after()
                        dve.tensor_tensor(cum[32:40, :], fe, cum[0:8, :].bitcast(F32), ALU.subtract).then_inc(cum_made, 1)

                turns_of(l, 1)
                scan_pair(l, 0)
                for step in range(STEPS):
                    side_work(step, 0)
                    if step >= 2 and step % 2 == 0 and step <= PAIRS:
                        read_state_output(l, step // 2 - 1)
                    if step + 2 < PAIRS:
                        turns_of(l, step + 2)
                    if step + 1 < PAIRS:
                        scan_pair(l, step + 1)
                    side_work(step, 1)
                dve.wait_ge(iwt_made, l + 1)
                for q, (qs, qn) in enumerate(QT):
                    last = dve.tensor_scalar(iw_tok[0:qn, q, 0:24], ps[0:qn, 6, 32 * q:32 * q + 24], IDX_HEADS ** -0.5, None,
                                             ALU.mult)
                last.then_inc(iw_made, 1)
                dve.wait_ge(iw_made, l + 1)
                def gate_apply(g):
                    dve.wait_ge(psum_free, first_group(l, "glu") + g + 3)
                    y2 = proj[:, 2 * g:2 * g + 2, :]
                    dve.tensor_tensor(y2, y2, yssm[:, 2 * g:2 * g + 2, :], ALU.mult).then_inc(glu_made, 1)

                for n in range(IDX_HEADS * NQ):
                    j, q = n // NQ, n % NQ
                    qs, qn = QT[q]
                    acc = work[0:qn, 0, q, 0:qs + qn]
                    src, wt = relu[0:qn, n % 4, 0:qs + qn], iw_tok[0:qn, q, 8 + j:9 + j]
                    dve.wait_ge(idx_relu, l * 48 + n + 1)
                    if j == 0:
                        dve.tensor_scalar(acc, src, wt, None, ALU.mult).then_inc(idx_used, 1)
                    else:
                        dve.wait_ge(idx_used, l * 48 + n - 2)
                        dve.scalar_tensor_tensor(out=acc, in0=src, scalar=wt, in1=acc, op0=ALU.mult,
                                                 op1=ALU.add).then_inc(idx_used, 1)
                    if n % 12 == 11:
                        gate_apply(n // 12)
                dve.wait_ge(idx_used, 48 * (l + 1))
                marks = []
                for q, (qs, qn) in enumerate(QT):
                    d = work[0:qn, 0, q, qs:qs + qn]
                    marks.append(mark(dve.tensor_tensor(d, d, const("causal", qn, qn), ALU.add)))

                def top_scores(rnd):
                    for q, (qs, qn) in enumerate(QT):
                        after(marks[q])
                        marks[q] = mark(dve.max(top8[0:qn, q, :], work[0:qn, rnd % 2, q, 0:qs + qn]))
                    for q, (qs, qn) in enumerate(QT):
                        after(marks[q])
                        marks[q] = mark(dve.match_replace(work[0:qn, 1 - rnd % 2, q, 0:qs + qn], top8[0:qn, q, :],
                                                          work[0:qn, rnd % 2, q, 0:qs + qn], TAKEN))

                def sparse_bias():
                    for q, (qs, qn) in enumerate(QT):
                        after(marks[q])
                        marks[q] = mark(dve.tensor_scalar(work[0:qn, 1, q, 0:qs + qn], work[0:qn, 0, q, 0:qs + qn], TAKEN, 1.0,
                                                          ALU.is_equal, ALU.subtract))
                    for q, (qs, qn) in enumerate(QT):
                        after(marks[q])
                        if q:
                            dve.tensor_scalar(dsa_bias[0:qn, q, 0:qs], work[0:qn, 1, q, 0:qs], -NEG, None, ALU.mult)
                        last = dve.scalar_tensor_tensor(out=dsa_bias[0:qn, q, qs:qs + qn], in0=work[0:qn, 1, q, qs:qs + qn],
                                                        scalar=-NEG, in1=const("causal", qn, qn), op0=ALU.mult, op1=ALU.add)
                    last.then_inc(bias_made, 1)

                def output_scale(kind, q):
                    n = kind * NQ + q
                    qn = QT[q][1]
                    dve.wait_ge(ysd, 6 * l + n + 1)
                    mark(dve.reciprocal(stat[0:qn, 4, n:n + 1], stat[0:qn, 4, n:n + 1]))
                    after()
                    y = y_tok[0:qn, kind, q, :]
                    dve.tensor_scalar(y, y, stat[0:qn, 4, n:n + 1], None, ALU.mult).then_inc(ynorm, 1)

                def output_read(kind, q):
                    n = kind * NQ + q
                    qs, qn = QT[q]
                    dve.wait_ge(yt_mm, 6 * l + n + 1)
                    for t in range(4):
                        last = dve.tensor_scalar(yssm[:, 4 * kind + t, qs:qs + qn], ps[:, Y_BANKS[n], t * MASK_T:t * MASK_T + qn],
                                                 param("mix_g", l * DT + UT + 4 * kind + t), None, ALU.mult)
                        if t == 3:
                            last.then_inc(yt_made, 1)

                def low_y(c):
                    dve.wait_ge(yhi_made, 4 * l + c + 1)
                    src = proj[:, 4 * c:4 * c + 4, :] if c < 2 else yssm[:, 4 * c - 8:4 * c - 4, :]
                    dve.tensor_tensor(y_lo[c // 2][:, 4 * (c % 2):4 * (c % 2) + 4, :], src, y_hi[:, 4 * c:4 * c + 4, :].bitcast(F32),
                                      ALU.subtract).then_inc(ylo_made, 1)

                for n in range(UNITS + 2):
                    if n < UNITS:
                        qs, qn = QT[n % NQ]
                        dve.wait_ge(score_made, l * UNITS + n + 1)
                        mark(dve.reduce_max(stat[0:qn, 0, 4 + n % 4:5 + n % 4], ps[0:qn, S_BANKS[n % 3], 0:qs + qn], AX_X))
                        after()
                        dve.tensor_scalar(stat[0:qn, 0, n % 4:n % 4 + 1], stat[0:qn, 0, 4 + n % 4:5 + n % 4], -SCALE, None,
                                          ALU.mult).then_inc(max_made, 1)
                    if n >= 2:
                        m = n - 2
                        q = m % NQ
                        qn = QT[q][1]
                        dve.wait_ge(ptr_made, l * UNITS + m + 1)
                        if m >= 2:
                            dve.wait_ge(o_made, l * UNITS + m - 1)
                        dve.tensor_copy(pt[0:MASK_T, m % 2, 0:q + 1, 0:qn],
                                        ps[0:MASK_T, 6, 0:NQ * MASK_T].rearrange("p (c t) -> p c t", c=NQ)[:, 0:q + 1, 0:qn]
                                        ).then_inc(pt_made, 1)
                        dve.reciprocal(stat[0:qn, 2, m % 4:m % 4 + 1], stat[0:qn, 1, m % 4:m % 4 + 1]).then_inc(den_made, 1)
                    if n == 1:
                        dve.wait_ge(glu_sq, 4 * (l + 1))
                        mark(dve.tensor_tensor(gate_sq[:, 4:8, :], gate_sq[:, 4:8, :], gate_sq[:, 0:4, :], ALU.add))
                        after()
                        dve.tensor_tensor(gate_sq[:, 6:8, :], gate_sq[:, 6:8, :], gate_sq[:, 4:6, :], ALU.add).then_inc(glu_summed, 1)
                    if n % 3 == 2 and n // 3 < TOPK // 8:
                        top_scores(n // 3)
                    if n == 3 * (TOPK // 8) - 1:
                        sparse_bias()
                    if n == GATE_NORM + 3:
                        dve.wait_ge(glu_sd, l + 1)
                        mark(dve.reciprocal(rstd[:, :], rstd[:, :]))
                        after()
                    if GATE_NORM + 4 <= n < GATE_NORM + 12:
                        k = n - GATE_NORM - 4
                        last = dve.scalar_tensor_tensor(out=proj[:, k, :], in0=proj[:, k, :], scalar=param("mix_g", l * DT + k),
                                                        in1=rstd[:, :], op0=ALU.mult, op1=ALU.mult)
                        if k % 4 == 3:
                            last.then_inc(ymul, 1)
                    if n in (GATE_NORM + 13, GATE_NORM + 17):
                        low_y((n - GATE_NORM - 13) // 4)
                    if FOX_NORM + 6 <= n < FOX_NORM + 9:
                        output_scale(0, n - FOX_NORM - 6)
                    if FOX_NORM + 9 <= n < FOX_NORM + 12:
                        output_read(0, n - FOX_NORM - 9)
                    if n == FOX_NORM + 15:
                        low_y(2)
                for q in range(NQ):
                    output_scale(1, q)
                dve.wait_ge(ynorm, 6 * (l + 1))
                low_part(l, "out", 0)
                low_part(l, "out", 1)
                for q in range(NQ):
                    output_read(1, q)
                low_part(l, "out", 2)
                low_y(3)
                low_part(l, "out", 3)
                for g in range(8):
                    for n in range(4):
                        if g:
                            low_part(l, "out", 4 * g + n)
                    if g:
                        residual(l, "out", g - 1)
                for c in range(4):
                    take_pivot(ln, c)
                for c in range(1, 4):
                    fold_squares(ln, c)
                residual(l, "out", 7)
                layer_norm(ln, (l, "up"))

                def convolve(g, odd, i=0):
                    n = FT * l + g
                    cv = conv[:, odd, :, :]
                    dve.wait_ge(conv_a, i * 2 + 2 * n + 2)
                    for tap in (1, 2):
                        if tap == 2:
                            dve.wait_ge(conv1_made, i * 2 + 2 * n + 2)
                        for j in range(2):
                            last = dve.scalar_tensor_tensor(
                                out=cv[:, j, tap:NT], in0=ps[:, 2 * odd + j, 0:NT - tap],
                                scalar=cpar[:, odd, 2 + 2 * tap + j:3 + 2 * tap + j], in1=cv[:, j, tap:NT],
                                op0=ALU.mult, op1=ALU.add)
                            if tap == 1:
                                last.then_inc(conv1_made, 1)
                    last.then_inc(psum_free, 1)
                    dve.wait_ge(gate_made, i + n + 1)
                    hi = g_hi[:, g:g + 1, :] if isinstance(i, int) else g_hi[:, bass.ds(i + g, 1), :]
                    lo = g_lo[:, g:g + 1, :] if isinstance(i, int) else g_lo[:, bass.ds(i + g, 1), :]
                    pr_ = prod[:, odd:odd + 1, :]
                    dve.tensor_tensor(pr_, gate[:, odd:odd + 1, :], cv[:, 0:1, :], ALU.mult).then_inc(prod_made, 1)
                    dve.tensor_tensor(hi, gate[:, odd:odd + 1, :], cv[:, 0:1, :], ALU.mult).then_inc(ghi_made, 1)
                    dve.wait_ge(prod_made, i + n + 1)
                    dve.wait_ge(ghi_made, i + n + 1)
                    dve.tensor_tensor(lo, pr_, hi.bitcast(F32), ALU.subtract).then_inc(g_made, 1)

                with dve.Fori(0, FT - 2, 2) as i:
                    for e in range(2):
                        for n in range(4):
                            low_part(l, "up", 4 * (e + 1) + n, loop=i * 4)
                        convolve(e, e, i)
                for n in range(4):
                    low_part(l, "up", 4 * (FT - 1) + n)
                convolve(FT - 2, 0)
                for n in range(4):
                    low_part(l, "down", n)
                convolve(FT - 1, 1)
                blocks = PHASES["down"][1]
                for g in range(8):
                    for n in range(4, blocks + 4):
                        if g * blocks + n < 8 * blocks:
                            low_part(l, "down", g * blocks + n)
                        if g == 7 and n < 8:
                            take_pivot(ln + 1, n - 4)
                        if g == 7 and 8 <= n < 11:
                            fold_squares(ln + 1, n - 7)
                    residual(l, "down", g)
                layer_norm(ln + 1)


def feature_major(a):
    t, f = a.shape
    return a.T.reshape(f // P, P, t).transpose(1, 0, 2)


def blocks_of(w):
    k, m = w.shape
    return w.reshape(k // (KB * P), KB, P, m // (2 * P), 2 * P).transpose(3, 0, 2, 1, 4).reshape(-1, P, KB * 2 * P)


def constants():
    c = np.zeros((P, CONST_COLS), np.float32)

    def put(name, a):
        at, n = CONST[name]
        c[:a.shape[0], at:at + n] = a

    put("ident", np.eye(P))
    rot = HEAD // 4
    perm = np.zeros((P, P))
    freq = np.float32(500000.0) ** (-np.arange(0, rot, 2, dtype=np.float32) / np.float32(rot))
    ang = np.arange(NT, dtype=np.float32)[None, :] * freq[:, None]
    cos, sin = np.ones((P, NT)), np.zeros((P, NT))
    for m in range(P):
        d = m % HEAD
        if d < rot:
            perm[m + rot // 2 if d < rot // 2 else m - rot // 2, m] = 1.0
            cos[m] = np.cos(ang[d % (rot // 2)])
            sin[m] = np.sin(ang[d % (rot // 2)]) * (-1 if d < rot // 2 else 1)
    put("perm", perm)
    put("rope_c", cos)
    put("rope_s", sin)
    put("time", np.tile(np.arange(NT) - NT // 2, (P, 1)))
    put("causal", np.where(np.arange(MASK_T)[None, :] <= np.arange(MASK_T)[:, None], 0.0, NEG))
    sel = np.zeros((40, 2 * HEADS))
    for part in (slice(0, HEADS), slice(32, 32 + HEADS)):
        sel[part] = np.concatenate([np.eye(HEADS), -np.eye(HEADS)], 1) / SCALE
    put("sel", sel)
    return c


def lay_out(i):
    z = np.zeros
    x = feature_major(np.concatenate([i["meta_tokens"], i["x"][0]], 0))
    stream = []
    for l in range(DEPTH):
        w = i["w_in"][l]
        at = np.cumsum([0, 1024, 512, 512, 512, 8, 512, 128, 1024, 64, 16])
        u, fq, fk, fv, ff, dq, ckv, iq, ik, iw = (w[:, at[n]:at[n + 1]] for n in range(10))
        pad = z((D_MODEL, P - 24), np.float32)
        stream.append(blocks_of(np.concatenate([u, iq, ckv, ff, iw, pad, ik, ik, z((D_MODEL, P), np.float32),
                                                dq, fk, fv, fq], 1)))
        stream.append(blocks_of(i["ssm_glu_w"][l]))
        stream.append(blocks_of(i["w_out"][l]))
        stream.append(blocks_of(i["w_up"][l].reshape(D_MODEL, 2, FT, P).transpose(0, 2, 1, 3).reshape(D_MODEL, -1)))
        stream.append(blocks_of(i["w_down"][l]))
    params = z((P, PARAM_COLS), np.float32)

    def put(name, a):
        o, n = PARAM[name]
        params[:a.shape[0], o:o + n] = a

    def tiles(a):
        return a.reshape(-1, P).T

    for name, key in (("ln_in_g", "ln_in_g"), ("ln_in_b", "ln_in_b"), ("ln1_g", "ln1_g"), ("ln1_b", "ln1_b"),
                      ("ln2_g", "ln2_g"), ("ln2_b", "ln2_b"), ("mix_g", "mix_norm_g"), ("glu_b", "ssm_glu_b"),
                      ("d_skip", "ssm_d"), ("kv_g", "kv_norm_g")):
        put(name, tiles(i[key]))
    put("f_bias", i["fox_f_bias"].T)
    taps = np.concatenate([i["conv_b"][:, None], i["conv_w"][:, ::-1]], 1)
    put("conv", taps.reshape(DEPTH, 4, 2, FT, P).transpose(4, 0, 3, 1, 2).reshape(P, -1))
    for name in ("lam_re", "lam_im"):
        put(name, i["ssm_" + name].reshape(DEPTH, ST, 2, STATE).transpose(2, 3, 0, 1).reshape(P, -1))
    put("log_dt", np.broadcast_to(i["ssm_log_dt"].reshape(DEPTH, ST, 2, 1), (DEPTH, ST, 2, STATE)
                                  ).transpose(2, 3, 0, 1).reshape(P, -1))
    b = z((DEPTH, 4, 2, GROUP, 2, UT, 2, STATE), np.float32)
    c = z((DEPTH, 2, STATE, 2, ST, 2, GROUP), np.float32)
    for part, (bk, ck) in enumerate((("ssm_b_re", "ssm_c_re"), ("ssm_b_im", "ssm_c_im"))):
        bb = i[bk].reshape(DEPTH, UT, 4, 2, STATE, GROUP)
        cc = i[ck].reshape(DEPTH, ST, 2, GROUP, STATE)
        for half in range(2):
            b[:, :, half, :, part, :, half, :] = bb[:, :, :, half].transpose(0, 2, 4, 1, 3)
            c[:, half, :, part, :, half, :] = cc[:, :, half].transpose(0, 3, 1, 2)
    return {"x": np.ascontiguousarray(x), "stream": np.concatenate(stream, 0), "consts": constants(), "params": params,
            "ssm_b": b.reshape(DEPTH, P, 2, UT, P), "ssm_c": c.reshape(DEPTH, P, 2, ST, 32),
            "w_kv": np.ascontiguousarray(i["w_kv_up"])}


def kernel(**inputs):
    import concourse.bacc as bacc
    from concourse.bass_utils import run_bass_kernel_spmd

    arrays = lay_out({n: np.asarray(a) for n, a in inputs.items()})
    nc = bacc.Bacc("TRN2", target_bir_lowering=False, num_devices=1)
    aps = {n: nc.dram_tensor(n, a.shape, F32, kind="ExternalInput").ap() for n, a in arrays.items()}
    out = nc.dram_tensor("out", (P, DT, NT), F32, kind="ExternalOutput").ap()
    hybrid_trunk(nc, **aps, out=out)
    r = run_bass_kernel_spmd(nc, [arrays], core_ids=[0])
    tokens = np.asarray(r.results[0]["out"]).transpose(2, 1, 0).reshape(NT, D_MODEL)
    return tokens[N_META:][None]
```
